# Optimizing a Trainium2 kernel written in Bass

```python
import jax, jax.numpy as jnp
from jax import lax
import numpy as np
import math

D_MODEL = 1024
BATCH = 1
SEQ = 512
DEPTH = 2

N_A_LAYERS = DEPTH // 2
N_B_LAYERS = DEPTH - N_A_LAYERS
HG_EXPAND = 128
HG_HEADS = D_MODEL // HG_EXPAND
HG_DV = D_MODEL // HG_HEADS
HG_CHUNK = 32
ATT_HEAD_DIM = 64
ATT_Q_HEADS = D_MODEL // ATT_HEAD_DIM
ATT_KV_HEADS = 2
ATT_GROUP = ATT_Q_HEADS // ATT_KV_HEADS
WINDOW = 128
D_FF = 2816
CONV_WIDTH = 3
EPS = 1e-6


F32 = jnp.float32

def rms_norm(x, g):
    xf = x.astype(F32)
    xf = xf * lax.rsqrt(jnp.mean(xf * xf, axis=-1, keepdims=True) + EPS)
    return (xf * g.astype(F32)).astype(x.dtype)

def alibi_slopes(n_heads):
    return jnp.asarray(2.0 ** (-8.0 * np.arange(1, n_heads + 1) / n_heads), F32)

def hgrn2_chunked(q, k, v, logf):
    b_, s_, h_, dk = q.shape
    dv = v.shape[-1]
    n_chunks = s_ // HG_CHUNK

    def to_chunks(t):
        return t.reshape(b_, n_chunks, HG_CHUNK, h_, t.shape[-1]).transpose(1, 0, 3, 2, 4)

    qc, kc, vc, gc = to_chunks(q), to_chunks(k), to_chunks(v), to_chunks(logf)
    causal = jnp.tril(jnp.ones((HG_CHUNK, HG_CHUNK), bool))[:, :, None]

    def step(state, inp):
        qb, kb, vb, gb = inp
        cum = jnp.cumsum(gb, axis=2)
        o_inter = jnp.einsum('bhtk,bhkv->bhtv', qb * jnp.exp(cum), state)
        rel = cum[:, :, :, None, :] - cum[:, :, None, :, :]
        decay = jnp.exp(jnp.where(causal, rel, -jnp.inf))
        scores = jnp.einsum('bhtk,bhsk,bhtsk->bhts', qb, kb, decay)
        o_intra = jnp.einsum('bhts,bhsv->bhtv', scores, vb)
        last = cum[:, :, -1:, :]
        new_state = (jnp.exp(last[:, :, 0, :])[..., None] * state
                     + jnp.einsum('bhsk,bhsv->bhkv', kb * jnp.exp(last - cum), vb))
        return new_state, o_inter + o_intra

    s0 = jnp.zeros((b_, h_, dk, dv), F32)
    _, o = lax.scan(step, s0, (qc, kc, vc, gc))
    return o.transpose(1, 0, 3, 2, 4).reshape(b_, s_, h_, dv)

def hgrn2_mixer(x, w_in, lower_bound, out_norm, w_out):
    b_, s_, _ = x.shape
    q, f, i, g = jnp.split(x @ w_in, 4, axis=-1)
    q = jax.nn.silu(q.astype(F32)) * HG_EXPAND ** -0.5
    forget = lower_bound + (1.0 - lower_bound) * jax.nn.sigmoid(f.astype(F32))
    logf = jnp.log(forget)
    k = 1.0 - forget
    heads = lambda t: t.reshape(b_, s_, HG_HEADS, -1)
    o = hgrn2_chunked(heads(q), heads(k), heads(i.astype(F32)), heads(logf))
    o = rms_norm(o, out_norm) * jax.nn.silu(heads(g.astype(F32)))
    return o.reshape(b_, s_, D_MODEL).astype(x.dtype) @ w_out

def shared_kv(h, kv_norm, w_kv):
    b_, s_, _ = h.shape
    k, v = jnp.split(rms_norm(h, kv_norm) @ w_kv, 2, axis=-1)
    return (k.reshape(b_, s_, ATT_KV_HEADS, ATT_HEAD_DIM),
            v.reshape(b_, s_, ATT_KV_HEADS, ATT_HEAD_DIM))

def swa_sink_attention(x, k, v, w_q, sinks, w_o):
    b_, s_, _ = x.shape
    nb = s_ // WINDOW
    q = (x @ w_q).reshape(b_, nb, WINDOW, ATT_KV_HEADS, ATT_GROUP, ATT_HEAD_DIM)

    def band(t):
        tb = t.reshape(b_, nb, WINDOW, ATT_KV_HEADS, ATT_HEAD_DIM)
        prev = jnp.pad(tb[:, :-1], ((0, 0), (1, 0), (0, 0), (0, 0), (0, 0)))
        return jnp.concatenate([prev, tb], axis=2)

    kb, vb = band(k), band(v)
    scores = jnp.einsum('bnqkgd,bnskd->bnkgqs', q.astype(F32), kb.astype(F32)) * ATT_HEAD_DIM ** -0.5
    q_idx = jnp.arange(WINDOW)[:, None] + WINDOW
    k_idx = jnp.arange(2 * WINDOW)[None, :]
    dist = q_idx - k_idx
    key_abs = (jnp.arange(nb) * WINDOW)[:, None] + jnp.arange(2 * WINDOW)[None, :] - WINDOW
    valid = ((dist >= 0) & (dist < WINDOW))[None] & (key_abs >= 0)[:, None, :]
    slopes = alibi_slopes(ATT_Q_HEADS).reshape(ATT_KV_HEADS, ATT_GROUP)
    scores = scores - slopes[:, :, None, None] * dist.astype(F32)
    scores = jnp.where(valid[None, :, None, None], scores, -jnp.inf)
    sink = sinks.astype(F32).reshape(ATT_KV_HEADS, ATT_GROUP)[None, None, :, :, None, None]
    m = jnp.maximum(jnp.max(scores, axis=-1, keepdims=True), sink)
    e = jnp.exp(scores - m)
    probs = e / (jnp.sum(e, axis=-1, keepdims=True) + jnp.exp(sink - m))
    out = jnp.einsum('bnkgqs,bnskd->bnqkgd', probs, vb.astype(F32))
    return out.reshape(b_, s_, ATT_Q_HEADS * ATT_HEAD_DIM).astype(x.dtype) @ w_o

def conv_ffn(x, w_up, conv_w, conv_b, w_down):
    s_ = x.shape[1]
    gate, val = jnp.split(x @ w_up, 2, axis=-1)
    gp = jnp.pad(gate, ((0, 0), (CONV_WIDTH - 1, 0), (0, 0)))
    conv = conv_b
    for j in range(CONV_WIDTH):
        conv = conv + conv_w[j] * gp[:, j:j + s_]
    return (jax.nn.silu(conv) * val) @ w_down

def first_inputs(seed: int = 0) -> dict:
    key = jax.random.key(seed)
    ks = jax.random.split(key, 18)
    D = D_MODEL
    HQD = ATT_Q_HEADS * ATT_HEAD_DIM
    KVD = ATT_KV_HEADS * ATT_HEAD_DIM

    def w(k, shape, fan_in):
        return jax.random.normal(k, shape, F32) * fan_in ** -0.5

    def gain(k, shape):
        return 1.0 + 0.02 * jax.random.normal(k, shape, F32)

    return {
        'x': jax.random.normal(ks[0], (BATCH, SEQ, D), F32),
        'hg_norm': gain(ks[1], (N_A_LAYERS, D)),
        'hg_w_in': w(ks[2], (N_A_LAYERS, D, 4 * D), D),
        'hg_lb_logits': 0.1 * jax.random.normal(ks[3], (N_A_LAYERS + 1, D), F32),
        'hg_out_norm': gain(ks[4], (N_A_LAYERS, HG_DV)),
        'hg_w_out': w(ks[5], (N_A_LAYERS, D, D), D),
        'kv_norm': gain(ks[6], (D,)),
        'w_kv': w(ks[7], (D, 2 * KVD), D),
        'attn_norm': gain(ks[8], (N_B_LAYERS, D)),
        'attn_w_q': w(ks[9], (N_B_LAYERS, D, HQD), D),
        'attn_sinks': 0.5 * jax.random.normal(ks[10], (N_B_LAYERS, ATT_Q_HEADS), F32),
        'attn_w_o': w(ks[11], (N_B_LAYERS, HQD, D), HQD),
        'ffn_norm': gain(ks[12], (DEPTH, D)),
        'ffn_w_up': w(ks[13], (DEPTH, D, 2 * D_FF), D),
        'ffn_conv_w': w(ks[14], (DEPTH, CONV_WIDTH, D_FF), CONV_WIDTH),
        'ffn_conv_b': 0.02 * jax.random.normal(ks[15], (DEPTH, D_FF), F32),
        'ffn_w_down': w(ks[16], (DEPTH, D_FF, D), D_FF),
        'final_norm': gain(ks[17], (D,)),
    }

def first_block(x, hg_norm, hg_w_in, hg_lb_logits, hg_out_norm, hg_w_out, kv_norm, w_kv,
              attn_norm, attn_w_q, attn_sinks, attn_w_o, ffn_norm, ffn_w_up, ffn_conv_w,
              ffn_conv_b, ffn_w_down, final_norm):
    lower_bounds = jnp.cumsum(jax.nn.softmax(hg_lb_logits.astype(F32), axis=0), axis=0)
    h = x
    k_sh, v_sh = None, None
    for layer in range(DEPTH):
        if layer < N_A_LAYERS:
            a = layer
            h = h + hgrn2_mixer(rms_norm(h, hg_norm[a]), hg_w_in[a], lower_bounds[a],
                                hg_out_norm[a], hg_w_out[a])
        else:
            bi = layer - N_A_LAYERS
            if bi == 0:
                k_sh, v_sh = shared_kv(h, kv_norm, w_kv)
            h = h + swa_sink_attention(rms_norm(h, attn_norm[bi]), k_sh, v_sh,
                                       attn_w_q[bi], attn_sinks[bi], attn_w_o[bi])
        h = h + conv_ffn(rms_norm(h, ffn_norm[layer]), ffn_w_up[layer], ffn_conv_w[layer],
                         ffn_conv_b[layer], ffn_w_down[layer])
    return rms_norm(h, final_norm)


GRID_W = 64
CTX_LEN = 256
N_MIXERS = 4
Q_BLOCK = 128
NORM_EPS = 1e-6
NEG_INF = -1e30
ROPE_BASE = 10000.0
ROPE_DIM = 64

MLA_HEADS = 8
MLA_Q_RANK = 384
MLA_KV_RANK = 256
MLA_NOPE = 128
MLA_ROPE = ROPE_DIM
MLA_V = 128
MLA_WIDTH = MLA_HEADS * MLA_V

HY_WIDTH = D_MODEL
HY_ORDER = 2
HY_SHORT = 3
HY_EMB = 33
HY_BANDS = (HY_EMB - 1) // 2
HY_FILT_HIDDEN = 64
HY_DECAY_TARGET = 1e-2
HY_FAST_DECAY = 0.3
HY_SLOW_DECAY = 1.5

SWA_Q_HEADS = 16
SWA_KV_HEADS = 4
SWA_GROUP = SWA_Q_HEADS // SWA_KV_HEADS
SWA_HEAD_DIM = ROPE_DIM
SWA_WINDOW = 128
SWA_WIDTH = SWA_Q_HEADS * SWA_HEAD_DIM

CF_WIDTH = D_MODEL
CF_KERNEL = 31


def n_layers_of(m):
    return len(range(m, DEPTH, N_MIXERS))

def rmsnorm(x, g):
    xf = x.astype(jnp.float32)
    y = xf * lax.rsqrt(jnp.mean(xf * xf, axis=-1, keepdims=True) + NORM_EPS)
    return (y * g.astype(jnp.float32)).astype(x.dtype)

def layernorm(x, g, b):
    xf = x.astype(jnp.float32)
    mu = jnp.mean(xf, axis=-1, keepdims=True)
    xc = xf - mu
    var = jnp.mean(xc * xc, axis=-1, keepdims=True)
    return (xc * lax.rsqrt(var + NORM_EPS) * g.astype(jnp.float32) + b.astype(jnp.float32)).astype(x.dtype)

def modulate(h, shift, scale):
    return h * (1 + scale) + shift

def grid_rope(L, dim, dtype):
    rows = L // GRID_W
    row = jnp.repeat(jnp.arange(rows, dtype=jnp.float32), GRID_W)
    col = jnp.tile(jnp.arange(GRID_W, dtype=jnp.float32), rows)
    n_freq = dim // 4
    inv = ROPE_BASE ** (-jnp.arange(n_freq, dtype=jnp.float32) / n_freq)
    ang = jnp.concatenate([row[:, None] * inv, col[:, None] * inv], axis=-1)
    return jnp.cos(ang).astype(dtype), jnp.sin(ang).astype(dtype)

def apply_rope(x, cos, sin):
    half = x.shape[-1] // 2
    x1, x2 = x[..., :half], x[..., half:]
    return jnp.concatenate([x1 * cos - x2 * sin, x1 * sin + x2 * cos], axis=-1)

def depthwise_conv(u, w, b):
    K, C = w.shape
    pad = (K - 1) // 2
    y = lax.conv_general_dilated(u, w[:, None, :].astype(u.dtype), window_strides=(1,),
                                 padding=[(pad, pad)], dimension_numbers=('NWC', 'WIO', 'NWC'),
                                 feature_group_count=C)
    return y + b

def to_blocks(t):
    B, L = t.shape[:2]
    return jnp.moveaxis(t.reshape(B, L // Q_BLOCK, Q_BLOCK, *t.shape[2:]), 1, 0)

def from_blocks(o):
    nb, B, Q = o.shape[:3]
    return jnp.moveaxis(o, 0, 1).reshape(B, nb * Q, *o.shape[3:])

def mla_mixer(a, ac, cos, sin, w_in, q_norm_g, kv_norm_g, w_uq, w_ukv, w_out, ctx_out):
    B, L, _ = a.shape
    splits = [MLA_Q_RANK, MLA_Q_RANK + MLA_KV_RANK, MLA_Q_RANK + MLA_KV_RANK + MLA_ROPE]

    def project(t):
        n = t.shape[1]
        cq, ckv, k_rope, gate = jnp.split(t @ w_in, splits, axis=-1)
        q = (rmsnorm(cq, q_norm_g) @ w_uq).reshape(B, n, MLA_HEADS, MLA_NOPE + MLA_ROPE)
        kv = (rmsnorm(ckv, kv_norm_g) @ w_ukv).reshape(B, n, MLA_HEADS, MLA_NOPE + MLA_V)
        return q[..., :MLA_NOPE], q[..., MLA_NOPE:], kv[..., :MLA_NOPE], k_rope, kv[..., MLA_NOPE:], gate

    qn, qr, kn, kr, v, gate = project(a)
    qr = apply_rope(qr, cos[:, None, :], sin[:, None, :])
    kr = apply_rope(kr, cos, sin)
    qnc, qrc, knc, krc, vc, gatec = project(ac)
    scale = (MLA_NOPE + MLA_ROPE) ** -0.5

    def scores(qn_, qr_, kn_, kr_):
        s = jnp.einsum('bqhd,bkhd->bhqk', qn_, kn_) + jnp.einsum('bqhr,bkr->bhqk', qr_, kr_)
        return s.astype(jnp.float32) * scale

    def attend(blk):
        qn_b, qr_b = blk
        s = jnp.concatenate([scores(qn_b, qr_b, kn, kr), scores(qn_b, qr_b, knc, krc)], axis=-1)
        p = jax.nn.softmax(s, axis=-1).astype(v.dtype)
        return (jnp.einsum('bhqk,bkhd->bqhd', p[..., :L], v)
                + jnp.einsum('bhqk,bkhd->bqhd', p[..., L:], vc))

    o = from_blocks(lax.map(attend, (to_blocks(qn), to_blocks(qr)))).reshape(B, L, MLA_WIDTH)
    y = (o * jax.nn.silu(gate)) @ w_out
    yc = None
    if ctx_out:
        pc = jax.nn.softmax(scores(qnc, qrc, knc, krc), axis=-1).astype(vc.dtype)
        oc = jnp.einsum('bhqk,bkhd->bqhd', pc, vc).reshape(B, -1, MLA_WIDTH)
        yc = (oc * jax.nn.silu(gatec)) @ w_out
    return y, yc

def hyena_filter_spectra(L, w_in, w_hid, b, freq, w_out):
    f32 = jnp.float32
    t = jnp.linspace(0.0, 1.0, L, dtype=f32)[:, None]
    wpos = (2.0 * math.pi / L) * jnp.arange(L, dtype=f32)[:, None]
    bands = jnp.linspace(1e-4, HY_BANDS - 1, HY_BANDS, dtype=f32)[None, :]
    hdn = jnp.concatenate([t, jnp.cos(bands * wpos), -jnp.sin(bands * wpos)], axis=-1)
    b, freq = b.astype(f32), freq.astype(f32)
    for k, w in enumerate((w_in, w_hid[0], w_hid[1])):
        hdn = jnp.sin(freq[k] * (hdn @ w.astype(f32) + b[k]))
    h = (hdn @ w_out.astype(f32)).reshape(L, HY_ORDER, 2, HY_WIDTH)
    deltas = jnp.abs(jnp.linspace(math.log(HY_DECAY_TARGET) / HY_FAST_DECAY,
                                  math.log(HY_DECAY_TARGET) / HY_SLOW_DECAY, HY_WIDTH, dtype=f32))
    h = h * jnp.exp(-t * deltas)[:, None, None, :]
    hf, hb = h[:, :, 0], h[:, :, 1]
    k_circ = jnp.concatenate([hf[:1] + hb[:1], hf[1:], jnp.zeros_like(hf[:1]), hb[:0:-1]], axis=0)
    return jnp.fft.rfft(k_circ, axis=0)

def fft_long_conv(u, spec):
    L = u.shape[1]
    U = jnp.fft.rfft(u.astype(jnp.float32), n=2 * L, axis=1)
    return jnp.fft.irfft(U * spec, n=2 * L, axis=1)[:, :L].astype(u.dtype)

def hyena_seq(t, w_in, conv_w, conv_b, spec, bias, w_out):
    u, gate = jnp.split(t @ w_in, [(HY_ORDER + 1) * HY_WIDTH], axis=-1)
    u = depthwise_conv(u, conv_w, conv_b)
    v, *gates = jnp.split(u, HY_ORDER + 1, axis=-1)
    z = v
    for o in range(HY_ORDER):
        z = gates[o] * (fft_long_conv(z, spec[:, o]) + z * bias[o])
    return (z * jax.nn.silu(gate)) @ w_out

def swa_mixer(a, ac, cos, sin, w_in, sink, w_out, ctx_out):
    B, L, _ = a.shape
    nq = SWA_Q_HEADS * SWA_HEAD_DIM
    nkv = SWA_KV_HEADS * SWA_HEAD_DIM

    def project(t):
        n = t.shape[1]
        q, k, v, gate = jnp.split(t @ w_in, [nq, nq + nkv, nq + 2 * nkv], axis=-1)
        return (q.reshape(B, n, SWA_KV_HEADS, SWA_GROUP, SWA_HEAD_DIM),
                k.reshape(B, n, SWA_KV_HEADS, SWA_HEAD_DIM),
                v.reshape(B, n, SWA_KV_HEADS, SWA_HEAD_DIM), gate)

    q, k, v, gate = project(a)
    q = apply_rope(q, cos[:, None, None, :], sin[:, None, None, :])
    k = apply_rope(k, cos[:, None, :], sin[:, None, :])
    qc, kc, vc, gatec = project(ac)
    scale = SWA_HEAD_DIM ** -0.5
    sink_logit = sink.astype(jnp.float32).reshape(SWA_KV_HEADS, SWA_GROUP, 1, 1)

    def softmax_with_sink(parts, n_q):
        s_sink = jnp.broadcast_to(sink_logit, (B, SWA_KV_HEADS, SWA_GROUP, n_q, 1))
        p = jax.nn.softmax(jnp.concatenate([*parts, s_sink], axis=-1), axis=-1)
        return p[..., :-1].astype(v.dtype)

    span = Q_BLOCK + 2 * SWA_WINDOW
    pad = ((0, 0), (SWA_WINDOW, SWA_WINDOW), (0, 0), (0, 0))
    kp, vp = jnp.pad(k, pad), jnp.pad(v, pad)
    rel = jnp.arange(span)[None, :] - jnp.arange(Q_BLOCK)[:, None]
    band = (rel >= 0) & (rel <= 2 * SWA_WINDOW)

    def attend(args):
        j, q_b = args
        start = j * Q_BLOCK
        k_b = lax.dynamic_slice_in_dim(kp, start, span, axis=1)
        v_b = lax.dynamic_slice_in_dim(vp, start, span, axis=1)
        kpos = start - SWA_WINDOW + jnp.arange(span)
        valid = band & ((kpos >= 0) & (kpos < L))[None, :]
        s_win = jnp.einsum('bqhgd,bkhd->bhgqk', q_b, k_b).astype(jnp.float32) * scale
        s_win = jnp.where(valid, s_win, NEG_INF)
        s_ctx = jnp.einsum('bqhgd,bkhd->bhgqk', q_b, kc).astype(jnp.float32) * scale
        p = softmax_with_sink([s_win, s_ctx], Q_BLOCK)
        return (jnp.einsum('bhgqk,bkhd->bqhgd', p[..., :span], v_b)
                + jnp.einsum('bhgqk,bkhd->bqhgd', p[..., span:], vc))

    o = from_blocks(lax.map(attend, (jnp.arange(L // Q_BLOCK), to_blocks(q)))).reshape(B, L, SWA_WIDTH)
    y = (o * jax.nn.silu(gate)) @ w_out
    yc = None
    if ctx_out:
        s = jnp.einsum('bqhgd,bkhd->bhgqk', qc, kc).astype(jnp.float32) * scale
        pc = softmax_with_sink([s], qc.shape[1])
        oc = jnp.einsum('bhgqk,bkhd->bqhgd', pc, vc).reshape(B, -1, SWA_WIDTH)
        yc = (oc * jax.nn.silu(gatec)) @ w_out
    return y, yc

def conformer_seq(t, w_in, dw_w, dw_b, ln_g, ln_b, w_out):
    a, b, gate = jnp.split(t @ w_in, 3, axis=-1)
    u = a * jax.nn.sigmoid(b)
    u = depthwise_conv(u, dw_w, dw_b)
    u = jax.nn.silu(layernorm(u, ln_g, ln_b))
    return (u * jax.nn.silu(gate)) @ w_out

def second_inputs(seed: int = 0) -> dict:
    key = jax.random.key(seed)
    ks = iter(jax.random.split(key, 40))
    D = D_MODEL
    f32 = jnp.float32

    def nrm(shape, std):
        return jax.random.normal(next(ks), shape, f32) * std

    def gain(shape):
        return 1.0 + nrm(shape, 0.02)

    nA, nB, nC, nD = (n_layers_of(m) for m in range(N_MIXERS))
    mla_in = MLA_Q_RANK + MLA_KV_RANK + MLA_ROPE + MLA_WIDTH
    swa_in = SWA_Q_HEADS * SWA_HEAD_DIM + 2 * SWA_KV_HEADS * SWA_HEAD_DIM + SWA_WIDTH
    return {
        "x": nrm((BATCH, SEQ, D), 1.0),
        "c": nrm((BATCH, D), 1.0),
        "ctx": nrm((BATCH, CTX_LEN, D), 1.0),
        "c_ctx": nrm((D,), 1.0),
        "norm_g": gain((DEPTH, D)),
        "ada_w": nrm((DEPTH, D, 3 * D), 0.5 * D ** -0.5),
        "ada_b": nrm((DEPTH, 3 * D), 0.02),
        "final_g": gain((D,)),
        "mla_w_in": nrm((nA, D, mla_in), D ** -0.5),
        "mla_q_norm_g": gain((nA, MLA_Q_RANK)),
        "mla_kv_norm_g": gain((nA, MLA_KV_RANK)),
        "mla_w_uq": nrm((nA, MLA_Q_RANK, MLA_HEADS * (MLA_NOPE + MLA_ROPE)), MLA_Q_RANK ** -0.5),
        "mla_w_ukv": nrm((nA, MLA_KV_RANK, MLA_HEADS * (MLA_NOPE + MLA_V)), MLA_KV_RANK ** -0.5),
        "mla_w_out": nrm((nA, MLA_WIDTH, D), MLA_WIDTH ** -0.5),
        "hy_w_in": nrm((nB, D, (HY_ORDER + 2) * HY_WIDTH), D ** -0.5),
        "hy_conv_w": nrm((nB, HY_SHORT, (HY_ORDER + 1) * HY_WIDTH), HY_SHORT ** -0.5),
        "hy_conv_b": nrm((nB, (HY_ORDER + 1) * HY_WIDTH), 0.02),
        "hy_filt_w_in": nrm((nB, HY_EMB, HY_FILT_HIDDEN), HY_EMB ** -0.5),
        "hy_filt_w_hid": nrm((nB, 2, HY_FILT_HIDDEN, HY_FILT_HIDDEN), HY_FILT_HIDDEN ** -0.5),
        "hy_filt_b": nrm((nB, 3, HY_FILT_HIDDEN), 0.2),
        "hy_filt_freq": gain((nB, 3, HY_FILT_HIDDEN)),
        "hy_filt_w_out": nrm((nB, HY_FILT_HIDDEN, HY_ORDER * 2 * HY_WIDTH), 0.005),
        "hy_bias": nrm((nB, HY_ORDER, HY_WIDTH), 0.5),
        "hy_w_out": nrm((nB, HY_WIDTH, D), HY_WIDTH ** -0.5),
        "swa_w_in": nrm((nC, D, swa_in), D ** -0.5),
        "swa_sink": nrm((nC, SWA_Q_HEADS), 0.5),
        "swa_w_out": nrm((nC, SWA_WIDTH, D), SWA_WIDTH ** -0.5),
        "cf_w_in": nrm((nD, D, 3 * CF_WIDTH), D ** -0.5),
        "cf_dw_w": nrm((nD, CF_KERNEL, CF_WIDTH), CF_KERNEL ** -0.5),
        "cf_dw_b": nrm((nD, CF_WIDTH), 0.02),
        "cf_ln_g": gain((nD, CF_WIDTH)),
        "cf_ln_b": nrm((nD, CF_WIDTH), 0.02),
        "cf_w_out": nrm((nD, CF_WIDTH, D), CF_WIDTH ** -0.5),
    }

def second_block(x, c, ctx, c_ctx, norm_g, ada_w, ada_b, final_g,
              mla_w_in, mla_q_norm_g, mla_kv_norm_g, mla_w_uq, mla_w_ukv, mla_w_out,
              hy_w_in, hy_conv_w, hy_conv_b, hy_filt_w_in, hy_filt_w_hid, hy_filt_b, hy_filt_freq,
              hy_filt_w_out, hy_bias, hy_w_out,
              swa_w_in, swa_sink, swa_w_out,
              cf_w_in, cf_dw_w, cf_dw_b, cf_ln_g, cf_ln_b, cf_w_out):
    B, L, _ = x.shape
    Lc = ctx.shape[1]
    cos, sin = grid_rope(L, ROPE_DIM, x.dtype)
    silu_c = jax.nn.silu(c)
    silu_cc = jax.nn.silu(c_ctx)
    xc = ctx
    for i in range(DEPTH):
        m, j = i % N_MIXERS, i // N_MIXERS
        ctx_out = i < DEPTH - 1
        shift, scale, gate = jnp.split((silu_c @ ada_w[i] + ada_b[i])[:, None, :], 3, axis=-1)
        a = modulate(rmsnorm(x, norm_g[i]), shift, scale)
        if ctx_out or m in (0, 2):
            shift_c, scale_c, gate_c = jnp.split(silu_cc @ ada_w[i] + ada_b[i], 3, axis=-1)
            ac = modulate(rmsnorm(xc, norm_g[i]), shift_c, scale_c)
        yc = None
        if m == 0:
            y, yc = mla_mixer(a, ac, cos, sin, mla_w_in[j], mla_q_norm_g[j], mla_kv_norm_g[j],
                              mla_w_uq[j], mla_w_ukv[j], mla_w_out[j], ctx_out)
        elif m == 1:
            filt = (hy_filt_w_in[j], hy_filt_w_hid[j], hy_filt_b[j], hy_filt_freq[j], hy_filt_w_out[j])
            y = hyena_seq(a, hy_w_in[j], hy_conv_w[j], hy_conv_b[j],
                          hyena_filter_spectra(L, *filt), hy_bias[j], hy_w_out[j])
            if ctx_out:
                yc = hyena_seq(ac, hy_w_in[j], hy_conv_w[j], hy_conv_b[j],
                               hyena_filter_spectra(Lc, *filt), hy_bias[j], hy_w_out[j])
        elif m == 2:
            y, yc = swa_mixer(a, ac, cos, sin, swa_w_in[j], swa_sink[j], swa_w_out[j], ctx_out)
        else:
            y = conformer_seq(a, cf_w_in[j], cf_dw_w[j], cf_dw_b[j], cf_ln_g[j], cf_ln_b[j], cf_w_out[j])
            if ctx_out:
                yc = conformer_seq(ac, cf_w_in[j], cf_dw_w[j], cf_dw_b[j], cf_ln_g[j], cf_ln_b[j], cf_w_out[j])
        x = x + gate * y
        if ctx_out:
            xc = xc + gate_c * yc
    return rmsnorm(x, final_g)


def setup_inputs(seed=0):
    out = dict(first_inputs(seed))
    for name, value in second_inputs(seed + 1).items():
        if name != "x":
            out[name + "_2"] = value
    return out


def reference(
    x, hg_norm, hg_w_in, hg_lb_logits, hg_out_norm, hg_w_out, kv_norm, w_kv, attn_norm,
    attn_w_q, attn_sinks, attn_w_o, ffn_norm, ffn_w_up, ffn_conv_w, ffn_conv_b, ffn_w_down,
    final_norm, c_2, ctx_2, c_ctx_2, norm_g_2, ada_w_2, ada_b_2, final_g_2, mla_w_in_2,
    mla_q_norm_g_2, mla_kv_norm_g_2, mla_w_uq_2, mla_w_ukv_2, mla_w_out_2, hy_w_in_2,
    hy_conv_w_2, hy_conv_b_2, hy_filt_w_in_2, hy_filt_w_hid_2, hy_filt_b_2, hy_filt_freq_2,
    hy_filt_w_out_2, hy_bias_2, hy_w_out_2, swa_w_in_2, swa_sink_2, swa_w_out_2, cf_w_in_2,
    cf_dw_w_2, cf_dw_b_2, cf_ln_g_2, cf_ln_b_2, cf_w_out_2,
):
    x = first_block(
        x, hg_norm, hg_w_in, hg_lb_logits, hg_out_norm, hg_w_out, kv_norm, w_kv, attn_norm,
        attn_w_q, attn_sinks, attn_w_o, ffn_norm, ffn_w_up, ffn_conv_w, ffn_conv_b, ffn_w_down,
        final_norm,
    )
    return second_block(
        x, c_2, ctx_2, c_ctx_2, norm_g_2, ada_w_2, ada_b_2, final_g_2, mla_w_in_2,
        mla_q_norm_g_2, mla_kv_norm_g_2, mla_w_uq_2, mla_w_ukv_2, mla_w_out_2, hy_w_in_2,
        hy_conv_w_2, hy_conv_b_2, hy_filt_w_in_2, hy_filt_w_hid_2, hy_filt_b_2, hy_filt_freq_2,
        hy_filt_w_out_2, hy_bias_2, hy_w_out_2, swa_w_in_2, swa_sink_2, swa_w_out_2, cf_w_in_2,
        cf_dw_w_2, cf_dw_b_2, cf_ln_g_2, cf_ln_b_2, cf_w_out_2,
    )


_drawn_inputs = setup_inputs


def setup_inputs(seed=0):
    import zlib

    import numpy as np

    out = dict(_drawn_inputs(seed))
    spreads = {}
    factors = {'hg_norm': 2.819,
     'hg_lb_logits': 6.912,
     'hg_out_norm': 4.362,
     'kv_norm': 8.0,
     'attn_norm': 8.0,
     'attn_sinks': 2.993,
     'ffn_norm': 3.039,
     'ffn_conv_b': 4.276,
     'final_norm': 2.858,
     'ctx_2': 7.584,
     'c_ctx_2': 3.128,
     'norm_g_2': 8.0,
     'ada_b_2': 7.149,
     'final_g_2': 2.801,
     'mla_q_norm_g_2': 8.0,
     'mla_kv_norm_g_2': 8.0,
     'mla_w_uq_2': 3.449,
     'hy_conv_b_2': 8.0,
     'hy_filt_freq_2': 8.0}
    for name, (base, spread) in spreads.items():
        noise = np.random.default_rng([zlib.crc32(name.encode()), seed]).standard_normal(out[name].shape)
        drawn = base * np.exp(spread * noise) if base else spread * noise
        out[name] = __import__('jax').numpy.asarray(drawn.astype(out[name].dtype))
    for name, factor in factors.items():
        out[name] = (out[name] * factor).astype(out[name].dtype)
    return out
```

```python
from contextlib import ExitStack

import numpy as np

import concourse.bass as bass
from concourse import mybir

F = mybir.dt.float32
FR = mybir.dt.float32r
I32 = mybir.dt.int32
ALU = mybir.AluOpType
ACT = mybir.ActivationFunctionType
AX_X = mybir.AxisListType.X
MUL, ADD, SUB = ALU.mult, ALU.add, ALU.subtract

T = 512
D = 1024
KD = 8
FT = 22
HF = 11
TC = 256
RAW, HL = 4, 3
EPS = 1e-6
LV = 7


PAR = [("hg_norm", 8), ("lb0", 8), ("lb1", 8), ("out_norm", 1), ("kv_norm", 8), ("attn_norm", 8),
       ("ffn_norm0", 8), ("ffn_norm1", 8), ("final_norm", 8), ("norm_g0", 8), ("norm_g1", 8),
       ("final_g", 8), ("q_norm", 3), ("kvl_norm", 2), ("sink", 16), ("eps", 1),
       ("cw0", 66), ("cw1", 66), ("cb0", 22), ("cb1", 22), ("ada_b0", 24), ("ada_b1", 24),
       ("c", 8), ("cc", 8), ("hw", 72), ("hb", 24), ("hbias", 16), ("fb", 3), ("ff", 3)]
PC = {}
_n = 0
for _name, _w in PAR:
    PC[_name] = _n
    _n += _w
NPAR = _n


class Op:
    __slots__ = ("eng", "fn", "waits", "inc", "sem", "val")

    def __init__(self, eng, fn, waits, sem=None, val=0):
        self.eng, self.fn, self.waits, self.sem, self.val, self.inc = eng, fn, waits, sem, val, False


def flat(x, out):
    for y in x:
        if isinstance(y, Op):
            out.append(y)
        elif y:
            flat(y, out)
    return out


class Queues:

    def __init__(self):
        self.q = {e: [] for e in ("pe", "act", "dve", "pool", "sp")}
        self.dmas = {}

    def add(self, eng, fn, *waits):
        op = Op(eng, fn, flat(waits, []))
        self.q[eng].append(op)
        return op

    def dma(self, eng, fn, sem, *waits):
        self.dmas[sem] = self.dmas.get(sem, 0) + 16
        op = Op(eng, fn, flat(waits, []), sem, self.dmas[sem])
        self.q[eng].append(op)
        return op

    def count(self):
        for ops in self.q.values():
            for op in ops:
                for w in op.waits:
                    if w.sem is None:
                        w.inc = True
        for ops in self.q.values():
            n = 0
            for op in ops:
                if op.sem is None and op.inc:
                    n += 1
                    op.val = n

    def emit(self, name, eng, sems):
        seen = {}
        for op in self.q[name]:
            need = {}
            for w in op.waits:
                s = w.sem or w.eng
                need[s] = max(need.get(s, 0), w.val)
            for s, v in need.items():
                if seen.get(s, 0) < v:
                    eng.wait_ge(sems[s], v)
                    seen[s] = v
            ins = op.fn(eng)
            if op.sem is not None:
                ins.then_inc(sems[op.sem], 16)
            elif op.inc:
                ins.then_inc(sems[name], 1)


class Bank:

    def __init__(self, ap):
        self.ap, self.free = ap, []


class Tile:
    __slots__ = ("hi", "lo", "tok", "chunk")


class Weights:

    def __init__(self, Q, dram, raw, hi, lo, chunks, plain):
        self.Q, self.dram, self.raw, self.hi, self.lo, self.chunks = Q, dram, raw, hi, lo, chunks
        self.plain, self.found = plain, set()
        self.spec, self.split, self.last, self.load, self.done = [], {}, {}, {}, set()
        self.at = self.loaded = 0

    def fetch(self):
        while self.loaded < self.chunks:
            c, old = self.loaded, self.loaded - RAW
            if old >= 0 and old not in self.split and old not in self.done:
                return
            waits = [] if old < 0 else self.split.get(old) or self.last[old]
            dst, src = self.raw[:, c % RAW, :], self.dram[c]
            self.load[c] = self.Q.dma("sp", lambda e, dst=dst, src=src: e.dma_start(dst, src), f"w{c % RAW}", [waits])
            self.loaded += 1
            if old < 0 and self.loaded % RAW:
                return

    def prepare(self, c):
        if c >= self.chunks or c in self.split or c in self.plain or c in self.found:
            return
        old = next((self.last[p] for p in range(c - HL, -1, -HL) if p in self.split), None)
        r, hi, lo = self.raw[:, c % RAW, :], self.hi[:, c % HL, :], self.lo[:, c % HL, :]
        a = self.Q.add("act", lambda e: e.activation(hi, r, ACT.Copy), self.load[c], old)
        v = self.Q.add("dve", lambda e: e.tensor_tensor(lo, r, hi.bitcast(F), SUB), a, old)
        self.split[c] = [a, v]
        self.fetch()

    def tiles(self, names):
        n, at = len(names), self.at
        c = at // 8
        assert (at + n - 1) // 8 == c
        if at % 8 == 0:
            self.prepare(c)
            self.prepare(c + 1)
        self.spec += names
        self.at += n
        t = Tile()
        o = at % 8 * 128
        t.hi, t.lo = self.hi[:, c % HL, o:o + n * 128], self.lo[:, c % HL, o:o + n * 128]
        t.tok, t.chunk = self.split.get(c, []), c
        return t

    def tile(self, name, k, m):
        return self.tiles([(name, k, m)])

    def whole(self, names):
        assert self.at % 8 == 0 and len(names) == 8
        c = self.at // 8
        self.found.add(c)
        self.prepare(c + 1)
        self.spec += names
        self.at += 8
        t = Tile()
        t.hi, t.lo, t.tok, t.chunk = self.raw[:, c % RAW, :], None, [self.load[c]], c
        return t

    def used(self, t, op):
        self.last[t.chunk] = op

    def finished(self, t):
        self.done.add(t.chunk)
        self.fetch()

    def align(self):
        while self.at % 8:
            self.spec.append(None)
            self.at += 1


def weave(main, side, per=1):
    side = iter(side) if side is not None else iter(())
    for _ in main:
        for _ in range(per):
            next(side, None)
    for _ in side:
        pass


def build(nc, A, chunks, plain, stage=99):
    Q = Queues()
    ctx = ExitStack()

    def sbt(stack, name, shape, dt=F):
        return stack.enter_context(nc.sbuf_tensor(name, shape, dt))

    def sb(name, shape, dt=F):
        return sbt(ctx, name, shape, dt)

    PE = lambda fn, *w: Q.add("pe", fn, *w)
    AC = lambda fn, *w: Q.add("act", fn, *w)
    V = lambda fn, *w: Q.add("dve", fn, *w)
    G = lambda fn, *w: Q.add("pool", fn, *w)

    def fence():
        return [Q.q[e][-1] for e in ("pe", "act", "dve", "pool") if Q.q[e]]

    hT = sb("hT", [128, KD, T])
    raw = sb("raw", [128, RAW, 1024])
    whi = sb("whi", [128, HL, 1024], FR)
    wlo = sb("wlo", [128, HL, 1024], FR)
    nhi = sb("nhi", [128, KD, T], FR)
    nlo = sb("nlo", [128, KD, T], FR)
    par = sb("par", [128, NPAR])
    ident = sb("ident", [128, 128])
    ones = sb("ones", [128, 128])
    rb = sb("rb", [128, T])
    rb2 = sb("rb2", [128, T])
    rc = sb("rc", [128, 8])
    sd = sb("sd", [128, 8])
    diag = sb("diag", [128, 4, 128])
    sqb = sb("sqb", [128, 2, T])
    lb = sb("lb", [128, 8, 8])
    PS = ctx.enter_context(nc.psum_tensor("PS", [128, 8 * 512], F))
    bank = [Bank(PS[:, 512 * i:512 * i + 512]) for i in range(8)]
    pc = lambda name, i=0: par[:, PC[name] + i:PC[name] + i + 1]

    W = Weights(Q, A["stream"], raw, whi, wlo, chunks, plain)

    par_l = Q.dma("sp", lambda e: e.dma_start(par[:, :], A["par"]), "par")
    x_l = []
    for m in range(KD):
        if m == 2:
            W.fetch()
        x_l.append(Q.dma("sp", lambda e, m=m: e.dma_start(hT[:, m, :], A["xT"][m]), f"x{m}"))
    id_l = Q.dma("sp", lambda e: e.dma_start(ident[:, :], A["ident"]), "id")
    for _ in range(RAW - 1):
        W.fetch()
    one_o = V(lambda e: e.memset(ones[:, :], 1.0))

    def mm_w(out, w, xh, xl, first, last, *waits):
        PE(lambda e: e.matmul(out, w.hi, xh, start=first, stop=False), w.tok, waits)
        PE(lambda e: e.matmul(out, w.hi, xl, start=False, stop=False))
        op = PE(lambda e: e.matmul(out, w.lo, xh, start=False, stop=last))
        W.used(w, op)
        return op

    def mm_x(out, w, xh, xl, first, last, *waits):
        PE(lambda e: e.matmul(out, xh, w.hi, start=first, stop=False), w.tok, waits)
        PE(lambda e: e.matmul(out, xh, w.lo, start=False, stop=False))
        op = PE(lambda e: e.matmul(out, xl, w.hi, start=False, stop=last))
        W.used(w, op)
        return op

    class State:
        pass

    st = State()
    st.n_tok = [[] for _ in range(KD)]
    st.n_free = []
    st.h_tok = [[x_l[m]] for m in range(KD)]
    st.h_read = [[] for _ in range(KD)]
    st.sq_free = [[], []]
    st.rb_free = []
    st.sc_free = []
    stat = bank[7]

    def project(b, name, m, ks=KD, k0=0, hi=None, lo=None, tok=None):
        hi, lo, tok = (nhi, nlo, st.n_tok) if hi is None else (hi, lo, tok)
        free = b.free
        for k in range(ks):
            w = W.tile(name, k0 + k, m)
            op = mm_w(b.ap, w, hi[:, k, :], lo[:, k, :], k == 0, k == ks - 1, tok[k], free if k == 0 else None)
            yield
        b.op = op

    def run(gen):
        for _ in gen:
            pass

    def square_in(m, src, waits, first, last, nt=4, width=T, col=0):
        s = m % 2
        dst = sqb[:, s, 0:width]
        q = AC(lambda e: e.activation(dst, src, ACT.Square), waits, st.sq_free[s])
        for t in range(nt):
            op = PE(lambda e, t=t: e.matmul(stat.ap[:, col + t:col + t + 1], sqb[:, s, 128 * t:128 * t + 128],
                                            ones[:, 0:1], start=first and t == 0, stop=last, skip_group_check=True),
                    q if t == 0 else None, one_o, stat.free if first and t == 0 else None)
        st.sq_free[s] = [op]
        return q, op

    def root(op, nt, width, dst_c, dst_b, col=0, scale2=None, free=()):
        a = AC(lambda e: e.activation(sd[:, 0:nt], stat.ap[:, col:col + nt], ACT.Sqrt, bias=pc("eps"),
                                      scale=1.0 / width), op, par_l, st.sc_free)
        r = V(lambda e: e.reciprocal(dst_c[:, 0:nt], sd[:, 0:nt]), a, free)
        out, prev = [], st.sc_free
        for g in range(0, nt, 4):
            n = min(4, nt - g)
            c = slice(128 * g, 128 * (g + n))
            d = V(lambda e, g=g, n=n: e.tensor_tensor(
                diag[:, 0:n, :], ident[:, :].unsqueeze(1).to_broadcast((128, n, 128)),
                dst_c[:, g:g + n].unsqueeze(2).to_broadcast((128, n, 128)), MUL), r, id_l, prev)
            p = PE(lambda e, n=n: e.matmul(stat.ap[:, 0:128 * n], ones[:, :],
                                           diag[:, 0:n, :].rearrange("p a b -> p (a b)"), start=True, stop=True),
                   d, a, out)
            prev = [p]
            o = [AC(lambda e, c=c, n=n: e.activation(dst_b[0][:, c], stat.ap[:, 0:128 * n], ACT.Copy), p, free)]
            if scale2 is not None:
                o.append(AC(lambda e, c=c, n=n: e.activation(dst_b[1][:, c], stat.ap[:, 0:128 * n], ACT.Copy,
                                                             scale=scale2), p, free))
            out = out + o
        stat.free = out
        st.sc_free = [p, a, r]
        st.r_tok = out + [r]
        return st.r_tok

    def split_scaled(src, gain, dh, dl, *waits):
        a = AC(lambda e: e.activation(dh, src, ACT.Copy, scale=gain), waits)
        v = V(lambda e: e.scalar_tensor_tensor(dl, src, gain, dh.bitcast(F), MUL, SUB), a, waits)
        return [a, v]

    def split(src, dh, dl, *waits):
        a = AC(lambda e: e.activation(dh, src, ACT.Copy), waits)
        v = V(lambda e: e.tensor_tensor(dl, src, dh.bitcast(F), SUB), a, waits)
        return [a, v]

    def after(gain):
        def go(m):
            q, op = square_in(m, hT[:, m, :], st.h_tok[m], m == 0, m == KD - 1)
            st.n_tok[m] = split_scaled(hT[:, m, :], pc(gain, m), nhi[:, m, :], nlo[:, m, :], st.h_tok[m],
                                       par_l, st.n_free)
            st.h_read[m] = [q] + st.n_tok[m]
            return op
        return go

    def residual(m, b, scale=None):
        h = hT[:, m, :]
        if scale is None:
            v = V(lambda e: e.tensor_tensor(h, h, b.ap, ADD), b.op, st.h_tok[m], st.h_read[m])
        else:
            v = V(lambda e: e.scalar_tensor_tensor(h, b.ap, scale, h, MUL, ADD), b.op, st.h_tok[m], st.h_read[m],
                  st.ada_tok)
        b.free = [v]
        st.h_tok[m] = [v]

    l0, l1 = par[:, PC["lb0"]:PC["lb0"] + 8], par[:, PC["lb1"]:PC["lb1"] + 8]
    go = after("hg_norm")
    for m in range(KD):
        op = go(m)
    root(op, 4, D, rc, (rb, rb2), scale2=0.5 * 128 ** -0.5)
    o = V(lambda e: e.tensor_tensor(lb[:, 0, :], l0, l1, ALU.max), par_l)
    o1 = V(lambda e: e.tensor_tensor(lb[:, 1, :], l0, lb[:, 0, :], SUB), o)
    o2 = V(lambda e: e.tensor_tensor(lb[:, 2, :], l1, lb[:, 0, :], SUB), o)
    o1 = AC(lambda e: e.activation(lb[:, 3, :], lb[:, 1, :], ACT.Exp), o1)
    o2 = AC(lambda e: e.activation(lb[:, 4, :], lb[:, 2, :], ACT.Exp), o2)
    o = V(lambda e: e.tensor_tensor(lb[:, 5, :], lb[:, 3, :], lb[:, 4, :], ADD), o1, o2)
    o = V(lambda e: e.reciprocal(lb[:, 6, :], lb[:, 5, :]), o)
    o = V(lambda e: e.tensor_tensor(lb[:, 7, :], lb[:, 3, :], lb[:, 6, :], MUL), o)
    o = V(lambda e: e.tensor_scalar(lb[:, 0, :], lb[:, 7, :], -0.5, 0.5, MUL, ADD), o)
    lb_o = V(lambda e: e.tensor_tensor(lb[:, 1, :], lb[:, 7, :], lb[:, 0, :], ADD), o)

    def hgrn():
        ph = ExitStack()
        p = lambda name, shape, dt=F: sbt(ph, name, shape, dt)
        v = p("v", [128, 4, D])
        ohi = p("ohi", [128, KD, T], FR)
        olo = p("olo", [128, KD, T], FR)
        tq = p("tq", [128, 2, T])
        th = p("th", [128, 2, T])
        q = p("q", [128, 2, T])
        ff = p("ff", [128, 2, T])
        kk = p("kk", [128, 2, T])
        sg = p("sg", [128, 2, T])
        qa = p("qa", [128, T])
        fb = p("fb", [128, T])
        sc = p("sc", [128, 4, 128])
        kt = p("kt", [128, 3, 128])
        S = p("S", [128, 3, 128])
        og = p("og", [128, 2, T])
        mask = p("mask", [128, LV + 1, 128])
        mk = Q.dma("sp", lambda e: e.dma_start(mask[:, :, :], A["masks"]), "mask")
        z = V(lambda e: e.memset(sc[:, :, :], 0.0))
        r = st.r_tok

        v_tok = []
        for g in range(2):
            bs = bank[0:4] if g == 0 else bank[3:7]
            bs = [bank[4 * g + t] if 4 * g + t < 7 else bank[0] for t in range(4)]
            for k in range(KD):
                w = W.tiles([("w_in", k, 16 + 4 * g + j) for j in range(4)])
                for t in range(4):
                    s = slice(128 * t, 128 * t + 128)
                    op = mm_x(bs[t].ap, w, nhi[:, k, s], nlo[:, k, s], k == 0, k == KD - 1, st.n_tok[k],
                              bs[t].free if k == 0 else None)
                    bs[t].op = op
            for t in range(4):
                b = bs[t]
                a = AC(lambda e, t=t, b=b, g=g: e.activation(v[:, t, 512 * g:512 * g + 512], b.ap, ACT.Copy,
                                                        scale=rc[:, t:t + 1]), b.op, r)
                b.free = [a]
                v_tok.append(a)

        st.q_free = [[], []]
        st.sg_free = [[], []]
        st.o_tok = [None] * KD

        def proj(h):
            s = h % 2
            bq, bf, bg = bank[0], bank[1], bank[2]
            old = st.q_free[s]
            yield from project(bq, "w_in", h)
            a = V(lambda e: e.tensor_tensor(tq[:, 0, :], bq.ap, rb2[:, :], MUL), bq.op, r, st.t_free)
            bq.free = [a]
            b = AC(lambda e: e.activation(th[:, 0, :], tq[:, 0, :], ACT.Tanh, scale=128 ** 0.5), a, st.t_free)
            qo = V(lambda e: e.scalar_tensor_tensor(q[:, s, :], th[:, 0, :], 1.0, tq[:, 0, :], ADD, MUL), b, old)
            yield from project(bf, "w_in", 8 + h)
            a = V(lambda e: e.tensor_tensor(tq[:, 1, :], bf.ap, rb[:, :], MUL), bf.op, st.t_free)
            bf.free = [a]
            b = AC(lambda e: e.activation(th[:, 1, :], tq[:, 1, :], ACT.Tanh, scale=0.5), a, st.t_free)
            f = V(lambda e: e.tensor_scalar(ff[:, s, :], th[:, 1, :], lb[:, 0, h:h + 1], lb[:, 1, h:h + 1], MUL, ADD),
                  b, lb_o, old)
            ko = V(lambda e: e.tensor_scalar(kk[:, s, :], ff[:, s, :], -1.0, 1.0, MUL, ADD), f)
            st.t_free = [qo]
            st.qkf = [qo, f, ko]
            yield from project(bg, "w_in", 24 + h)
            a = V(lambda e: e.tensor_tensor(tq[:, 0, :], bg.ap, rb[:, :], MUL), bg.op, qo)
            bg.free = [a]
            b = AC(lambda e: e.activation(th[:, 0, :], tq[:, 0, :], ACT.Tanh, scale=0.5), a, qo)
            g = V(lambda e: e.scalar_tensor_tensor(sg[:, s, :], th[:, 0, :], 1.0, tq[:, 0, :], ADD, MUL), b,
                  st.sg_free[s])
            st.t_free = [g, f]
            st.sg_tok = [g]

        st.t_free = []
        st.kt_free, st.S_free, st.og_free = [], [], []
        st.sc_tok = [z]

        def scan(h):
            s = h % 2
            qq, kx, fx = q[:, s, :], kk[:, s, :], ff[:, s, :]
            qo, fo, ko = st.qkf
            sgt = st.sg_tok
            hc = slice(128 * h, 128 * h + 128)

            def scores(level, b, qx, *waits):
                for c in range(4):
                    cs = slice(128 * c, 128 * c + 128)
                    op = PE(lambda e, cs=cs: e.matmul(b.ap[:, cs], kx[:, cs], qx[:, cs], start=True, stop=True),
                            waits if c == 0 else None, b.free if c == 0 else None)
                cp = V(lambda e: e.copy_predicated(sc[:, :, :],
                                                   mask[:, level, :].bitcast(I32).unsqueeze(1).to_broadcast((128, 4, 128)),
                                                   b.ap.rearrange("p (c t) -> p c t", c=4)), op, mk, st.sc_tok)
                st.sc_tok = [cp]
                b.free = [cp]
                return op, cp

            a = V(lambda e: e.tensor_tensor(qa[:, :], qq, fx, MUL), qo, fo, st.qa_free)
            yield
            op, cp = scores(0, bank[3], qq, qo, ko)
            cps = [cp]
            yield
            qt, kt_, ft = [a], [ko], [fo]
            fsrc = fx
            for lv in range(LV):
                b = 1 << lv
                op, cp = scores(lv + 1, bank[4 - lv % 2], qa, qt, kt_)
                cps.append(cp)
                n = T // (2 * b)
                fs = fsrc[:, 0:2 * n].rearrange("p (n a) -> p n a", a=2)
                qv = qa[:, :].rearrange("p (n a b) -> p n a b", a=2, b=b)
                kv = kx.rearrange("p (n a b) -> p n a b", a=2, b=b)
                sh = (128, n, b)
                qt = [V(lambda e, qv=qv, fs=fs, sh=sh: e.tensor_tensor(
                    qv[:, :, 1, :], qv[:, :, 1, :], fs[:, :, 0:1].to_broadcast(sh), MUL), op, qt, ft)]
                kt_ = [G(lambda e, kv=kv, fs=fs, sh=sh: e.tensor_tensor(
                    kv[:, :, 0, :], kv[:, :, 0, :], fs[:, :, 1:2].to_broadcast(sh), MUL), op, kt_, ft)]
                o0 = 0 if lv % 2 == 0 else 256
                fdst = fb[:, o0:o0 + n]
                ft = [G(lambda e, fs=fs, fdst=fdst, n=n: e.tensor_tensor(
                    fdst.unsqueeze(2), fs[:, :, 0:1], fs[:, :, 1:2], MUL), ft, st.fb_free, qt)]
                fsrc = fdst
                yield
            b3 = bank[3]
            for c in range(3):
                cs = slice(128 * c, 128 * c + 128)
                op = PE(lambda e, cs=cs: e.transpose(b3.ap[:, cs], kx[:, cs], ident[:, :]), kt_, b3.free, id_l)
            a = AC(lambda e: e.activation(kt[:, :, :].rearrange("p a b -> p (a b)"), b3.ap[:, 0:384], ACT.Copy),
                   op, st.kt_free)
            b3.free = [a]
            yield
            b4 = bank[4]
            for c in range(3):
                cs = slice(128 * c, 128 * c + 128)
                op = PE(lambda e, c=c, cs=cs: e.matmul(b4.ap[:, cs], kt[:, c, :], v[:, c, hc], start=True, stop=True),
                        a, b4.free, v_tok)
            st.kt_free = [op]
            so = [V(lambda e: e.tensor_copy(S[:, 0, :], b4.ap[:, 0:128]), op, st.S_free)]
            for c in (1, 2):
                so.append(V(lambda e, c=c: e.scalar_tensor_tensor(S[:, c, :], S[:, c - 1, :], fsrc[:, c:c + 1],
                                                                  b4.ap[:, 128 * c:128 * c + 128], MUL, ADD),
                            so[-1], ft, st.S_free))
            b4.free = [so[-1]]
            st.fb_free = [so[-1]]
            yield
            bo = bank[5 + h % 2]
            for c in range(4):
                cs = slice(128 * c, 128 * c + 128)
                op = PE(lambda e, c=c, cs=cs: e.matmul(bo.ap[:, cs], v[:, c, hc], sc[:, c, :], start=True,
                                                       stop=c == 0), bo.free, cps, v_tok)
                st.sc_tok = st.sc_tok + [op]
                if c:
                    op = PE(lambda e, c=c, cs=cs: e.matmul(bo.ap[:, cs], S[:, c - 1, :], qa[:, cs], start=False,
                                                           stop=True), so[c - 1], qt)
            st.S_free = st.qa_free = [op]
            st.q_free[s] = [op, kt_[0], ft[0], qt[0]]
            yield
            qs, op = square_in(h, bo.ap, op, True, True)
            yield
            rt = root(op, 4, 128, rch, (rbh,), free=st.og_free)
            a = V(lambda e: e.scalar_tensor_tensor(og[:, 0, :], bo.ap, pc("out_norm"), rbh[:, :], MUL, MUL), rt, qs,
                  st.og_free)
            bo.free = [a]
            m = V(lambda e: e.scalar_tensor_tensor(og[:, 1, :], og[:, 0, :], 0.5, sg[:, s, :], MUL, MUL), a, sgt,
                  st.og_free)
            st.sg_free[s] = [m]
            st.o_tok[h] = split(og[:, 1, :], ohi[:, h, :], olo[:, h, :], m)
            st.og_free = [a] + st.o_tok[h]
            yield

        st.qa_free, st.fb_free = [], []
        rch = p("rch", [128, 4])
        rbh = p("rbh", [128, T])
        run(proj(0))
        for h in range(KD):
            nxt = proj(h + 1) if h + 1 < KD else None
            weave(scan(h), nxt, 2)
        st.n_free = [Q.q["pe"][-1]]
        go = after("ffn_norm0")
        for m in range(KD):
            b = bank[m % 4]
            run(project(b, "w_out", m, hi=ohi, lo=olo, tok=st.o_tok))
            residual(m, b)
            op = go(m)
        root(op, 4, D, rc, (rb, rb2), scale2=0.5)
        ph.close()

    def ffn(layer, go):
        ph = ExitStack()
        f0 = fence()
        p = lambda name, shape, dt=F: sbt(ph, f"{name}_f{layer}", shape, dt)
        hh = p("hh", [128, HF, T], FR)
        hl = p("hl", [128, HF, T], FR)
        gp = p("gp", [128, 2, T + 2])
        t = p("t", [128, 6, 2, T])
        up, dn = f"up{layer}", f"down{layer}"
        z = V(lambda e: e.memset(gp[:, :, 0:2], 0.0), f0)
        r = st.r_tok
        cw, cb = f"cw{layer}", f"cb{layer}"
        gfree, tfree = [[z], [z]], [f0, f0]
        hid, hfree = [None] * HF, f0

        def tail(f, bg, bv):
            s, i = f % 2, f % HF
            g = V(lambda e: e.tensor_tensor(gp[:, s, 2:T + 2], bg.ap, rb[:, :], MUL), bg.op, r, gfree[s])
            bg.free = [g]
            c0 = AC(lambda e: e.activation(t[:, 0, s, :], gp[:, s, 2:T + 2], ACT.Identity, bias=pc(cb, f),
                                           scale=pc(cw, 44 + f)), g, tfree[s])
            c1 = V(lambda e: e.scalar_tensor_tensor(t[:, 1, s, :], gp[:, s, 1:T + 1], pc(cw, 22 + f), t[:, 0, s, :],
                                                    MUL, ADD), c0, tfree[s])
            c2 = V(lambda e: e.scalar_tensor_tensor(t[:, 2, s, :], gp[:, s, 0:T], pc(cw, f), t[:, 1, s, :],
                                                    MUL, ADD), c1)
            gfree[s] = [c0, c2]
            vv = V(lambda e: e.tensor_tensor(t[:, 4, s, :], bv.ap, rb2[:, :], MUL), bv.op)
            bv.free = [vv]
            th = AC(lambda e: e.activation(t[:, 3, s, :], t[:, 2, s, :], ACT.Tanh, scale=0.5), c2)
            s2 = V(lambda e: e.scalar_tensor_tensor(t[:, 0, s, :], t[:, 3, s, :], 1.0, t[:, 2, s, :], ADD, MUL), th)
            mo = V(lambda e: e.tensor_tensor(t[:, 5, s, :], t[:, 0, s, :], t[:, 4, s, :], MUL), s2, vv)
            hid[i] = split(t[:, 5, s, :], hh[:, i, :], hl[:, i, :], mo, hfree)
            tfree[s] = hid[i]

        for half in range(2):
            for f in range(half * HF, half * HF + HF):
                bg, bv = bank[2 * f % 6], bank[(2 * f + 1) % 6]
                run(project(bg, up, f))
                run(project(bv, up, FT + f))
                tail(f, bg, bv)
            if half:
                st.n_free = [Q.q["pe"][-1]]
            for m in range(KD):
                b = bank[m % 6]
                run(project(b, dn, m, ks=HF, k0=half * HF, hi=hh, lo=hl, tok=hid))
                residual(m, b)
                if half:
                    op = go(m)
            hfree = [Q.q["pe"][-1]]
        ph.close()
        return op

    def swa(go):
        ph = ExitStack()
        f0 = fence()
        p = lambda name, shape, dt=F: sbt(ph, name + "_s", shape, dt)
        khi = p("khi", [128, KD, T], FR)
        klo = p("klo", [128, KD, T], FR)
        kz = p("kz", [128, 2, 2, T + 128])
        vz = p("vz", [128, 4, 2, 2, 128])
        qb = p("qb", [128, 2, T])
        s = p("s", [128, 8, 256])
        pt = p("pt", [128, 4, 512])
        dist = p("dist", [128, 2, 256])
        sm = p("sm", [128, 8, 8])
        ds = Q.dma("sp", lambda e: e.dma_start(dist[:, :, :], A["dist"]), "dist", f0)
        zk = V(lambda e: e.memset(kz[:, :, :, :], 0.0), f0)
        zv = V(lambda e: e.memset(vz[:, :, :, :, :], 0.0), f0)
        sink = par[:, PC["sink"]:PC["sink"] + 16]

        ktok = [split_scaled(hT[:, k, :], pc("kv_norm", k), khi[:, k, :], klo[:, k, :], st.h_tok[k], f0)
                for k in range(KD)]
        for k in range(KD):
            st.h_read[k] = st.h_read[k] + ktok[k]
        q_tok, q_free = [None, None], [f0, f0]

        def proj(i):
            b = bank[7]
            yield from project(b, "wq", i)
            q_tok[i % 2] = V(lambda e: e.tensor_tensor(qb[:, i % 2, :], b.ap, rb2[:, :], MUL), b.op, st.r_tok,
                             q_free[i % 2])
            b.free = [q_tok[i % 2]]

        run(proj(0))
        kt = []
        for n in range(2):
            b = bank[n]
            run(project(b, "kv", n, hi=khi, lo=klo, tok=ktok))
            for e_ in range(2):
                ps = slice(64 * e_, 64 * e_ + 64)
                o = V(lambda e, n=n, e_=e_, ps=ps, b=b: e.tensor_tensor(kz[ps, n, e_, 128:T + 128], b.ap[ps, :],
                                                                        rb[ps, :], MUL), b.op, st.r_tok, zk)
                kt.append(o)
            b.free = [o]
        bs = bank[2:6]
        for k in range(KD):
            w = W.tile("kv", k, 2)
            for t in range(4):
                c = slice(128 * t, 128 * t + 128)
                bs[t].op = mm_x(bs[t].ap[:, 0:128], w, khi[:, k, c], klo[:, k, c], k == 0, k == KD - 1, ktok[k],
                                bs[t].free if k == 0 else None)
        kv_read = [bs[3].op]
        vt = []
        for t in range(4):
            for e_ in range(2):
                o = AC(lambda e, t=t, e_=e_: e.activation(
                    vz[:, t, :, e_, 64 * e_:64 * e_ + 64], bs[t].ap[:, 0:128].rearrange("p (a d) -> p a d", a=2),
                    ACT.Copy, scale=rc[:, t:t + 1]), bs[t].op, st.r_tok, zv)
                vt.append(o)
            bs[t].free = [o]
        on_tok = [None] * KD
        fr = {"s": f0, "pt": [f0] * 4, "sm": f0}

        def attend(i):
            kv, z = i // 4, i % 2
            sc_o = []
            for blk in range(4):
                b = bank[blk]
                for e_ in range(2):
                    op = PE(lambda e, b=b, e_=e_, blk=blk: e.matmul(
                        b.ap[:, 256 * e_:256 * e_ + 256], qb[:, z, 128 * blk:128 * blk + 128],
                        kz[:, kv, e_, 128 * blk:128 * blk + 256], start=True, stop=True), q_tok[z], kt, b.free)
                for e_ in range(2):
                    slope = float(np.float32(2.0 ** (-8.0 * (2 * i + e_ + 1) / 16)))
                    o = V(lambda e, b=b, e_=e_, blk=blk, slope=slope: e.scalar_tensor_tensor(
                        s[:, 2 * blk + e_, :], dist[:, min(blk, 1), :], -slope, b.ap[:, 256 * e_:256 * e_ + 256],
                        MUL, ADD), op, ds, fr["s"])
                    sc_o.append(o)
                b.free = [o]
                yield
            q_free[z] = [op]
            mx = V(lambda e: e.tensor_reduce(sm[:, 0, :], s[:, :, :], AX_X, ALU.max), sc_o, fr["sm"])
            sk = sink[:, 2 * i:2 * i + 2].unsqueeze(1).to_broadcast((128, 4, 2))
            v4 = lambda j: sm[:, j, :].rearrange("p (b h) -> p b h", h=2)
            o = V(lambda e: e.tensor_tensor(v4(1), v4(0), sk, ALU.max), mx, fr["sm"])
            nm = V(lambda e: e.tensor_scalar(sm[:, 2, :], sm[:, 1, :], -1.0, None, MUL), o, fr["sm"])
            d = V(lambda e: e.tensor_tensor(v4(3), v4(2), sk, ADD), nm, fr["sm"])
            ex = []
            for j in range(8):
                ex.append(AC(lambda e, j=j: e.activation(s[:, j, :], s[:, j, :], ACT.Exp, bias=sm[:, 2, j:j + 1],
                                                         accum_out=sm[:, 4, j:j + 1]), nm, mx, fr["sm"]))
            es = AC(lambda e: e.activation(sm[:, 5, :], sm[:, 3, :], ACT.Exp), d, fr["sm"])
            yield
            o = V(lambda e: e.tensor_tensor(sm[:, 6, :], sm[:, 4, :], sm[:, 5, :], ADD), es, ex)
            rd = V(lambda e: e.reciprocal(sm[:, 7, :], sm[:, 6, :]), o)
            pn = [V(lambda e, j=j: e.tensor_scalar(s[:, j, :], s[:, j, :], sm[:, 7, j:j + 1], None, MUL), rd, ex[j])
                  for j in range(8)]
            fr["sm"] = [pn[-1], es]
            yield
            b6 = bank[6]
            for blk in range(4):
                b = bank[4 + blk % 2]
                for j in range(4):
                    op = PE(lambda e, b=b, j=j, blk=blk: e.transpose(
                        b.ap[:, 128 * j:128 * j + 128], s[:, 2 * blk + j // 2, 128 * (j % 2):128 * (j % 2) + 128],
                        ident[:, :]), pn[2 * blk + j // 2], b.free, id_l)
                fr["s"] = [op]
                c = AC(lambda e, b=b, blk=blk: e.activation(pt[:, blk, :], b.ap, ACT.Copy), op, fr["pt"][blk])
                b.free = [c]
                yield
                todo = [(e_, kb) for e_ in range(2) for kb in range(2) if blk or kb]
                for n, (e_, kb) in enumerate(todo):
                    op = PE(lambda e, n=n, e_=e_, kb=kb, blk=blk, last=len(todo) - 1: e.matmul(
                        b6.ap[:, 128 * blk:128 * blk + 128], vz[:, blk - 1 + kb, kv, e_, :],
                        pt[:, blk, 128 * (2 * e_ + kb):128 * (2 * e_ + kb) + 128], start=n == 0, stop=n == last),
                        c, vt, b6.free if blk == 0 else None)
                fr["pt"][blk] = [op]
            on_tok[i] = split(b6.ap, khi[:, i, :], klo[:, i, :], op, kv_read)
            b6.free = on_tok[i]
            yield

        for i in range(KD):
            weave(attend(i), proj(i + 1) if i + 1 < KD else None, 1)
        st.n_free = [Q.q["pe"][-1]]
        for m in range(KD):
            b = bank[m % 4]
            run(project(b, "wo", m, hi=khi, lo=klo, tok=on_tok))
            residual(m, b)
            op = go(m)
        ph.close()
        return op

    scv = sb("scv", [128, 3, KD, 2])
    ada = sb("ada", [128, 24, 2])
    gs = sb("gs", [128, KD, 2])
    cv = par[:, PC["c"]:PC["c"] + 16].rearrange("p (v k) -> p k v", v=2)
    a_ = AC(lambda e: e.activation(scv[:, 0], cv, ACT.Tanh, scale=0.5), par_l)
    a_ = V(lambda e: e.scalar_tensor_tensor(scv[:, 1], scv[:, 0], 1.0, cv, ADD, MUL), a_)
    sc_o = V(lambda e: e.tensor_scalar(scv[:, 2], scv[:, 1], 0.5, None, MUL), a_)
    st.ada_tok, st.ada_read = [], []

    def adapt(layer, b, nv):
        for m in range(24):
            w = W.whole([(f"ada{layer}", k, m) for k in range(KD)])
            for k in range(KD):
                op = PE(lambda e, w=w, k=k, m=m: e.matmul(b.ap[:, 2 * m:2 * m + nv], w.hi[:, 128 * k:128 * k + 128],
                                                          scv[:, 2, k, 0:nv], start=k == 0, stop=k == KD - 1),
                        w.tok, sc_o, b.free)
            W.used(w, op)
            W.finished(w)
            yield
        bias = par[:, PC[f"ada_b{layer}"]:PC[f"ada_b{layer}"] + 24].unsqueeze(2).to_broadcast((128, 24, nv))
        o = V(lambda e: e.tensor_tensor(ada[:, :, 0:nv], b.ap[:, 0:48].rearrange("p (m v) -> p m v", v=2)[:, :, 0:nv],
                                        bias, ADD), op, st.ada_read, par_l)
        b.free = [o]
        g = par[:, PC[f"norm_g{layer}"]:PC[f"norm_g{layer}"] + 8].unsqueeze(2).to_broadcast((128, KD, nv))
        o1 = V(lambda e: e.tensor_scalar(gs[:, :, 0:nv], ada[:, 8:16, 0:nv], 1.0, None, ADD), o, st.ada_read)
        o2 = V(lambda e: e.tensor_tensor(gs[:, :, 0:nv], gs[:, :, 0:nv], g, MUL), o1)
        st.ada_tok = [o, o2]

    def modulated(src, r, dh, dl, k, v, tmp, n, waits, tfree, dfree):
        a = V(lambda e: e.tensor_tensor(tmp[:, 0, 0:n], src, r, MUL), waits, tfree)
        u = V(lambda e: e.tensor_scalar(tmp[:, 1, 0:n], tmp[:, 0, 0:n], gs[:, k, v:v + 1], ada[:, k, v:v + 1],
                                        MUL, ADD), a, st.ada_tok, tfree)
        return a, split(tmp[:, 1, 0:n], dh, dl, u, dfree)

    def only_squares(m):
        q, op = square_in(m, hT[:, m, :], st.h_tok[m], m == 0, m == KD - 1)
        st.h_read[m] = [q]
        return op

    def end_first():
        for m in range(KD):
            h = hT[:, m, :]
            o = V(lambda e, h=h, m=m: e.scalar_tensor_tensor(h, h, pc("final_norm", m), rb[:, :], MUL, MUL),
                  st.h_tok[m], st.h_read[m], st.r_tok)
            st.h_tok[m] = [o]
            op = only_squares(m)
        return op, o

    def mla(go):
        ph = ExitStack()
        f0 = fence()
        p = lambda name, shape, dt=F: sbt(ph, name + "_m", shape, dt)
        cqh, cql = p("cqh", [128, 3, T], FR), p("cql", [128, 3, T], FR)
        ckh, ckl = p("ckh", [128, 2, T + TC], FR), p("ckl", [128, 2, T + TC], FR)
        v = p("v", [128, 6, D])
        krz = p("krz", [128, 2, T + TC])
        cs = p("cs", [128, 2, T])
        rbq = rb2
        rbk = p("rbk", [128, T + TC])
        rcq, rck = p("rcq", [128, 4]), p("rck", [128, 6])
        ph2 = ExitStack()
        p2 = lambda name, shape, dt=F: sbt(ph2, name + "_m", shape, dt)
        ctx_t = p2("ctx", [128, KD, TC])
        chi, clo = p2("chi", [128, KD, TC], FR), p2("clo", [128, KD, TC], FR)
        tmp = p2("tmp", [128, 2, 2, T])
        tmc = p2("tmc", [128, 2, 2, TC])
        rbc = p2("rbc", [128, TC])
        krt = p2("krt", [64, 2, T])
        cl = Q.dma("sp", lambda e: e.dma_start(ctx_t[:, :, :], A["ctx"]), "ctx", f0)
        rl = Q.dma("sp", lambda e: e.dma_start(cs[:, :, :], A["rope"]), "rope", f0)
        z = V(lambda e: e.memset(krz[:, :, :], 0.0), f0)

        ad = adapt(0, bank[0], 2)
        step = lambda n: [next(ad, None) for _ in range(n)]
        step(6)
        op, o = end_first()
        step(6)
        r_x = root(op, 4, D, rc, (rb,), free=o)
        for k in range(KD):
            q, op = square_in(k, ctx_t[:, k, :], [cl, f0], k == 0, k == KD - 1, nt=2, width=TC)
        step(6)
        r_c = root(op, 2, D, rcq, (rbc,), free=f0)
        run(ad)
        tf = [[], []]
        for k in range(KD):
            a, st.n_tok[k] = modulated(hT[:, k, :], rb[:, :], nhi[:, k, :], nlo[:, k, :], k, 0, tmp[:, k % 2], T,
                                       [st.h_tok[k], r_x, f0], tf[k % 2], st.n_free)
            st.h_read[k] = st.h_read[k] + [a]
            tf[k % 2] = st.n_tok[k]
        c_tok, tf2 = [None] * KD, [[], []]

        def ctx_operand():
            for k in range(KD):
                a, c_tok[k] = modulated(ctx_t[:, k, :], rbc[:, :], chi[:, k, :], clo[:, k, :], k, 1,
                                        tmc[:, k % 2], TC, [r_c, cl, f0], tf2[k % 2], f0)
                tf2[k % 2] = c_tok[k]
                yield

        def both(bx, bc, name, m):
            for k in range(KD):
                w = W.tile(name, k, m)
                op = mm_w(bx.ap, w, nhi[:, k, :], nlo[:, k, :], k == 0, k == KD - 1, st.n_tok[k],
                          bx.free if k == 0 else None)
                bx.op = op
                bc.op = mm_w(bc.ap[:, 0:TC], w, chi[:, k, :], clo[:, k, :], k == 0, k == KD - 1, c_tok[k],
                             bc.free if k == 0 else None)

        def cq():
            for j in range(3):
                b = bank[1 + j]
                yield from project(b, "mla_in", j)
                q, op = square_in(j, b.ap, b.op, j == 0, j == 2)
                b.free = [q] + split_scaled(b.ap, pc("q_norm", j), cqh[:, j, :], cql[:, j, :], b.op, f0)
                cq_tok.append(b.free[1:])
            st.cq_stat = op

        cq_tok, ck_tok = [], []
        weave(cq(), ctx_operand(), 1)
        r_q = root(st.cq_stat, 4, 384, rcq, (rbk, rbq), scale2=192 ** -0.5, free=r_c)
        for j in range(2):
            bx, bc = bank[1 + 2 * j], bank[2 + 2 * j]
            both(bx, bc, "mla_in", 3 + j)
            q, op = square_in(0, bx.ap, bx.op, j == 0, j == 1)
            q2, op = square_in(1, bc.ap[:, 0:TC], bc.op, False, j == 1, nt=2, width=TC, col=4)
            bx.free = [q] + split_scaled(bx.ap, pc("kvl_norm", j), ckh[:, j, 0:T], ckl[:, j, 0:T], bx.op, f0)
            bc.free = [q2] + split_scaled(bc.ap[:, 0:TC], pc("kvl_norm", j), ckh[:, j, T:], ckl[:, j, T:], bc.op, f0)
            ck_tok.append(bx.free[1:] + bc.free[1:])
        kv_stat = op
        bx, bc = bank[5], bank[6]
        both(bx, bc, "mla_in", 5)
        r_k = root(kv_stat, 6, 256, rck, (rbk,), free=r_q)
        t1 = V(lambda e: e.tensor_tensor(krt[:, 0, :], bx.ap[0:64, :], cs[0:64, 0, :], MUL), bx.op, rl, f0)
        t2 = V(lambda e: e.tensor_tensor(krt[:, 1, :], bx.ap[64:128, :], cs[64:128, 1, :], MUL), bx.op, rl, f0)
        bx.free = [t2]
        kr = []
        for e_ in range(2):
            ps = slice(64 * e_, 64 * e_ + 64)
            kr.append(V(lambda e, ps=ps, e_=e_: e.tensor_tensor(krz[ps, e_, 0:T], krt[:, 0, :], krt[:, 1, :], ADD),
                        t1, t2, z))
            kr.append(AC(lambda e, ps=ps, e_=e_: e.activation(krz[ps, e_, T:], bc.ap[0:64, 0:TC], ACT.Copy),
                         bc.op, z))
        bc.free = [kr[3]]
        cso = [V(lambda e, j=j: e.tensor_tensor(cs[:, j, :], cs[:, j, :], rbq[:, :], MUL), r_q, rl, t1, t2)
               for j in range(2)]
        v_tok = []
        for g in range(2):
            for k in range(2):
                w = W.tiles([("ukv", k, 8 + 4 * g + j) for j in range(4)])
                for t in range(6):
                    c = slice(128 * t, 128 * t + 128)
                    bank[t].op = mm_x(bank[t].ap, w, ckh[:, k, c], ckl[:, k, c], k == 0, k == 1, ck_tok[k],
                                      bank[t].free if k == 0 else None)
            for t in range(6):
                a = AC(lambda e, t=t, g=g: e.activation(v[:, t, 512 * g:512 * g + 512], bank[t].ap, ACT.Copy,
                                                        scale=rck[:, t:t + 1]), bank[t].op, r_k, f0)
                bank[t].free = [a]
                v_tok.append(a)
        f1 = fence()
        ph2.close()
        qn = p("qn", [128, 2, T])
        kn = p("kn", [128, 2, T + TC])
        qr = p("qr", [128, 2, T])
        tr = sqb
        s = p("s", [128, 2, T + TC])
        pt = p("pt", [128, 2, T + TC])
        sg = p("sg", [128, 2, T])
        ov = p("o", [128, KD - 1, T])
        o = [ov[:, j, :] for j in range(KD - 1)] + [qn[:, 0, :]]
        sm = p("sm", [128, 4, 4])
        fr = {"qn": [f1, f1], "kn": [f1, f1], "qr": [f1, f1], "tr": [f1, st.sq_free], "s": [f1, f1], "pt": [f1, f1],
              "sg": [f1, f1], "sm": [f1, f1]}
        tk = {}
        rk = [r_q, r_k]

        def proj(h):
            z = h % 2
            y = h // 2 % 2
            b = bank[7]
            if z == 0:
                for j in range(2):
                    yield from project(b, "uq", 8 + 2 * (h // 2) + j, ks=3, hi=cqh, lo=cql, tok=cq_tok)
                    a = V(lambda e, j=j: e.tensor_tensor(tr[:, j, :], b.ap, cs[:, j, :], MUL), b.op, cso, fr["tr"])
                    b.free = [a]
                a = V(lambda e: e.tensor_tensor(qr[:, y, :], tr[:, 0, :], tr[:, 1, :], ADD), a, fr["qr"][y])
                fr["tr"] = [a]
                tk["qr", y] = a
            yield from project(b, "uq", h, ks=3, hi=cqh, lo=cql, tok=cq_tok)
            a = V(lambda e: e.tensor_tensor(qn[:, z, :], b.ap, rbq[:, :], MUL), b.op, rk, fr["qn"][z])
            b.free = [a]
            tk["qn", z] = a
            b5 = bank[5]
            for k in range(2):
                w = W.tile("ukv", k, h)
                b.op = mm_w(b.ap, w, ckh[:, k, 0:T], ckl[:, k, 0:T], k == 0, k == 1, ck_tok[k], b.free)
                b5.op = mm_w(b5.ap[:, 256:512], w, ckh[:, k, T:], ckl[:, k, T:], k == 0, k == 1, ck_tok[k], b5.free)
            a = V(lambda e: e.tensor_tensor(kn[:, z, 0:T], b.ap, rbk[:, 0:T], MUL), b.op, rk, fr["kn"][z])
            a2 = V(lambda e: e.tensor_tensor(kn[:, z, T:], b5.ap[:, 256:512], rbk[:, T:], MUL), b5.op, rk,
                   fr["kn"][z])
            b.free = [a]
            b5.free = b5.free + [a2]
            tk["kn", z] = [a, a2]
            yield
            yield from project(b, "mla_in", 6 + h)
            a = AC(lambda e: e.activation(sg[:, z, :], b.ap, ACT.Tanh, scale=0.5), b.op, fr["sg"][z])
            a = V(lambda e: e.scalar_tensor_tensor(sg[:, z, :], sg[:, z, :], 1.0, b.ap, ADD, MUL), a)
            b.free = [a]
            tk["sg", z] = a

        def attend(h):
            z, y, e_ = h % 2, h // 2 % 2, h % 2
            exps = {}

            def scores(blk):
                i = blk % 2
                ba, bb = bank[2 * i], bank[2 * i + 1]
                c = slice(128 * blk, 128 * blk + 128)
                for b, ks, n in ((ba, slice(0, T), T), (bb, slice(T, T + TC), TC)):
                    PE(lambda e, b=b, ks=ks, n=n: e.matmul(b.ap[:, 0:n], qn[:, z, c], kn[:, z, ks], start=True,
                                                           stop=False), tk["qn", z], tk["kn", z], b.free)
                    op = PE(lambda e, b=b, ks=ks, n=n: e.matmul(b.ap[:, 0:n], qr[:, y, c], krz[:, e_, ks],
                                                                start=False, stop=True), tk["qr", y], kr)
                sv = PS[:, 1024 * i:1024 * i + T + TC]
                mx = V(lambda e: e.tensor_reduce(sm[:, i, 0:1], sv, AX_X, ALU.max), op, fr["sm"][i])
                nm = V(lambda e: e.tensor_scalar(sm[:, i, 1:2], sm[:, i, 0:1], -1.0, None, MUL), mx, fr["sm"][i])
                ex = AC(lambda e: e.activation(s[:, i, :], sv, ACT.Exp, bias=sm[:, i, 1:2], accum_out=sm[:, i, 2:3]),
                        nm, fr["s"][i], fr["sm"][i])
                ba.free = bb.free = [ex, mx]
                rd = V(lambda e: e.reciprocal(sm[:, i, 3:4], sm[:, i, 2:3]), ex)
                exps[blk] = V(lambda e: e.tensor_scalar(s[:, i, :], s[:, i, :], sm[:, i, 3:4], None, MUL), rd)
                fr["sm"][i] = [exps[blk], ex]
                return op

            op = scores(0)
            b4, b5, b6 = bank[4], bank[5], bank[6]
            for blk in range(4):
                i = blk % 2
                yield
                if blk < 3:
                    op = scores(blk + 1)
                    if blk == 2:
                        fr["qn"][z] = fr["kn"][z] = [op]
                        if e_:
                            fr["qr"][y] = [op]
                yield
                for t in range(6):
                    tr_ = PE(lambda e, t=t, i=i: e.transpose(PS[:, 2048 + 128 * t:2176 + 128 * t],
                                                             s[:, i, 128 * t:128 * t + 128], ident[:, :]),
                             exps[blk], b4.free, b5.free)
                fr["s"][i] = [tr_]
                cp = AC(lambda e, i=i: e.activation(pt[:, i, :], PS[:, 2048:2048 + T + TC], ACT.Copy), tr_,
                        fr["pt"][i])
                b4.free = b5.free = [cp]
                yield
                for t in range(6):
                    op2 = PE(lambda e, t=t, i=i, blk=blk: e.matmul(
                        b6.ap[:, 128 * blk:128 * blk + 128], v[:, t, 128 * h:128 * h + 128],
                        pt[:, i, 128 * t:128 * t + 128], start=t == 0, stop=t == 5), cp, v_tok,
                        b6.free if blk == 0 else None)
                fr["pt"][i] = [op2]
                yield
            m = V(lambda e: e.scalar_tensor_tensor(o[h], b6.ap, 0.5, sg[:, z, :], MUL, MUL), op2, tk["sg", z],
                  f1, fr["qn"][0] if h == KD - 1 else None)
            b6.free = [m]
            fr["sg"][z] = [m]
            o_op.append(m)

        o_op, o_tok = [], []
        run(proj(0))
        for h in range(KD):
            if h == KD - 1:
                st.n_free = [Q.q["pe"][-1]]
                o_tok = [split(o[j], nhi[:, j, :], nlo[:, j, :], o_op[j], st.n_free) for j in range(KD - 1)]
            weave(attend(h), proj(h + 1) if h + 1 < KD else None, 2)
        o_tok.append(split(o[7], nhi[:, 7, :], nlo[:, 7, :], o_op[7], st.n_free))
        for m in range(KD):
            b = bank[m % 4]
            run(project(b, "mla_out", m, tok=o_tok, hi=nhi, lo=nlo))
            residual(m, b, ada[:, 16 + m, 0:1])
            op = go(m)
        st.ada_read = [Q.q["dve"][-1]]
        st.n_free = [Q.q["pe"][-1]]
        ph.close()
        return op

    def hyena(stat_op):
        ph = ExitStack()
        f0 = fence()
        p = lambda name, shape, dt=F: sbt(ph, name + "_h", shape, dt)
        zh, zl = p("zh", [128, 4, 512], FR), p("zl", [128, 4, 512], FR)
        hh, hl = p("hh", [128, 2, 4, 512], FR), p("hl", [128, 2, 4, 512], FR)
        z = p("z", [128, 4, T])
        g = p("g", [128, 4, T])
        o = p("o", [128, 4, T])
        tmp = p("tmp", [128, 5, T])
        up = p("up", [128, 2, T + 2])
        hdn = rb2
        zu = V(lambda e: e.memset(up[:, :, 0:1], 0.0), f0)
        zu = V(lambda e: e.memset(up[:, :, T + 1:T + 2], 0.0), zu)

        ad = adapt(1, bank[0], 1)
        for _ in range(8):
            next(ad)
        r = root(stat_op, 4, D, rc, (rb,), free=f0)
        run(ad)

        fs = ExitStack()
        pos = sbt(fs, "pos", [64, T])
        fw = sbt(fs, "fw", [64, 3, 64])
        fa = sbt(fs, "fa", [64, 4, T])
        pl = Q.dma("sp", lambda e: e.dma_start(pos[:, :], A["pos"]), "pos", f0)
        fl = Q.dma("sp", lambda e: e.dma_start(fw[:, :, :], A["filt"]), "filt", f0)

        def hidden():
            src, tok = pos, [pl, fl]
            for l in range(3):
                b = bank[1]
                op = PE(lambda e, src=src, l=l: e.matmul(b.ap[0:64, :], fw[:, l, :], src[0:64, :], start=True,
                                                         stop=True), tok, fl, b.free)
                a = V(lambda e, l=l: e.tensor_scalar(fa[:, 0, :], b.ap[0:64, :], par[0:64, PC["fb"] + l:PC["fb"] + l + 1],
                                                     par[0:64, PC["ff"] + l:PC["ff"] + l + 1], ADD, MUL), op, par_l, f0)
                b.free = [a]
                n = V(lambda e: e.tensor_scalar(fa[:, 1, :], fa[:, 0, :], float(np.float32(1 / (2 * np.pi))), None, MUL),
                      a)
                n = V(lambda e: e.tensor_scalar(fa[:, 2, :], fa[:, 1, :], 12582912.0, None, ADD), n)
                n = V(lambda e: e.tensor_scalar(fa[:, 1, :], fa[:, 2, :], -12582912.0, None, ADD), n)
                n = V(lambda e: e.scalar_tensor_tensor(fa[:, 2, :], fa[:, 1, :], -6.28125, fa[:, 0, :], MUL, ADD), n)
                n = V(lambda e: e.scalar_tensor_tensor(fa[:, 3, :], fa[:, 1, :], -(2 * np.pi - 6.28125), fa[:, 2, :],
                                                       MUL, ADD), n)
                n = V(lambda e: e.tensor_scalar(fa[:, 0, :], fa[:, 3, :], 3.1415925, -3.1415925, ALU.min, ALU.max), n)
                a = AC(lambda e: e.activation(hdn[0:64, :], fa[:, 0, :], ACT.Sin), n, f0, op)
                src, tok = hdn, [a]
                yield
            st.hd_tok = tok

        def operands():
            for k in range(KD):
                a, st.n_tok[k] = modulated(hT[:, k, :], rb[:, :], nhi[:, k, :], nlo[:, k, :], k, 0,
                                           tmp[:, 2 * (k % 2):2 * (k % 2) + 2], T, [st.h_tok[k], r, f0], tf[k % 2],
                                           st.n_free)
                st.h_read[k] = st.h_read[k] + [a]
                tf[k % 2] = st.n_tok[k]
                yield

        tf = [[], []]
        weave(operands(), hidden(), 1)
        tmp_free, up_free = [tf, zu], [[zu], [zu]]
        st.f_h = fence()
        fs.close()
        z_tok, g_tok, zt_tok = [None] * 4, [None] * 4, [None] * 4
        fr = {"z": [f0] * 4, "g": [f0] * 4, "zt": f0, "h": f0, "tmp": tmp_free, "up": up_free, "y": [[], []]}

        def conv(m, b, dst, *waits):
            i = m % 2
            a = AC(lambda e: e.activation(up[:, i, 1:T + 1], b.ap, ACT.Copy), b.op, fr["up"][i])
            c0 = AC(lambda e: e.activation(tmp[:, 2 * i, :], b.ap, ACT.Identity, bias=pc("hb", m), scale=pc("hw", 24 + m)),
                    b.op, fr["tmp"])
            b.free = [a, c0]
            c1 = V(lambda e: e.scalar_tensor_tensor(tmp[:, 2 * i + 1, :], up[:, i, 0:T], pc("hw", m), tmp[:, 2 * i, :],
                                                    MUL, ADD), a, c0, fr["tmp"])
            c2 = V(lambda e: e.scalar_tensor_tensor(dst, up[:, i, 2:T + 2], pc("hw", 48 + m), tmp[:, 2 * i + 1, :],
                                                    MUL, ADD), c1, waits)
            fr["up"][i] = [c1, c2]
            fr["tmp"] = [fr["tmp"], c1, c2][-3:]
            return c2

        def filters(od, c):
            hs = ExitStack()
            f = fence()
            n_ = f"_{od}{c}"
            wl = sbt(hs, "wl" + n_, [64, 2, 512])
            ws = sbt(hs, "ws" + n_, [64, 2, 512])
            dc = sbt(hs, "dc" + n_, [128, 2, 512])
            ht = sbt(hs, "ht" + n_, [128, 2, 512])
            hs.close()
            base = od * 2048 + 512 * c
            l0_ = Q.dma("sp", lambda e: e.dma_start(wl[:, 0, :], A["filt_out"][:, base:base + 512]), "fo0", f, st.f_h)
            l1_ = Q.dma("sp", lambda e: e.dma_start(wl[:, 1, :], A["filt_out"][:, base + 1024:base + 1536]), "fo1", f,
                        st.f_h)
            w = [V(lambda e, j=j: e.tensor_tensor(ws[:, j, :], wl[:, 0, :], wl[:, 1, :], (ADD, SUB)[j]), l0_, l1_, f)
                 for j in range(2)]
            dfree, hfree, tok = [f, f], [f, f], []
            yield
            for t in range(4):
                i = t % 2
                dl = Q.dma("sp", lambda e, t=t, i=i: e.dma_start(dc[:, i, :], A["decay"][t, :, 512 * c:512 * c + 512]),
                           f"dc{i}", dfree[i], st.f_h)
                for j in range(2):
                    b = bank[4 + j]
                    op = PE(lambda e, b=b, t=t, j=j: e.matmul(b.ap, hdn[0:64, 128 * t:128 * t + 128], ws[:, j, :],
                                                              start=True, stop=True), w, st.hd_tok, b.free)
                    a = V(lambda e, b=b, i=i, j=j: e.tensor_tensor(ht[:, j, :], b.ap, dc[:, i, :], MUL), op, dl,
                          hfree[j])
                    b.free = [a]
                    sp = split(ht[:, j, :], hh[:, j, t, :], hl[:, j, t, :], a, fr["h"])
                    hfree[j] = sp
                    tok.append(sp)
                    dfree[i] = [a]
                    yield
            st.hf_tok = tok

        def turn():
            for t in range(4):
                b = bank[6 + t % 2]
                for ct in range(4):
                    op = PE(lambda e, b=b, t=t, ct=ct: e.transpose(b.ap[:, 128 * ct:128 * ct + 128],
                                                                   z[:, ct, 128 * t:128 * t + 128], ident[:, :]),
                            z_tok[ct], b.free, id_l)
                zt_tok[t] = split(b.ap, zh[:, t, :], zl[:, t, :], op, fr["zt"])
                b.free = zt_tok[t]
                yield
            st.turned = [op]

        def convolve(od, c, last):
            ys = ExitStack()
            f = fence()
            yh = sbt(ys, f"yh_{od}{c}", [128, 2, 2, 512], FR)
            yl = sbt(ys, f"yl_{od}{c}", [128, 2, 2, 512], FR)
            ys.close()
            bu, bk, bi, bj = bank[4:8]
            ks = sqb
            tf_ = [fr["tmp"], f]
            ktf = [st.sq_free, f]
            yfree = [f, f]
            y_tok = [None] * 4

            def forward(j):
                nonlocal tf_, ktf
                i = j % 2
                tok = [zt_tok, st.hf_tok]
                first = [True, False, False, False]
                for k in range(4):
                    w = W.tile("dft", k, j)
                    bu.op = mm_w(bu.ap, w, zh[:, k, :], zl[:, k, :], k == 0, k == 3, zt_tok[k], bu.free)
                    bk.op = mm_w(bk.ap, w, hh[:, 0, k, :], hl[:, 0, k, :], k == 0, k == 3, st.hf_tok, bk.free)
                kr = AC(lambda e: e.activation(ks[:, 0, :], bk.ap, ACT.Copy), bk.op, ktf)
                bk.free = [kr]
                if j == 0:
                    for k in range(4):
                        w = W.tile("alt", k, 0)
                        bk.op = mm_w(bk.ap, w, hh[:, 0, k, :], hl[:, 0, k, :], k == 0, k == 3, st.hf_tok, bk.free)
                    kp = AC(lambda e: e.activation(tmp[:, 4, :], bk.ap, ACT.Copy), bk.op, tf_)
                    bk.free = [kp]
                    kx = tmp[:, 4, :]
                else:
                    kp, kx = kr, ks[:, 0, :]
                for k in range(4):
                    w = W.tile("dft", k, 4 + j)
                    bi.op = mm_w(bi.ap, w, zh[:, k, :], zl[:, k, :], k == 0, k == 3, zt_tok[k], bi.free)
                    bj.op = mm_w(bj.ap, w, hh[:, 1, k, :], hl[:, 1, k, :], k == 0, k == 3, st.hf_tok, bj.free)
                ki = AC(lambda e: e.activation(ks[:, 1, :], bj.ap, ACT.Copy), bj.op, ktf)
                bj.free = [ki]
                if j == 0:
                    ki = V(lambda e: e.memset(ks[0:1, 1, :], 0.0), ki)
                a = V(lambda e: e.tensor_tensor(tmp[:, 0, :], bu.ap, ks[:, 0, :], MUL), bu.op, kr, tf_)
                b = V(lambda e: e.tensor_tensor(tmp[:, 1, :], bi.ap, ks[:, 1, :], MUL), bi.op, ki, tf_)
                c_ = V(lambda e: e.tensor_tensor(tmp[:, 2, :], bu.ap, ks[:, 1, :], MUL), ki, tf_)
                d = V(lambda e: e.tensor_tensor(tmp[:, 3, :], bi.ap, kx, MUL), kp, tf_)
                bu.free, bi.free = [c_], [d]
                ktf = [d]
                yr = V(lambda e: e.tensor_tensor(tmp[:, 0, :], tmp[:, 0, :], tmp[:, 1, :], SUB), a, b)
                yi = V(lambda e: e.tensor_tensor(tmp[:, 2, :], tmp[:, 2, :], tmp[:, 3, :], ADD), c_, d)
                s1 = split(tmp[:, 0, :], yh[:, i, 0, :], yl[:, i, 0, :], yr, yfree[i])
                s2 = split(tmp[:, 2, :], yh[:, i, 1, :], yl[:, i, 1, :], yi, yfree[i])
                y_tok[j] = [s1, s2]
                tf_ = [s1, s2]

            def inverse(j):
                i = j % 2
                for q in range(2):
                    w = W.tiles([("idft", 4 * q + j, m) for m in range(4)])
                    for ct in range(4):
                        cs = slice(128 * ct, 128 * ct + 128)
                        b = bank[ct]
                        b.op = mm_x(b.ap, w, yh[:, i, q, cs], yl[:, i, q, cs], j == 0 and q == 0, j == 3 and q == 1,
                                    y_tok[j][q], b.free)
                yfree[i] = [bank[3].op]

            forward(0)
            for j in range(1, 4):
                forward(j)
                inverse(j - 1)
            fr["h"] = fr["zt"] = [Q.q["pe"][-13]]
            inverse(3)
            fr["h"] = fr["zt"] = [Q.q["pe"][-1]]
            st.sq_free = [ktf, ktf]
            o_tok = []
            for ct in range(4):
                b = bank[ct]
                m = 4 * c + ct
                a = V(lambda e, b=b, ct=ct, m=m: e.scalar_tensor_tensor(tmp[:, ct, :], z[:, ct, :],
                                                                        pc("hbias", 8 * od + m), b.ap, MUL, ADD),
                      b.op, z_tok[ct], tf_)
                b.free = [a]
                dst = z[:, ct, :] if not last else o[:, ct, :]
                r_ = V(lambda e, ct=ct, dst=dst: e.tensor_tensor(dst, tmp[:, ct, :], g[:, ct, :], MUL), a, g_tok[ct],
                       st.turned, st.o_free)
                if not last:
                    z_tok[ct] = r_
                else:
                    o_tok.append(r_)
                fr["g"][ct] = [r_]
                fr["z"][ct] = [a, r_]
            fr["tmp"] = [Q.q["dve"][-1], f]
            return o_tok

        st.o_free = f0
        n_done = []
        fin = [None] * KD

        def channels(c, part):
            for ct in range(4):
                m = 8 * part + 4 * c + ct
                b = bank[ct % 2]
                yield from project(b, "hy_in", m)
                if part == 0:
                    z_tok[ct] = conv(m, b, z[:, ct, :], fr["z"][ct], st.turned)
                else:
                    g_tok[ct] = conv(m, b, g[:, ct, :], fr["g"][ct])
                if part == 2:
                    b = bank[2 + ct % 2]
                    yield from project(b, "hy_in", 24 + 4 * c + ct)
                    th = AC(lambda e, b=b: e.activation(tmp[:, 4, :], b.ap, ACT.Tanh, scale=0.5), b.op, fr["tmp"])
                    s2 = V(lambda e, b=b: e.scalar_tensor_tensor(tmp[:, 4, :], tmp[:, 4, :], 1.0, b.ap, ADD, MUL), th)
                    b.free = [s2]
                    x = V(lambda e, ct=ct: e.scalar_tensor_tensor(g[:, ct, :], g[:, ct, :], 0.5, tmp[:, 4, :],
                                                                  MUL, MUL), s2, g_tok[ct])
                    fr["tmp"] = [fr["tmp"], x]
                    g_tok[ct] = x

        def chain(*gens):
            for x in gens:
                yield from x

        st.turned = f0
        for c in range(2):
            weave(channels(c, 0), filters(0, c), 1)
            weave(channels(c, 1), turn(), 1)
            convolve(0, c, False)
            weave(channels(c, 2), chain(filters(1, c), turn()), 1)
            if c == 1:
                st.n_free = [Q.q["pe"][-1]]
                for ct in range(4):
                    fin[ct] = split(o[:, ct, :], nhi[:, ct, :], nlo[:, ct, :], o_tok[ct], st.n_free)
                st.o_free = [fin[0:4]]
            o_tok = convolve(1, c, True)
        for ct in range(4):
            fin[4 + ct] = split(o[:, ct, :], nhi[:, 4 + ct, :], nlo[:, 4 + ct, :], o_tok[ct], st.n_free)
        for m in range(KD):
            b = bank[m % 4]
            run(project(b, "hy_out", m, tok=fin, hi=nhi, lo=nlo))
            residual(m, b, ada[:, 16 + m, 0:1])
            op = only_squares(m)
        root(op, 4, D, rc, (rb,))
        for m in range(KD):
            h = hT[:, m, :]
            st.h_tok[m] = [V(lambda e, h=h, m=m: e.scalar_tensor_tensor(h, h, pc("final_g", m), rb[:, :], MUL, MUL),
                             st.h_tok[m], st.h_read[m], st.r_tok)]
        ph.close()

    hgrn()
    if stage >= 2:
        op = ffn(0, after("attn_norm"))
        root(op, 4, D, rc, (rb, rb2), scale2=0.125)
    if stage >= 3:
        op = swa(after("ffn_norm1"))
        root(op, 4, D, rc, (rb, rb2), scale2=0.5)
    if stage >= 4:
        op = ffn(1, after("final_norm"))
        root(op, 4, D, rc, (rb, rb2), scale2=0.5)
    if stage >= 6:
        op = mla(only_squares)
    if stage >= 7:
        hyena(op)

    outs = [Q.dma("sp", lambda e, m=m: e.dma_start(A["out"][m], hT[:, m, :]), "out", st.h_tok[m]) for m in range(KD)]
    W.align()
    Q.count()
    if chunks == 10 ** 6:
        ctx.close()
        return W.at // 8, W.spec, W.found
    with ctx:
        sems = {n: ctx.enter_context(nc.semaphore(f"s_{n}")) for n in ("pe", "act", "dve", "pool", *Q.dmas)}
        block = ctx.enter_context(nc.Block())

        @block.sync
        def _(eng):
            Q.emit("sp", eng, sems)
            eng.wait_ge(sems["out"], Q.dmas["out"])

        @block.scalar
        def _(eng):
            Q.emit("act", eng, sems)

        @block.vector
        def _(eng):
            Q.emit("dve", eng, sems)

        @block.gpsimd
        def _(eng):
            Q.emit("pool", eng, sems)

        @block.tensor
        def _(eng):
            Q.emit("pe", eng, sems)
    return W.at // 8, W.spec, W.found


def masks():
    s = np.arange(128)[:, None]
    t = np.arange(128)[None, :]
    out = [s == t]
    for lv in range(LV):
        b = 1 << lv
        out.append((s // (2 * b) == t // (2 * b)) & (s // b % 2 == 0) & (t // b % 2 == 1))
    return np.ascontiguousarray(np.stack(out, 1).astype(np.float32))


def distances():
    d = np.arange(128)[:, None] + 128 - np.arange(256)[None, :]
    ok = (d >= 0) & (d < 128)
    first = ok & (np.arange(256)[None, :] >= 128)
    return np.ascontiguousarray(np.stack([np.where(first, d, 1e30), np.where(ok, d, 1e30)], 1).astype(np.float32))


def rope():
    t = np.arange(T)
    inv = np.float32(10000.0) ** (-np.arange(16, dtype=np.float32) / np.float32(16))
    ang = np.concatenate([(t // 64).astype(np.float32)[:, None] * inv, (t % 64).astype(np.float32)[:, None] * inv], 1)
    c, s = np.cos(ang, dtype=np.float32).T, np.sin(ang, dtype=np.float32).T
    return np.ascontiguousarray(np.stack([np.concatenate([c, c, c, c]), np.concatenate([-s, s, -s, s])], 1))


def fourier():
    t = np.arange(T)
    w = 2 * np.pi * (np.outer(t, t) % 1024) / 1024
    c, s = np.cos(w), -np.sin(w)
    alt = np.where(t % 2, -1.0, 1.0)
    s[:, 0] = alt
    c2 = c[:, 0:128].copy()
    c2[:, 0] = alt
    ic, isn = 2 * np.cos(w) / 1024, -2 * np.sin(w) / 1024
    ic[0, :] = 1 / 1024
    isn[0, :] = alt / 1024
    f = np.float32
    return np.concatenate([c, s], 1).astype(f), c2.astype(f), np.concatenate([ic, isn], 0).astype(f)


def filter_tables():
    f = np.float32
    t = np.linspace(0.0, 1.0, T, dtype=f)[:, None]
    wpos = f(2.0 * np.pi / T) * np.arange(T, dtype=f)[:, None]
    bands = np.linspace(1e-4, 15, 16, dtype=f)[None, :]
    x = np.concatenate([t, np.cos(bands * wpos), -np.sin(bands * wpos)], 1).astype(f)
    pos = np.zeros((64, T), f)
    pos[0:33] = x.T
    deltas = np.abs(np.linspace(np.log(1e-2) / 0.3, np.log(1e-2) / 1.5, D, dtype=f))
    return pos, np.exp(-t * deltas).astype(f).reshape(4, 128, D)


def filter_weights(i):
    w = np.zeros((64, 3, 64), np.float32)
    w[0:33, 0] = i["hy_filt_w_in_2"][0]
    w[:, 1], w[:, 2] = i["hy_filt_w_hid_2"][0][0], i["hy_filt_w_hid_2"][0][1]
    return w


def cols(a):
    a = np.asarray(a).reshape(-1)
    return a.reshape(-1, 128).T


def params(i):
    p = {
        "hg_norm": cols(i["hg_norm"][0]), "lb0": cols(i["hg_lb_logits"][0]), "lb1": cols(i["hg_lb_logits"][1]),
        "out_norm": cols(i["hg_out_norm"][0]), "kv_norm": cols(i["kv_norm"]), "attn_norm": cols(i["attn_norm"][0]),
        "ffn_norm0": cols(i["ffn_norm"][0]), "ffn_norm1": cols(i["ffn_norm"][1]),
        "final_norm": cols(i["final_norm"]), "norm_g0": cols(i["norm_g_2"][0]), "norm_g1": cols(i["norm_g_2"][1]),
        "final_g": cols(i["final_g_2"]), "q_norm": cols(i["mla_q_norm_g_2"][0]),
        "kvl_norm": cols(i["mla_kv_norm_g_2"][0]),
        "sink": np.broadcast_to(np.asarray(i["attn_sinks"][0])[None, :], (128, 16)),
        "eps": np.full((128, 1), EPS, np.float32),
        "cw0": cols(i["ffn_conv_w"][0]), "cw1": cols(i["ffn_conv_w"][1]),
        "cb0": cols(i["ffn_conv_b"][0]), "cb1": cols(i["ffn_conv_b"][1]),
        "ada_b0": cols(i["ada_b_2"][0]), "ada_b1": cols(i["ada_b_2"][1]),
        "c": cols(i["c_2"][0]), "cc": cols(i["c_ctx_2"]),
        "hw": cols(i["hy_conv_w_2"][0]), "hb": cols(i["hy_conv_b_2"][0]), "hbias": cols(i["hy_bias_2"][0]),
        "fb": np.pad(np.asarray(i["hy_filt_b_2"][0]).T, ((0, 64), (0, 0))),
        "ff": np.pad(np.asarray(i["hy_filt_freq_2"][0]).T, ((0, 64), (0, 0))),
    }
    out = np.empty((128, NPAR), np.float32)
    for name, w in PAR:
        out[:, PC[name]:PC[name] + w] = p[name]
    return out


def matrices(i):
    kv = np.asarray(i["w_kv"])
    k0, k1, vv = kv[:, 0:64], kv[:, 64:128], kv[:, 128:256]
    mi = np.asarray(i["mla_w_in_2"][0])
    uq = np.asarray(i["mla_w_uq_2"][0]).reshape(384, 8, 192)
    ukv = np.asarray(i["mla_w_ukv_2"][0]).reshape(256, 8, 256)
    dft, alt, idft = fourier()
    return {
        "w_in": i["hg_w_in"][0], "w_out": i["hg_w_out"][0],
        "up0": i["ffn_w_up"][0], "up1": i["ffn_w_up"][1],
        "down0": i["ffn_w_down"][0], "down1": i["ffn_w_down"][1],
        "kv": np.concatenate([k0, k0, k1, k1, vv], 1),
        "mla_in": np.concatenate([mi[:, 0:704], mi[:, 672:704], mi[:, 640:672], mi[:, 704:]], 1),
        "uq": np.concatenate([uq[:, :, 0:128].reshape(384, 1024)] + [
            x for h in range(0, 8, 2) for x in (
                uq[:, h, 128:], uq[:, h + 1, 128:], uq[:, h, 160:], uq[:, h, 128:160], uq[:, h + 1, 160:],
                uq[:, h + 1, 128:160])], 1),
        "ukv": np.concatenate([ukv[:, :, 0:128].reshape(256, 1024), ukv[:, :, 128:].reshape(256, 1024)], 1),
        "mla_out": i["mla_w_out_2"][0], "ada0": i["ada_w_2"][0], "ada1": i["ada_w_2"][1],
        "hy_in": i["hy_w_in_2"][0], "hy_out": i["hy_w_out_2"][0], "dft": dft, "alt": alt, "idft": idft,
        "wq": i["attn_w_q"][0], "wo": i["attn_w_o"][0],
    }


def pack(spec, mats):
    out = np.zeros((len(spec) // 8, 128, 1024), np.float32)
    mats = {n: np.asarray(a) for n, a in mats.items()}
    for j, x in enumerate(spec):
        if x is not None:
            name, k, m = x
            out[j // 8, :, j % 8 * 128:j % 8 * 128 + 128] = mats[name][128 * k:128 * k + 128, 128 * m:128 * m + 128]
    return out


def feature_major(x):
    return np.ascontiguousarray(np.asarray(x).T.reshape(KD, 128, -1))


def prepare(inputs, fresh, stage=99):
    def declare(nc, shapes):
        return {n: nc.dram_tensor(f"in_{n}", s, F, kind="ExternalInput").ap()
                for n, s in shapes.items()}

    i = inputs
    pos, decay = filter_tables()
    arrays = {
        "par": params(i), "xT": feature_major(i["x"][0]), "ident": np.eye(128, dtype=np.float32), "masks": masks(),
        "pos": pos, "decay": decay, "filt": filter_weights(i), "filt_out": np.asarray(i["hy_filt_w_out_2"][0]),
        "dist": distances(), "rope": rope(),
        "ctx": np.ascontiguousarray(np.asarray(i["ctx_2"][0]).T.reshape(KD, 128, TC).transpose(1, 0, 2)),
    }
    res = (10 ** 6, None, set())
    for _ in range(2):
        nc = fresh()
        n = res[0]
        A = declare(nc, {**{k: a.shape for k, a in arrays.items()}, "stream": (n, 128, 1024)})
        A["out"] = nc.dram_tensor("out_0", (KD, 128, T), F, kind="ExternalOutput").ap()
        res = build(nc, A, n, res[2], stage)
    arrays["stream"] = pack(res[1], matrices(i))
    return nc, {f"in_{k}": a for k, a in arrays.items()}


def kernel(**inputs):
    import concourse.bacc as _bacc
    from concourse.bass_utils import run_bass_kernel_spmd as _run

    nc, arrays = prepare(inputs, lambda: _bacc.Bacc("TRN2", target_bir_lowering=False, num_devices=1))
    r = _run(nc, [arrays], core_ids=[0])
    out = r.results[0]["out_0"]
    return np.ascontiguousarray(out.reshape(D, T).T).reshape(1, T, D)
```

```python
from contextlib import ExitStack

import numpy as np

import concourse.bass as bass
from concourse import mybir

F = mybir.dt.float32
FR = mybir.dt.float32r
I32 = mybir.dt.int32
ALU = mybir.AluOpType
ACT = mybir.ActivationFunctionType
AX_X = mybir.AxisListType.X
MUL, ADD, SUB = ALU.mult, ALU.add, ALU.subtract

T = 512
D = 1024
KD = 8
FT = 22
HF = 11
TC = 256
RAW, HL = 4, 3
EPS = 1e-6
LV = 7


PAR = [("hg_norm", 8), ("lb0", 8), ("lb1", 8), ("out_norm", 1), ("kv_norm", 8), ("attn_norm", 8),
       ("ffn_norm0", 8), ("ffn_norm1", 8), ("final_norm", 8), ("norm_g0", 8), ("norm_g1", 8),
       ("final_g", 8), ("q_norm", 3), ("kvl_norm", 2), ("sink", 16), ("eps", 1),
       ("cw0", 66), ("cw1", 66), ("cb0", 22), ("cb1", 22), ("ada_b0", 24), ("ada_b1", 24),
       ("c", 8), ("cc", 8), ("hw", 72), ("hb", 24), ("hbias", 16), ("fb", 3), ("ff", 3)]
PC = {}
_n = 0
for _name, _w in PAR:
    PC[_name] = _n
    _n += _w
NPAR = _n


class Op:
    __slots__ = ("eng", "fn", "waits", "inc", "sem", "val")

    def __init__(self, eng, fn, waits, sem=None, val=0):
        self.eng, self.fn, self.waits, self.sem, self.val, self.inc = eng, fn, waits, sem, val, False


def flat(x, out):
    for y in x:
        if isinstance(y, Op):
            out.append(y)
        elif y:
            flat(y, out)
    return out


class Queues:

    def __init__(self):
        self.q = {e: [] for e in ("pe", "act", "dve", "pool", "sp")}
        self.dmas = {}

    def add(self, eng, fn, *waits):
        op = Op(eng, fn, flat(waits, []))
        self.q[eng].append(op)
        return op

    def dma(self, eng, fn, sem, *waits):
        self.dmas[sem] = self.dmas.get(sem, 0) + 16
        op = Op(eng, fn, flat(waits, []), sem, self.dmas[sem])
        self.q[eng].append(op)
        return op

    def count(self):
        for ops in self.q.values():
            for op in ops:
                for w in op.waits:
                    if w.sem is None:
                        w.inc = True
        for ops in self.q.values():
            n = 0
            for op in ops:
                if op.sem is None and op.inc:
                    n += 1
                    op.val = n

    def emit(self, name, eng, sems):
        seen = {}
        for op in self.q[name]:
            need = {}
            for w in op.waits:
                s = w.sem or w.eng
                need[s] = max(need.get(s, 0), w.val)
            for s, v in need.items():
                if seen.get(s, 0) < v:
                    eng.wait_ge(sems[s], v)
                    seen[s] = v
            ins = op.fn(eng)
            if op.sem is not None:
                ins.then_inc(sems[op.sem], 16)
            elif op.inc:
                ins.then_inc(sems[name], 1)


class Bank:

    def __init__(self, ap):
        self.ap, self.free = ap, []


class Tile:
    __slots__ = ("hi", "lo", "tok", "chunk")


class Weights:

    def __init__(self, Q, dram, raw, hi, lo, chunks, plain):
        self.Q, self.dram, self.raw, self.hi, self.lo, self.chunks = Q, dram, raw, hi, lo, chunks
        self.plain, self.found = plain, set()
        self.spec, self.split, self.last, self.load, self.done = [], {}, {}, {}, set()
        self.at = self.loaded = 0

    def fetch(self):
        while self.loaded < self.chunks:
            c, old = self.loaded, self.loaded - RAW
            if old >= 0 and old not in self.split and old not in self.done:
                return
            waits = [] if old < 0 else self.split.get(old) or self.last[old]
            dst, src = self.raw[:, c % RAW, :], self.dram[c]
            self.load[c] = self.Q.dma("sp", lambda e, dst=dst, src=src: e.dma_start(dst, src), f"w{c % RAW}", [waits])
            self.loaded += 1
            if old < 0 and self.loaded % RAW:
                return

    def prepare(self, c):
        if c >= self.chunks or c in self.split or c in self.plain or c in self.found:
            return
        old = next((self.last[p] for p in range(c - HL, -1, -HL) if p in self.split), None)
        r, hi, lo = self.raw[:, c % RAW, :], self.hi[:, c % HL, :], self.lo[:, c % HL, :]
        a = self.Q.add("act", lambda e: e.activation(hi, r, ACT.Copy), self.load[c], old)
        v = self.Q.add("dve", lambda e: e.tensor_tensor(lo, r, hi.bitcast(F), SUB), a, old)
        self.split[c] = [a, v]
        self.fetch()

    def tiles(self, names):
        n, at = len(names), self.at
        c = at // 8
        assert (at + n - 1) // 8 == c
        if at % 8 == 0:
            self.prepare(c)
            self.prepare(c + 1)
        self.spec += names
        self.at += n
        t = Tile()
        o = at % 8 * 128
        t.hi, t.lo = self.hi[:, c % HL, o:o + n * 128], self.lo[:, c % HL, o:o + n * 128]
        t.tok, t.chunk = self.split.get(c, []), c
        return t

    def tile(self, name, k, m):
        return self.tiles([(name, k, m)])

    def whole(self, names):
        assert self.at % 8 == 0 and len(names) == 8
        c = self.at // 8
        self.found.add(c)
        self.prepare(c + 1)
        self.spec += names
        self.at += 8
        t = Tile()
        t.hi, t.lo, t.tok, t.chunk = self.raw[:, c % RAW, :], None, [self.load[c]], c
        return t

    def used(self, t, op):
        self.last[t.chunk] = op

    def finished(self, t):
        self.done.add(t.chunk)
        self.fetch()

    def align(self):
        while self.at % 8:
            self.spec.append(None)
            self.at += 1


def weave(main, side, nm=1, ns=1):
    side = iter(side) if side is not None else iter(())
    done = 0
    for n, _ in enumerate(main):
        while done * nm < (n + 1) * ns:
            next(side, None)
            done += 1
    for _ in side:
        pass


def build(nc, A, chunks, plain, stage=99):
    Q = Queues()
    ctx = ExitStack()

    def sbt(stack, name, shape, dt=F):
        return stack.enter_context(nc.sbuf_tensor(name, shape, dt))

    def sb(name, shape, dt=F):
        return sbt(ctx, name, shape, dt)

    PE = lambda fn, *w: Q.add("pe", fn, *w)
    AC = lambda fn, *w: Q.add("act", fn, *w)
    V = lambda fn, *w: Q.add("dve", fn, *w)
    G = lambda fn, *w: Q.add("pool", fn, *w)

    def fence():
        return [Q.q[e][-1] for e in ("pe", "act", "dve", "pool") if Q.q[e]]

    hT = sb("hT", [128, KD, T])
    raw = sb("raw", [128, RAW, 1024])
    whi = sb("whi", [128, HL, 1024], FR)
    wlo = sb("wlo", [128, HL, 1024], FR)
    nhi = sb("nhi", [128, KD, T], FR)
    nlo = sb("nlo", [128, KD, T], FR)
    par = sb("par", [128, NPAR])
    ident = sb("ident", [128, 128])
    ones = sb("ones", [128, 128])
    rb = sb("rb", [128, T])
    rb2 = sb("rb2", [128, T])
    rc = sb("rc", [128, 8])
    sd = sb("sd", [128, 8])
    diag = sb("diag", [128, 4, 128])
    sqb = sb("sqb", [128, 2, T])
    lb = sb("lb", [128, 8, 8])
    PS = ctx.enter_context(nc.psum_tensor("PS", [128, 8 * 512], F))
    bank = [Bank(PS[:, 512 * i:512 * i + 512]) for i in range(8)]
    pc = lambda name, i=0: par[:, PC[name] + i:PC[name] + i + 1]

    W = Weights(Q, A["stream"], raw, whi, wlo, chunks, plain)

    par_l = Q.dma("sp", lambda e: e.dma_start(par[:, :], A["par"]), "par")
    x_l = []
    for m in range(KD):
        if m == 2:
            W.fetch()
        x_l.append(Q.dma("sp", lambda e, m=m: e.dma_start(hT[:, m, :], A["xT"][m]), f"x{m}"))
    id_l = Q.dma("sp", lambda e: e.dma_start(ident[:, :], A["ident"]), "id")
    for _ in range(RAW - 1):
        W.fetch()
    one_o = V(lambda e: e.memset(ones[:, :], 1.0))

    def mm_w(out, w, xh, xl, first, last, *waits):
        PE(lambda e: e.matmul(out, w.hi, xh, start=first, stop=False), w.tok, waits)
        PE(lambda e: e.matmul(out, w.hi, xl, start=False, stop=False))
        op = PE(lambda e: e.matmul(out, w.lo, xh, start=False, stop=last))
        W.used(w, op)
        return op

    def mm_x(out, w, xh, xl, first, last, *waits):
        PE(lambda e: e.matmul(out, xh, w.hi, start=first, stop=False), w.tok, waits)
        PE(lambda e: e.matmul(out, xh, w.lo, start=False, stop=False))
        op = PE(lambda e: e.matmul(out, xl, w.hi, start=False, stop=last))
        W.used(w, op)
        return op

    class State:
        pass

    st = State()
    st.n_tok = [[] for _ in range(KD)]
    st.n_free = []
    st.h_tok = [[x_l[m]] for m in range(KD)]
    st.h_read = [[] for _ in range(KD)]
    st.sq_free = [[], []]
    st.rb_free = []
    st.sc_free = []
    stat = bank[7]

    def project(b, name, m, ks=KD, k0=0, hi=None, lo=None, tok=None):
        hi, lo, tok = (nhi, nlo, st.n_tok) if hi is None else (hi, lo, tok)
        free = b.free
        for k in range(ks):
            w = W.tile(name, k0 + k, m)
            op = mm_w(b.ap, w, hi[:, k, :], lo[:, k, :], k == 0, k == ks - 1, tok[k], free if k == 0 else None)
            b.op = op
            if k in (3, 7) and later:
                later.pop(0)()
            yield

    def run(gen):
        for _ in gen:
            pass

    later = []

    def drain():
        while later:
            later.pop(0)()

    def square_in(m, src, waits, first, last, nt=4, width=T, col=0, gain=1.0, put_off=False):
        s = m % 2
        dst = sqb[:, s, 0:width]
        q = AC(lambda e: e.activation(dst, src, ACT.Square, scale=gain), waits, st.sq_free[s])

        def sums():
            for t in range(nt):
                op = PE(lambda e, t=t: e.matmul(stat.ap[:, col + t:col + t + 1], sqb[:, s, 128 * t:128 * t + 128],
                                                ones[:, 0:1], start=first and t == 0, stop=last,
                                                skip_group_check=True),
                        q if t == 0 else None, one_o, stat.free if first and t == 0 else None)
            st.sq_free[s] = [op]
            st.stat_op = op

        if put_off:
            later.append(sums)
        else:
            sums()
        return q

    def spread(r, nt, dst_c, dsts, free=()):
        out, prev = [], st.sc_free
        for g in range(0, nt, 4):
            n = min(4, nt - g)
            c = slice(128 * g, 128 * (g + n))
            d = V(lambda e, g=g, n=n: e.tensor_tensor(
                diag[:, 0:n, :], ident[:, :].unsqueeze(1).to_broadcast((128, n, 128)),
                dst_c[:, g:g + n].unsqueeze(2).to_broadcast((128, n, 128)), MUL), r, id_l, prev)

            def rest(d=d, n=n, c=c):
                nonlocal out
                p = PE(lambda e: e.matmul(stat.ap[:, 0:128 * n], ones[:, :],
                                          diag[:, 0:n, :].rearrange("p a b -> p (a b)"), start=True, stop=True),
                       d, r, out, stat.free)
                o = [AC(lambda e, t=t, f=f: e.activation(t[:, c], stat.ap[:, 0:128 * n], ACT.Copy, scale=f), p, free)
                     for t, f in dsts]
                out = out + o
                st.sc_free = [p]
                stat.free = out

            if g + 4 < nt:
                rest()
                prev = st.sc_free
            else:
                last = rest
        return last, lambda: out

    def root(nt, width, dst_c, dsts, free=(), put_off=False):
        def first():
            a = AC(lambda e: e.activation(sd[:, 0:nt], stat.ap[:, 0:nt], ACT.Sqrt, bias=pc("eps"),
                                          scale=1.0 / width), st.stat_op, par_l, st.sc_free)
            stat.free = [a]
            r = V(lambda e: e.reciprocal(dst_c[:, 0:nt], sd[:, 0:nt]), a, free)
            last, out = spread(r, nt, dst_c, dsts, free)

            def second():
                last()
                st.r_tok = out() + [r]

            if put_off:
                later.insert(0, second)
            else:
                second()

        if put_off:
            later.append(first)
        else:
            first()
            return st.r_tok

    def split_scaled(src, gain, dh, dl, *waits):
        a = AC(lambda e: e.activation(dh, src, ACT.Copy, scale=gain), waits)
        v = V(lambda e: e.scalar_tensor_tensor(dl, src, gain, dh.bitcast(F), MUL, SUB), a, waits)
        return [a, v]

    def split(src, dh, dl, *waits):
        a = AC(lambda e: e.activation(dh, src, ACT.Copy), waits)
        v = V(lambda e: e.tensor_tensor(dl, src, dh.bitcast(F), SUB), a, waits)
        return [a, v]

    def after(gain, put_off=True):
        def go(m):
            q = square_in(m, hT[:, m, :], st.h_tok[m], m == 0, m == KD - 1, put_off=put_off)
            st.n_tok[m] = split_scaled(hT[:, m, :], pc(gain, m), nhi[:, m, :], nlo[:, m, :], st.h_tok[m],
                                       par_l, st.n_free)
            st.h_read[m] = [q] + st.n_tok[m]
        return go

    def residual(m, b, scale=None):
        h = hT[:, m, :]
        if scale is None:
            v = V(lambda e: e.tensor_tensor(h, h, b.ap, ADD), b.op, st.h_tok[m], st.h_read[m])
        else:
            v = V(lambda e: e.scalar_tensor_tensor(h, b.ap, scale, h, MUL, ADD), b.op, st.h_tok[m], st.h_read[m],
                  st.ada_tok)
        b.free = [v]
        st.h_tok[m] = [v]

    def outputs(name, go, scale=None, bs=4, **kw):
        for m in range(KD):
            b = bank[m % bs]
            run(project(b, name, m, **kw))
            residual(m, b, scale and scale(m))
            if go:
                go(m)

    l0, l1 = par[:, PC["lb0"]:PC["lb0"] + 8], par[:, PC["lb1"]:PC["lb1"] + 8]
    go = after("hg_norm", False)
    for m in range(KD):
        go(m)
    root(4, D, rc, [(rb, 1.0), (rb2, 0.5 * 128 ** -0.5)], put_off=True)
    o = V(lambda e: e.tensor_tensor(lb[:, 0, :], l0, l1, ALU.max), par_l)
    o1 = V(lambda e: e.tensor_tensor(lb[:, 1, :], l0, lb[:, 0, :], SUB), o)
    o2 = V(lambda e: e.tensor_tensor(lb[:, 2, :], l1, lb[:, 0, :], SUB), o)
    o1 = AC(lambda e: e.activation(lb[:, 3, :], lb[:, 1, :], ACT.Exp), o1)
    o2 = AC(lambda e: e.activation(lb[:, 4, :], lb[:, 2, :], ACT.Exp), o2)
    o = V(lambda e: e.tensor_tensor(lb[:, 5, :], lb[:, 3, :], lb[:, 4, :], ADD), o1, o2)
    o = V(lambda e: e.reciprocal(lb[:, 6, :], lb[:, 5, :]), o)
    o = V(lambda e: e.tensor_tensor(lb[:, 7, :], lb[:, 3, :], lb[:, 6, :], MUL), o)
    o = V(lambda e: e.tensor_scalar(lb[:, 0, :], lb[:, 7, :], -0.5, 0.5, MUL, ADD), o)
    lb_o = V(lambda e: e.tensor_tensor(lb[:, 1, :], lb[:, 7, :], lb[:, 0, :], ADD), o)

    def hgrn():
        ph = ExitStack()
        p = lambda name, shape, dt=F: sbt(ph, name, shape, dt)
        v = p("v", [128, 4, D])
        ohi = p("ohi", [128, KD, T], FR)
        olo = p("olo", [128, KD, T], FR)
        tq = p("tq", [128, 2, T])
        th = p("th", [128, 2, T])
        q = p("q", [128, 2, T])
        ff = p("ff", [128, 2, T])
        kk = p("kk", [128, 2, T])
        sg = p("sg", [128, 2, T])
        qa = p("qa", [128, T])
        fb = p("fb", [128, T])
        sc = p("sc", [128, 4, 128])
        kt = p("kt", [128, 3, 128])
        S = p("S", [128, 3, 128])
        og = p("og", [128, 2, T])
        mask = p("mask", [128, LV + 1, 128])
        mk = Q.dma("sp", lambda e: e.dma_start(mask[:, :, :], A["masks"]), "mask")
        z = V(lambda e: e.memset(sc[:, :, :], 0.0))

        v_tok = []
        for g in range(2):
            bs = bank[0:4] if g == 0 else bank[3:7]
            bs = [bank[4 * g + t] if 4 * g + t < 7 else bank[0] for t in range(4)]
            for k in range(KD):
                w = W.tiles([("w_in", k, 16 + 4 * g + j) for j in range(4)])
                for t in range(4):
                    s = slice(128 * t, 128 * t + 128)
                    op = mm_x(bs[t].ap, w, nhi[:, k, s], nlo[:, k, s], k == 0, k == KD - 1, st.n_tok[k],
                              bs[t].free if k == 0 else None)
                    bs[t].op = op
                if later:
                    later.pop(0)()
            drain()
            r = st.r_tok
            for t in range(4):
                b = bs[t]
                a = AC(lambda e, t=t, b=b, g=g: e.activation(v[:, t, 512 * g:512 * g + 512], b.ap, ACT.Copy,
                                                        scale=rc[:, t:t + 1]), b.op, r)
                b.free = [a]
                v_tok.append(a)

        st.q_free = [[], []]
        st.sg_free = [[], []]
        st.o_tok = [None] * KD

        def proj(h):
            s = h % 2
            bq, bf, bg = bank[0], bank[1], bank[2]
            old = st.q_free[s]
            yield from project(bq, "w_in", h)
            a = V(lambda e: e.tensor_tensor(tq[:, 0, :], bq.ap, rb2[:, :], MUL), bq.op, r, st.t_free)
            bq.free = [a]
            b = AC(lambda e: e.activation(th[:, 0, :], tq[:, 0, :], ACT.Tanh, scale=128 ** 0.5), a, st.t_free)
            qo = V(lambda e: e.scalar_tensor_tensor(q[:, s, :], th[:, 0, :], 1.0, tq[:, 0, :], ADD, MUL), b, old)
            yield from project(bf, "w_in", 8 + h)
            a = V(lambda e: e.tensor_tensor(tq[:, 1, :], bf.ap, rb[:, :], MUL), bf.op, st.t_free)
            bf.free = [a]
            b = AC(lambda e: e.activation(th[:, 1, :], tq[:, 1, :], ACT.Tanh, scale=0.5), a, st.t_free)
            f = V(lambda e: e.tensor_scalar(ff[:, s, :], th[:, 1, :], lb[:, 0, h:h + 1], lb[:, 1, h:h + 1], MUL, ADD),
                  b, lb_o, old)
            ko = V(lambda e: e.tensor_scalar(kk[:, s, :], ff[:, s, :], -1.0, 1.0, MUL, ADD), f)
            st.t_free = [qo]
            st.qkf = [qo, f, ko]
            yield from project(bg, "w_in", 24 + h)
            a = V(lambda e: e.tensor_tensor(tq[:, 0, :], bg.ap, rb[:, :], MUL), bg.op, qo)
            bg.free = [a]
            b = AC(lambda e: e.activation(th[:, 0, :], tq[:, 0, :], ACT.Tanh, scale=0.5), a, qo)
            g = V(lambda e: e.scalar_tensor_tensor(sg[:, s, :], th[:, 0, :], 1.0, tq[:, 0, :], ADD, MUL), b,
                  st.sg_free[s])
            st.t_free = [g, f]
            st.sg_tok = [g]

        st.t_free = []
        st.kt_free, st.S_free, st.og_free = [], [], []
        st.sc_tok = [z]

        def scan(h):
            s = h % 2
            qq, kx, fx = q[:, s, :], kk[:, s, :], ff[:, s, :]
            qo, fo, ko = st.qkf
            sgt = st.sg_tok
            hc = slice(128 * h, 128 * h + 128)

            def scores(level, b, qx, *waits):
                for c in range(4):
                    cs = slice(128 * c, 128 * c + 128)
                    op = PE(lambda e, cs=cs: e.matmul(b.ap[:, cs], kx[:, cs], qx[:, cs], start=True, stop=True),
                            waits if c == 0 else None, b.free if c == 0 else None)

                def pick():
                    cp = V(lambda e: e.copy_predicated(
                        sc[:, :, :], mask[:, level, :].bitcast(I32).unsqueeze(1).to_broadcast((128, 4, 128)),
                        b.ap.rearrange("p (c t) -> p c t", c=4)), op, mk, st.sc_tok)
                    st.sc_tok = [cp]
                    b.free = [cp]
                    cps.append(cp)

                cp_later.append(pick)
                return op

            a = V(lambda e: e.tensor_tensor(qa[:, :], qq, fx, MUL), qo, fo, st.qa_free)
            yield
            cps, cp_later = [], []
            op = scores(0, bank[3], qq, qo, ko)
            cp_later.pop()()
            yield
            qt, kt_, ft = [a], [ko], [fo]
            fsrc = fx
            for lv in range(LV):
                b = 1 << lv
                op = scores(lv + 1, bank[4 - lv % 2], qa, qt, kt_)
                n = T // (2 * b)
                fs = fsrc[:, 0:2 * n].rearrange("p (n a) -> p n a", a=2)
                qv = qa[:, :].rearrange("p (n a b) -> p n a b", a=2, b=b)
                kv = kx.rearrange("p (n a b) -> p n a b", a=2, b=b)
                sh = (128, n, b)
                qt = [V(lambda e, qv=qv, fs=fs, sh=sh: e.tensor_tensor(
                    qv[:, :, 1, :], qv[:, :, 1, :], fs[:, :, 0:1].to_broadcast(sh), MUL), op, qt, ft)]
                if cp_later:
                    cp_later.pop()()
                kt_ = [G(lambda e, kv=kv, fs=fs, sh=sh: e.tensor_tensor(
                    kv[:, :, 0, :], kv[:, :, 0, :], fs[:, :, 1:2].to_broadcast(sh), MUL), op, kt_, ft)]
                o0 = 0 if lv % 2 == 0 else 256
                fdst = fb[:, o0:o0 + n]
                ft = [G(lambda e, fs=fs, fdst=fdst, n=n: e.tensor_tensor(
                    fdst.unsqueeze(2), fs[:, :, 0:1], fs[:, :, 1:2], MUL), ft, st.fb_free, qt)]
                fsrc = fdst
                yield
            b3 = bank[3]
            for c in range(3):
                cs = slice(128 * c, 128 * c + 128)
                op = PE(lambda e, cs=cs: e.transpose(b3.ap[:, cs], kx[:, cs], ident[:, :]), kt_, b3.free, id_l)
            a = AC(lambda e: e.activation(kt[:, :, :].rearrange("p a b -> p (a b)"), b3.ap[:, 0:384], ACT.Copy),
                   op, st.kt_free)
            b3.free = [a]
            yield
            b4 = bank[4]
            for c in range(3):
                cs = slice(128 * c, 128 * c + 128)
                op = PE(lambda e, c=c, cs=cs: e.matmul(b4.ap[:, cs], kt[:, c, :], v[:, c, hc], start=True, stop=True),
                        a, b4.free, v_tok)
            st.kt_free = [op]
            so = [V(lambda e: e.tensor_copy(S[:, 0, :], b4.ap[:, 0:128]), op, st.S_free)]
            for c in (1, 2):
                so.append(V(lambda e, c=c: e.scalar_tensor_tensor(S[:, c, :], S[:, c - 1, :], fsrc[:, c:c + 1],
                                                                  b4.ap[:, 128 * c:128 * c + 128], MUL, ADD),
                            so[-1], ft, st.S_free))
            b4.free = [so[-1]]
            st.fb_free = [so[-1]]
            yield
            bo = bank[5 + h % 2]
            for c in range(4):
                cs = slice(128 * c, 128 * c + 128)
                op = PE(lambda e, c=c, cs=cs: e.matmul(bo.ap[:, cs], v[:, c, hc], sc[:, c, :], start=True,
                                                       stop=c == 0), bo.free, cps, v_tok)
                st.sc_tok = st.sc_tok + [op]
                if c:
                    op = PE(lambda e, c=c, cs=cs: e.matmul(bo.ap[:, cs], S[:, c - 1, :], qa[:, cs], start=False,
                                                           stop=True), so[c - 1], qt)
            st.S_free = st.qa_free = [op]
            st.q_free[s] = [op, kt_[0], ft[0], qt[0]]
            yield
            qs = square_in(h, bo.ap, op, True, True, put_off=True)
            yield
            drain()
            root(4, 128, rch, [(rbh, 1.0)], free=st.og_free, put_off=True)
            later.pop(0)()
            yield
            yield
            drain()
            rt = st.r_tok
            a = V(lambda e: e.scalar_tensor_tensor(og[:, 0, :], bo.ap, pc("out_norm"), rbh[:, :], MUL, MUL), rt, qs,
                  st.og_free)
            bo.free = [a]
            m = V(lambda e: e.scalar_tensor_tensor(og[:, 1, :], og[:, 0, :], 0.5, sg[:, s, :], MUL, MUL), a, sgt,
                  st.og_free)
            st.sg_free[s] = [m]
            st.o_tok[h] = split(og[:, 1, :], ohi[:, h, :], olo[:, h, :], m)
            st.og_free = [a] + st.o_tok[h]
            yield

        st.qa_free, st.fb_free = [], []
        rch = p("rch", [128, 4])
        rbh = p("rbh", [128, T])
        run(proj(0))
        for h in range(KD):
            nxt = proj(h + 1) if h + 1 < KD else None
            weave(scan(h), nxt, 16, 24)
        st.n_free = [Q.q["pe"][-1]]
        go = after("ffn_norm0")
        drain()
        outputs("w_out", after("ffn_norm0"), hi=ohi, lo=olo, tok=st.o_tok)
        root(4, D, rc, [(rb, 1.0), (rb2, 0.5)], put_off=True)
        ph.close()

    def ffn(layer, go):
        ph = ExitStack()
        f0 = fence()
        p = lambda name, shape, dt=F: sbt(ph, f"{name}_f{layer}", shape, dt)
        hh = p("hh", [128, HF, T], FR)
        hl = p("hl", [128, HF, T], FR)
        gp = p("gp", [128, 2, T + 2])
        t = p("t", [128, 6, 2, T])
        up, dn = f"up{layer}", f"down{layer}"
        z = V(lambda e: e.memset(gp[:, :, 0:2], 0.0), f0)
        ad = adapt(layer, bank[6], 2 - layer)
        cw, cb = f"cw{layer}", f"cb{layer}"
        gfree, tfree = [[z], [z]], [f0, f0]
        hid, hfree = [None] * HF, f0

        def tail(f, bg, bv):
            s, i = f % 2, f % HF
            g = V(lambda e: e.tensor_tensor(gp[:, s, 2:T + 2], bg.ap, rb[:, :], MUL), bg.op, st.r_tok, gfree[s])
            bg.free = [g]
            c0 = AC(lambda e: e.activation(t[:, 0, s, :], gp[:, s, 2:T + 2], ACT.Identity, bias=pc(cb, f),
                                           scale=pc(cw, 44 + f)), g, tfree[s])
            c1 = V(lambda e: e.scalar_tensor_tensor(t[:, 1, s, :], gp[:, s, 1:T + 1], pc(cw, 22 + f), t[:, 0, s, :],
                                                    MUL, ADD), c0, tfree[s])
            c2 = V(lambda e: e.scalar_tensor_tensor(t[:, 2, s, :], gp[:, s, 0:T], pc(cw, f), t[:, 1, s, :],
                                                    MUL, ADD), c1)
            gfree[s] = [c0, c2]
            vv = V(lambda e: e.tensor_tensor(t[:, 4, s, :], bv.ap, rb2[:, :], MUL), bv.op)
            bv.free = [vv]
            th = AC(lambda e: e.activation(t[:, 3, s, :], t[:, 2, s, :], ACT.Tanh, scale=0.5), c2)
            s2 = V(lambda e: e.scalar_tensor_tensor(t[:, 0, s, :], t[:, 3, s, :], 1.0, t[:, 2, s, :], ADD, MUL), th)
            mo = V(lambda e: e.tensor_tensor(t[:, 5, s, :], t[:, 0, s, :], t[:, 4, s, :], MUL), s2, vv)
            hid[i] = split(t[:, 5, s, :], hh[:, i, :], hl[:, i, :], mo, hfree)
            tfree[s] = hid[i]

        for half in range(2):
            for f in range(half * HF, half * HF + HF):
                bg, bv = bank[2 * f % 6], bank[(2 * f + 1) % 6]
                run(project(bg, up, f))
                next(ad, None)
                run(project(bv, up, FT + f))
                if f:
                    next(ad, None)
                drain()
                tail(f, bg, bv)
            if half:
                st.n_free = [Q.q["pe"][-1]]
            outputs(dn, go if half else None, bs=6, ks=HF, k0=half * HF, hi=hh, lo=hl, tok=hid)
            hfree = [Q.q["pe"][-1]]
        ph.close()

    def swa(go):
        ph = ExitStack()
        f0 = fence()
        p = lambda name, shape, dt=F: sbt(ph, name + "_s", shape, dt)
        khi = p("khi", [128, KD, T], FR)
        klo = p("klo", [128, KD, T], FR)
        kz = p("kz", [128, 2, 2, T + 128])
        vz = p("vz", [128, 4, 2, 2, 128])
        qb = p("qb", [128, 2, T])
        s = p("s", [128, 8, 256])
        pt = p("pt", [128, 4, 512])
        dist = p("dist", [128, 2, 256])
        sm = p("sm", [128, 8, 8])
        ds = Q.dma("sp", lambda e: e.dma_start(dist[:, :, :], A["dist"]), "dist", f0)
        zk = V(lambda e: e.memset(kz[:, :, :, :], 0.0), f0)
        zv = V(lambda e: e.memset(vz[:, :, :, :, :], 0.0), f0)
        sink = par[:, PC["sink"]:PC["sink"] + 16]

        ktok = [split_scaled(hT[:, k, :], pc("kv_norm", k), khi[:, k, :], klo[:, k, :], st.h_tok[k], f0)
                for k in range(KD)]
        for k in range(KD):
            st.h_read[k] = st.h_read[k] + ktok[k]
        q_tok, q_free = [None, None], [f0, f0]

        def proj(i):
            b = bank[7]
            yield from project(b, "wq", i)
            q_tok[i % 2] = V(lambda e: e.tensor_tensor(qb[:, i % 2, :], b.ap, rb2[:, :], MUL), b.op, st.r_tok,
                             q_free[i % 2])
            b.free = [q_tok[i % 2]]

        b0 = bank[6]
        run(project(b0, "wq", 0))
        kt = []
        for n in range(2):
            b = bank[n]
            run(project(b, "kv", n, hi=khi, lo=klo, tok=ktok))
            if n == 0:
                drain()
                q_tok[0] = V(lambda e: e.tensor_tensor(qb[:, 0, :], b0.ap, rb2[:, :], MUL), b0.op, st.r_tok, f0)
                b0.free = [q_tok[0]]
            for e_ in range(2):
                ps = slice(64 * e_, 64 * e_ + 64)
                o = V(lambda e, n=n, e_=e_, ps=ps, b=b: e.tensor_tensor(kz[ps, n, e_, 128:T + 128], b.ap[ps, :],
                                                                        rb[ps, :], MUL), b.op, st.r_tok, zk)
                kt.append(o)
            b.free = [o]
        bs = bank[2:6]
        for k in range(KD):
            w = W.tile("kv", k, 2)
            for t in range(4):
                c = slice(128 * t, 128 * t + 128)
                bs[t].op = mm_x(bs[t].ap[:, 0:128], w, khi[:, k, c], klo[:, k, c], k == 0, k == KD - 1, ktok[k],
                                bs[t].free if k == 0 else None)
        kv_read = [bs[3].op]
        vt = []
        for t in range(4):
            for e_ in range(2):
                o = AC(lambda e, t=t, e_=e_: e.activation(
                    vz[:, t, :, e_, 64 * e_:64 * e_ + 64], bs[t].ap[:, 0:128].rearrange("p (a d) -> p a d", a=2),
                    ACT.Copy, scale=rc[:, t:t + 1]), bs[t].op, st.r_tok, zv)
                vt.append(o)
            bs[t].free = [o]
        on_tok = [None] * KD
        fr = {"s": f0, "pt": [f0] * 4, "sm": f0}

        def attend(i):
            kv, z = i // 4, i % 2
            sc_o = []
            for blk in range(4):
                b = bank[blk]
                for e_ in range(2):
                    op = PE(lambda e, b=b, e_=e_, blk=blk: e.matmul(
                        b.ap[:, 256 * e_:256 * e_ + 256], qb[:, z, 128 * blk:128 * blk + 128],
                        kz[:, kv, e_, 128 * blk:128 * blk + 256], start=True, stop=True), q_tok[z], kt, b.free)
                for e_ in range(2):
                    slope = float(np.float32(2.0 ** (-8.0 * (2 * i + e_ + 1) / 16)))
                    o = V(lambda e, b=b, e_=e_, blk=blk, slope=slope: e.scalar_tensor_tensor(
                        s[:, 2 * blk + e_, :], dist[:, min(blk, 1), :], -slope, b.ap[:, 256 * e_:256 * e_ + 256],
                        MUL, ADD), op, ds, fr["s"])
                    sc_o.append(o)
                b.free = [o]
                yield
            q_free[z] = [op]
            mx = V(lambda e: e.tensor_reduce(sm[:, 0, :], s[:, :, :], AX_X, ALU.max), sc_o, fr["sm"])
            sk = sink[:, 2 * i:2 * i + 2].unsqueeze(1).to_broadcast((128, 4, 2))
            v4 = lambda j: sm[:, j, :].rearrange("p (b h) -> p b h", h=2)
            o = V(lambda e: e.tensor_tensor(v4(1), v4(0), sk, ALU.max), mx, fr["sm"])
            nm = V(lambda e: e.tensor_scalar(sm[:, 2, :], sm[:, 1, :], -1.0, None, MUL), o, fr["sm"])
            d = V(lambda e: e.tensor_tensor(v4(3), v4(2), sk, ADD), nm, fr["sm"])
            ex = []
            for j in range(8):
                ex.append(AC(lambda e, j=j: e.activation(s[:, j, :], s[:, j, :], ACT.Exp, bias=sm[:, 2, j:j + 1],
                                                         accum_out=sm[:, 4, j:j + 1]), nm, mx, fr["sm"]))
            es = AC(lambda e: e.activation(sm[:, 5, :], sm[:, 3, :], ACT.Exp), d, fr["sm"])
            yield
            o = V(lambda e: e.tensor_tensor(sm[:, 6, :], sm[:, 4, :], sm[:, 5, :], ADD), es, ex)
            rd = V(lambda e: e.reciprocal(sm[:, 7, :], sm[:, 6, :]), o)
            pn = [V(lambda e, j=j: e.tensor_scalar(s[:, j, :], s[:, j, :], sm[:, 7, j:j + 1], None, MUL), rd, ex[j])
                  for j in range(8)]
            fr["sm"] = [pn[-1], es]
            yield
            b6 = bank[6]
            for blk in range(4):
                b = bank[4 + blk % 2]
                for j in range(4):
                    op = PE(lambda e, b=b, j=j, blk=blk: e.transpose(
                        b.ap[:, 128 * j:128 * j + 128], s[:, 2 * blk + j // 2, 128 * (j % 2):128 * (j % 2) + 128],
                        ident[:, :]), pn[2 * blk + j // 2], b.free, id_l)
                fr["s"] = [op]
                c = AC(lambda e, b=b, blk=blk: e.activation(pt[:, blk, :], b.ap, ACT.Copy), op, fr["pt"][blk])
                b.free = [c]
                yield
                todo = [(e_, kb) for e_ in range(2) for kb in range(2) if blk or kb]
                for n, (e_, kb) in enumerate(todo):
                    op = PE(lambda e, n=n, e_=e_, kb=kb, blk=blk, last=len(todo) - 1: e.matmul(
                        b6.ap[:, 128 * blk:128 * blk + 128], vz[:, blk - 1 + kb, kv, e_, :],
                        pt[:, blk, 128 * (2 * e_ + kb):128 * (2 * e_ + kb) + 128], start=n == 0, stop=n == last),
                        c, vt, b6.free if blk == 0 else None)
                fr["pt"][blk] = [op]
            on_tok[i] = split(b6.ap, khi[:, i, :], klo[:, i, :], op, kv_read)
            b6.free = on_tok[i]
            yield

        for i in range(KD):
            weave(attend(i), proj(i + 1) if i + 1 < KD else None, 1)
        st.n_free = [Q.q["pe"][-1]]
        outputs("wo", go, hi=khi, lo=klo, tok=on_tok)
        ph.close()

    scv = sb("scv", [128, 3, KD, 2])
    adas = [sb(f"ada{j}", [128, 24, 2]) for j in range(2)]
    gss = [sb(f"gs{j}", [128, KD, 2]) for j in range(2)]
    cv = par[:, PC["c"]:PC["c"] + 16].rearrange("p (v k) -> p k v", v=2)
    a_ = AC(lambda e: e.activation(scv[:, 0], cv, ACT.Tanh, scale=0.5), par_l)
    a_ = V(lambda e: e.scalar_tensor_tensor(scv[:, 1], scv[:, 0], 1.0, cv, ADD, MUL), a_)
    sc_o = V(lambda e: e.tensor_scalar(scv[:, 2], scv[:, 1], 0.5, None, MUL), a_)
    st.ada_tok = []

    def adapt(layer, b, nv):
        ada, gs = adas[layer], gss[layer]
        for m in range(24):
            w = W.whole([(f"ada{layer}", k, m) for k in range(KD)])
            for k in range(KD):
                op = PE(lambda e, w=w, k=k, m=m: e.matmul(b.ap[:, 2 * m:2 * m + nv], w.hi[:, 128 * k:128 * k + 128],
                                                          scv[:, 2, k, 0:nv], start=k == 0, stop=k == KD - 1),
                        w.tok, sc_o, b.free)
            W.used(w, op)
            W.finished(w)
            yield
        bias = par[:, PC[f"ada_b{layer}"]:PC[f"ada_b{layer}"] + 24].unsqueeze(2).to_broadcast((128, 24, nv))
        o = V(lambda e: e.tensor_tensor(ada[:, :, 0:nv], b.ap[:, 0:48].rearrange("p (m v) -> p m v", v=2)[:, :, 0:nv],
                                        bias, ADD), op, par_l)
        b.free = [o]
        g = par[:, PC[f"norm_g{layer}"]:PC[f"norm_g{layer}"] + 8].unsqueeze(2).to_broadcast((128, KD, nv))
        o1 = V(lambda e: e.tensor_scalar(gs[:, :, 0:nv], ada[:, 8:16, 0:nv], 1.0, None, ADD), o)
        o2 = V(lambda e: e.tensor_tensor(gs[:, :, 0:nv], gs[:, :, 0:nv], g, MUL), o1)
        if layer == 0:
            fn = par[:, PC["final_norm"]:PC["final_norm"] + 8]
            o2 = V(lambda e: e.tensor_tensor(gs[:, :, 0], gs[:, :, 0], fn, MUL), o2)
        st.ada_tok = st.ada_tok + [o, o2]

    def modulated(layer, src, r, dh, dl, k, v, tmp, n, waits, tfree, dfree):
        a = V(lambda e: e.tensor_tensor(tmp[:, 0, 0:n], src, r, MUL), waits, tfree)
        u = V(lambda e: e.tensor_scalar(tmp[:, 1, 0:n], tmp[:, 0, 0:n], gss[layer][:, k, v:v + 1],
                                        adas[layer][:, k, v:v + 1],
                                        MUL, ADD), a, st.ada_tok, tfree)
        return a, split(tmp[:, 1, 0:n], dh, dl, u, dfree)

    def only_squares(m):
        q = square_in(m, hT[:, m, :], st.h_tok[m], m == 0, m == KD - 1, put_off=True)
        st.h_read[m] = [q]

    def squares_of_both(m):
        q = square_in(0, hT[:, m, :], st.h_tok[m], m == 0, m == KD - 1, put_off=True)
        q2 = square_in(1, hT[:, m, :], st.h_tok[m], False, m == KD - 1, col=4, gain=pc("final_norm", m),
                       put_off=True)
        st.h_read[m] = [q, q2]

    def mla(go):
        ph = ExitStack()
        f0 = fence()
        p = lambda name, shape, dt=F: sbt(ph, name + "_m", shape, dt)
        cqh, cql = p("cqh", [128, 3, T], FR), p("cql", [128, 3, T], FR)
        ckh, ckl = p("ckh", [128, 2, T + TC], FR), p("ckl", [128, 2, T + TC], FR)
        v = p("v", [128, 6, D])
        krz = p("krz", [128, 2, T + TC])
        cs = p("cs", [128, 2, T])
        rbq = rb2
        rbk = p("rbk", [128, T + TC])
        rcq, rck = p("rcq", [128, 4]), p("rck", [128, 6])
        ph2 = ExitStack()
        p2 = lambda name, shape, dt=F: sbt(ph2, name + "_m", shape, dt)
        ctx_t = p2("ctx", [128, KD, TC])
        chi, clo = p2("chi", [128, KD, TC], FR), p2("clo", [128, KD, TC], FR)
        tmp = p2("tmp", [128, 2, 2, T])
        tmc = p2("tmc", [128, 2, 2, TC])
        rbc = p2("rbc", [128, TC])
        krt = p2("krt", [64, 2, T])
        cl = Q.dma("sp", lambda e: e.dma_start(ctx_t[:, :, :], A["ctx"]), "ctx", f0)
        rl = Q.dma("sp", lambda e: e.dma_start(cs[:, :, :], A["rope"]), "rope", f0)
        z = V(lambda e: e.memset(krz[:, :, :], 0.0), f0)

        drain()
        a = AC(lambda e: e.activation(sd[:, 0:4], stat.ap[:, 0:4], ACT.Sqrt, bias=pc("eps"), scale=1.0 / D),
               st.stat_op, st.sc_free)
        r1 = V(lambda e: e.reciprocal(rc[:, 0:4], sd[:, 0:4]), a)
        a = V(lambda e: e.tensor_tensor(rc[:, 4:8], rc[:, 0:4], rc[:, 0:4], MUL), r1)
        a = V(lambda e: e.tensor_tensor(sd[:, 4:8], rc[:, 4:8], stat.ap[:, 4:8], MUL), a)
        stat.free = [a]
        a = AC(lambda e: e.activation(sd[:, 0:4], sd[:, 4:8], ACT.Sqrt, bias=pc("eps"), scale=1.0 / D), a)
        a = V(lambda e: e.reciprocal(rc[:, 4:8], sd[:, 0:4]), a)
        r2 = V(lambda e: e.tensor_tensor(rc[:, 4:8], rc[:, 4:8], rc[:, 0:4], MUL), a)
        last, out = spread(r2, 4, rc[:, 4:8], [(rb2, 1.0)])
        last()
        r_x = out()
        last, out = spread(r1, 4, rc[:, 0:4], [(rb, 1.0)])
        last()
        r_h = out()
        tf = [[], []]
        for k in range(KD):
            a, st.n_tok[k] = modulated(0, hT[:, k, :], rb2[:, :], nhi[:, k, :], nlo[:, k, :], k, 0, tmp[:, k % 2], T,
                                       [st.h_tok[k], r_x, f0], tf[k % 2], st.n_free)
            st.h_read[k] = st.h_read[k] + [a]
            tf[k % 2] = st.n_tok[k]
        for k in range(KD):
            square_in(k, ctx_t[:, k, :], [cl, f0], k == 0, k == KD - 1, nt=2, width=TC)
        r_c = root(2, D, rcq, [(rbc, 1.0)], free=f0)
        for m in range(KD):
            h = hT[:, m, :]
            o = V(lambda e, h=h, m=m: e.scalar_tensor_tensor(h, h, pc("final_norm", m), rb[:, :], MUL, MUL),
                  st.h_tok[m], st.h_read[m], r_h)
            st.h_tok[m] = [o]
        c_tok, tf2 = [None] * KD, [[], []]

        def ctx_operand():
            for k in range(KD):
                a, c_tok[k] = modulated(0, ctx_t[:, k, :], rbc[:, :], chi[:, k, :], clo[:, k, :], k, 1,
                                        tmc[:, k % 2], TC, [r_c, cl, f0], tf2[k % 2], f0)
                tf2[k % 2] = c_tok[k]
                yield

        def both(bx, bc, name, m):
            for k in range(KD):
                w = W.tile(name, k, m)
                op = mm_w(bx.ap, w, nhi[:, k, :], nlo[:, k, :], k == 0, k == KD - 1, st.n_tok[k],
                          bx.free if k == 0 else None)
                bx.op = op
                bc.op = mm_w(bc.ap[:, 0:TC], w, chi[:, k, :], clo[:, k, :], k == 0, k == KD - 1, c_tok[k],
                             bc.free if k == 0 else None)

        def cq():
            for j in range(3):
                b = bank[1 + j]
                yield from project(b, "mla_in", j)
                q = square_in(j, b.ap, b.op, j == 0, j == 2)
                b.free = [q] + split_scaled(b.ap, pc("q_norm", j), cqh[:, j, :], cql[:, j, :], b.op, f0)
                cq_tok.append(b.free[1:])

        cq_tok, ck_tok = [], []
        weave(cq(), ctx_operand(), 1)
        r_q = root(4, 384, rcq, [(rbq, 192 ** -0.5)], free=[r_c, [t[0] for t in st.n_tok]])
        for j in range(2):
            bx, bc = bank[1 + 2 * j], bank[2 + 2 * j]
            both(bx, bc, "mla_in", 3 + j)
            q = square_in(0, bx.ap, bx.op, j == 0, j == 1)
            q2 = square_in(1, bc.ap[:, 0:TC], bc.op, False, j == 1, nt=2, width=TC, col=4)
            bx.free = [q] + split_scaled(bx.ap, pc("kvl_norm", j), ckh[:, j, 0:T], ckl[:, j, 0:T], bx.op, f0)
            bc.free = [q2] + split_scaled(bc.ap[:, 0:TC], pc("kvl_norm", j), ckh[:, j, T:], ckl[:, j, T:], bc.op, f0)
            ck_tok.append(bx.free[1:] + bc.free[1:])
        bx, bc = bank[5], bank[6]
        both(bx, bc, "mla_in", 5)
        r_k = root(6, 256, rck, [(rbk, 1.0)], free=r_q)
        t1 = V(lambda e: e.tensor_tensor(krt[:, 0, :], bx.ap[0:64, :], cs[0:64, 0, :], MUL), bx.op, rl, f0)
        t2 = V(lambda e: e.tensor_tensor(krt[:, 1, :], bx.ap[64:128, :], cs[64:128, 1, :], MUL), bx.op, rl, f0)
        bx.free = [t2]
        kr = []
        for e_ in range(2):
            ps = slice(64 * e_, 64 * e_ + 64)
            kr.append(V(lambda e, ps=ps, e_=e_: e.tensor_tensor(krz[ps, e_, 0:T], krt[:, 0, :], krt[:, 1, :], ADD),
                        t1, t2, z))
            kr.append(AC(lambda e, ps=ps, e_=e_: e.activation(krz[ps, e_, T:], bc.ap[0:64, 0:TC], ACT.Copy),
                         bc.op, z))
        bc.free = [kr[3]]
        cso = [V(lambda e, j=j: e.tensor_tensor(cs[:, j, :], cs[:, j, :], rbq[:, :], MUL), r_q, rl, t1, t2)
               for j in range(2)]
        v_tok = []
        for g in range(2):
            for k in range(2):
                w = W.tiles([("ukv", k, 8 + 4 * g + j) for j in range(4)])
                for t in range(6):
                    c = slice(128 * t, 128 * t + 128)
                    bank[t].op = mm_x(bank[t].ap, w, ckh[:, k, c], ckl[:, k, c], k == 0, k == 1, ck_tok[k],
                                      bank[t].free if k == 0 else None)
            for t in range(6):
                a = AC(lambda e, t=t, g=g: e.activation(v[:, t, 512 * g:512 * g + 512], bank[t].ap, ACT.Copy,
                                                        scale=rck[:, t:t + 1]), bank[t].op, r_k, f0)
                bank[t].free = [a]
                v_tok.append(a)
        f1 = fence()
        ph2.close()
        qn = p("qn", [128, 2, T])
        kn = p("kn", [128, 2, T + TC])
        qr = p("qr", [128, 2, T])
        tr = sqb
        s = p("s", [128, 2, T + TC])
        pt = p("pt", [128, 2, T + TC])
        sg = p("sg", [128, 2, T])
        ov = p("o", [128, KD - 1, T])
        o = [ov[:, j, :] for j in range(KD - 1)] + [qn[:, 0, :]]
        sm = p("sm", [128, 4, 4])
        fr = {"qn": [f1, f1], "kn": [f1, f1], "qr": [f1, f1], "tr": [f1, st.sq_free], "s": [f1, f1], "pt": [f1, f1],
              "sg": [f1, f1], "sm": [f1, f1]}
        tk = {}
        rk = [r_q, r_k]

        def proj(h):
            z = h % 2
            y = h // 2 % 2
            b = bank[7]
            if z == 0:
                for j in range(2):
                    yield from project(b, "uq", 8 + 2 * (h // 2) + j, ks=3, hi=cqh, lo=cql, tok=cq_tok)
                    a = V(lambda e, j=j: e.tensor_tensor(tr[:, j, :], b.ap, cs[:, j, :], MUL), b.op, cso, fr["tr"])
                    b.free = [a]
                a = V(lambda e: e.tensor_tensor(qr[:, y, :], tr[:, 0, :], tr[:, 1, :], ADD), a, fr["qr"][y])
                fr["tr"] = [a]
                tk["qr", y] = a
            yield from project(b, "uq", h, ks=3, hi=cqh, lo=cql, tok=cq_tok)
            a = V(lambda e: e.tensor_tensor(qn[:, z, :], b.ap, rbq[:, :], MUL), b.op, rk, fr["qn"][z])
            b.free = [a]
            tk["qn", z] = a
            b5 = bank[5]
            for k in range(2):
                w = W.tile("ukv", k, h)
                b.op = mm_w(b.ap, w, ckh[:, k, 0:T], ckl[:, k, 0:T], k == 0, k == 1, ck_tok[k], b.free)
                b5.op = mm_w(b5.ap[:, 256:512], w, ckh[:, k, T:], ckl[:, k, T:], k == 0, k == 1, ck_tok[k], b5.free)
            a = V(lambda e: e.tensor_tensor(kn[:, z, 0:T], b.ap, rbk[:, 0:T], MUL), b.op, rk, fr["kn"][z])
            a2 = V(lambda e: e.tensor_tensor(kn[:, z, T:], b5.ap[:, 256:512], rbk[:, T:], MUL), b5.op, rk,
                   fr["kn"][z])
            b.free = [a]
            b5.free = b5.free + [a2]
            tk["kn", z] = [a, a2]
            yield
            yield from project(b, "mla_in", 6 + h)
            a = AC(lambda e: e.activation(sg[:, z, :], b.ap, ACT.Tanh, scale=0.5), b.op, fr["sg"][z])
            a = V(lambda e: e.scalar_tensor_tensor(sg[:, z, :], sg[:, z, :], 1.0, b.ap, ADD, MUL), a)
            b.free = [a]
            tk["sg", z] = a

        def attend(h):
            z, y, e_ = h % 2, h // 2 % 2, h % 2
            exps = {}

            def scores(blk):
                i = blk % 2
                ba, bb = bank[2 * i], bank[2 * i + 1]
                c = slice(128 * blk, 128 * blk + 128)
                for b, ks, n in ((ba, slice(0, T), T), (bb, slice(T, T + TC), TC)):
                    PE(lambda e, b=b, ks=ks, n=n: e.matmul(b.ap[:, 0:n], qn[:, z, c], kn[:, z, ks], start=True,
                                                           stop=False), tk["qn", z], tk["kn", z], b.free)
                    op = PE(lambda e, b=b, ks=ks, n=n: e.matmul(b.ap[:, 0:n], qr[:, y, c], krz[:, e_, ks],
                                                                start=False, stop=True), tk["qr", y], kr)
                sv = PS[:, 1024 * i:1024 * i + T + TC]
                mx = V(lambda e: e.tensor_reduce(sm[:, i, 0:1], sv, AX_X, ALU.max), op, fr["sm"][i])
                nm = V(lambda e: e.tensor_scalar(sm[:, i, 1:2], sm[:, i, 0:1], -1.0, None, MUL), mx, fr["sm"][i])
                ex = AC(lambda e: e.activation(s[:, i, :], sv, ACT.Exp, bias=sm[:, i, 1:2], accum_out=sm[:, i, 2:3]),
                        nm, fr["s"][i], fr["sm"][i])
                ba.free = bb.free = [ex, mx]
                rd = V(lambda e: e.reciprocal(sm[:, i, 3:4], sm[:, i, 2:3]), ex)
                exps[blk] = V(lambda e: e.tensor_scalar(s[:, i, :], s[:, i, :], sm[:, i, 3:4], None, MUL), rd)
                fr["sm"][i] = [exps[blk], ex]
                return op

            op = scores(0)
            b4, b5, b6 = bank[4], bank[5], bank[6]
            for blk in range(4):
                i = blk % 2
                yield
                if blk < 3:
                    op = scores(blk + 1)
                    if blk == 2:
                        fr["qn"][z] = fr["kn"][z] = [op]
                        if e_:
                            fr["qr"][y] = [op]
                yield
                for t in range(6):
                    tr_ = PE(lambda e, t=t, i=i: e.transpose(PS[:, 2048 + 128 * t:2176 + 128 * t],
                                                             s[:, i, 128 * t:128 * t + 128], ident[:, :]),
                             exps[blk], b4.free, b5.free)
                fr["s"][i] = [tr_]
                cp = AC(lambda e, i=i: e.activation(pt[:, i, :], PS[:, 2048:2048 + T + TC], ACT.Copy), tr_,
                        fr["pt"][i])
                b4.free = b5.free = [cp]
                yield
                for t in range(6):
                    op2 = PE(lambda e, t=t, i=i, blk=blk: e.matmul(
                        b6.ap[:, 128 * blk:128 * blk + 128], v[:, t, 128 * h:128 * h + 128],
                        pt[:, i, 128 * t:128 * t + 128], start=t == 0, stop=t == 5), cp, v_tok,
                        b6.free if blk == 0 else None)
                fr["pt"][i] = [op2]
                yield
            m = V(lambda e: e.scalar_tensor_tensor(o[h], b6.ap, 0.5, sg[:, z, :], MUL, MUL), op2, tk["sg", z],
                  f1, fr["qn"][0] if h == KD - 1 else None)
            b6.free = [m]
            fr["sg"][z] = [m]
            o_op.append(m)

        o_op, o_tok = [], []
        run(proj(0))
        for h in range(KD):
            if h == KD - 1:
                st.n_free = [Q.q["pe"][-1]]
                o_tok = [split(o[j], nhi[:, j, :], nlo[:, j, :], o_op[j], st.n_free) for j in range(KD - 1)]
            weave(attend(h), proj(h + 1) if h + 1 < KD else None, 16, 12 if h % 2 == 0 else 18)
        o_tok.append(split(o[7], nhi[:, 7, :], nlo[:, 7, :], o_op[7], st.n_free))
        outputs("mla_out", go, lambda m: adas[0][:, 16 + m, 0:1], tok=o_tok, hi=nhi, lo=nlo)
        st.n_free = [Q.q["pe"][-1]]
        ph.close()

    def hyena():
        ph = ExitStack()
        f0 = fence()
        p = lambda name, shape, dt=F: sbt(ph, name + "_h", shape, dt)
        zh, zl = p("zh", [128, 4, 512], FR), p("zl", [128, 4, 512], FR)
        hh, hl = p("hh", [128, 2, 4, 512], FR), p("hl", [128, 2, 4, 512], FR)
        z = p("z", [128, 4, T])
        g = p("g", [128, 4, T])
        o = p("o", [128, 4, T])
        tmp = p("tmp", [128, 5, T])
        up = p("up", [128, 2, T + 2])
        hdn = rb2
        zu = V(lambda e: e.memset(up[:, :, 0:1], 0.0), f0)
        zu = V(lambda e: e.memset(up[:, :, T + 1:T + 2], 0.0), zu)

        drain()
        r = root(4, D, rc, [(rb, 1.0)], free=f0)

        fs = ExitStack()
        pos = sbt(fs, "pos", [64, T])
        fw = sbt(fs, "fw", [64, 3, 64])
        fa = sbt(fs, "fa", [64, 4, T])
        pl = Q.dma("sp", lambda e: e.dma_start(pos[:, :], A["pos"]), "pos", f0)
        fl = Q.dma("sp", lambda e: e.dma_start(fw[:, :, :], A["filt"]), "filt", f0)

        def hidden():
            src, tok = pos, [pl, fl]
            for l in range(3):
                b = bank[1]
                op = PE(lambda e, src=src, l=l: e.matmul(b.ap[0:64, :], fw[:, l, :], src[0:64, :], start=True,
                                                         stop=True), tok, fl, b.free)
                a = V(lambda e, l=l: e.tensor_scalar(fa[:, 0, :], b.ap[0:64, :], par[0:64, PC["fb"] + l:PC["fb"] + l + 1],
                                                     par[0:64, PC["ff"] + l:PC["ff"] + l + 1], ADD, MUL), op, par_l, f0)
                b.free = [a]
                n = V(lambda e: e.tensor_scalar(fa[:, 1, :], fa[:, 0, :], float(np.float32(1 / (2 * np.pi))), None, MUL),
                      a)
                n = V(lambda e: e.tensor_scalar(fa[:, 2, :], fa[:, 1, :], 12582912.0, None, ADD), n)
                n = V(lambda e: e.tensor_scalar(fa[:, 1, :], fa[:, 2, :], -12582912.0, None, ADD), n)
                n = V(lambda e: e.scalar_tensor_tensor(fa[:, 2, :], fa[:, 1, :], -6.28125, fa[:, 0, :], MUL, ADD), n)
                n = V(lambda e: e.scalar_tensor_tensor(fa[:, 3, :], fa[:, 1, :], -(2 * np.pi - 6.28125), fa[:, 2, :],
                                                       MUL, ADD), n)
                n = V(lambda e: e.tensor_scalar(fa[:, 0, :], fa[:, 3, :], 3.1415925, -3.1415925, ALU.min, ALU.max), n)
                a = AC(lambda e: e.activation(hdn[0:64, :], fa[:, 0, :], ACT.Sin), n, f0, op)
                src, tok = hdn, [a]
                yield
            st.hd_tok = tok

        def operands():
            for k in range(KD):
                a, st.n_tok[k] = modulated(1, hT[:, k, :], rb[:, :], nhi[:, k, :], nlo[:, k, :], k, 0,
                                           tmp[:, 2 * (k % 2):2 * (k % 2) + 2], T, [st.h_tok[k], r, f0], tf[k % 2],
                                           st.n_free)
                st.h_read[k] = st.h_read[k] + [a]
                tf[k % 2] = st.n_tok[k]
                yield

        tf = [[], []]
        weave(operands(), hidden())
        tmp_free, up_free = [tf, zu], [[zu], [zu]]
        st.f_h = fence()
        fs.close()
        z_tok, g_tok, zt_tok = [None] * 4, [None] * 4, [None] * 4
        fr = {"z": [f0] * 4, "g": [f0] * 4, "zt": f0, "h": f0, "tmp": tmp_free, "up": up_free, "y": [[], []]}

        def conv(m, b, dst, *waits):
            i = m % 2
            a = AC(lambda e: e.activation(up[:, i, 1:T + 1], b.ap, ACT.Copy), b.op, fr["up"][i])
            c0 = AC(lambda e: e.activation(tmp[:, 2 * i, :], b.ap, ACT.Identity, bias=pc("hb", m), scale=pc("hw", 24 + m)),
                    b.op, fr["tmp"])
            b.free = [a, c0]
            c1 = V(lambda e: e.scalar_tensor_tensor(tmp[:, 2 * i + 1, :], up[:, i, 0:T], pc("hw", m), tmp[:, 2 * i, :],
                                                    MUL, ADD), a, c0, fr["tmp"])
            c2 = V(lambda e: e.scalar_tensor_tensor(dst, up[:, i, 2:T + 2], pc("hw", 48 + m), tmp[:, 2 * i + 1, :],
                                                    MUL, ADD), c1, waits)
            fr["up"][i] = [c1, c2]
            fr["tmp"] = [fr["tmp"], c1, c2][-3:]
            return c2

        def filters(od, c):
            hs = ExitStack()
            f = fence()
            n_ = f"_{od}{c}"
            wl = sbt(hs, "wl" + n_, [64, 2, 512])
            ws = sbt(hs, "ws" + n_, [64, 2, 512])
            dc = sbt(hs, "dc" + n_, [128, 2, 512])
            ht = sbt(hs, "ht" + n_, [128, 2, 512])
            hs.close()
            base = od * 2048 + 512 * c
            l0_ = Q.dma("sp", lambda e: e.dma_start(wl[:, 0, :], A["filt_out"][:, base:base + 512]), "fo0", f, st.f_h)
            l1_ = Q.dma("sp", lambda e: e.dma_start(wl[:, 1, :], A["filt_out"][:, base + 1024:base + 1536]), "fo1", f,
                        st.f_h)
            w = [V(lambda e, j=j: e.tensor_tensor(ws[:, j, :], wl[:, 0, :], wl[:, 1, :], (ADD, SUB)[j]), l0_, l1_, f)
                 for j in range(2)]
            dfree, hfree, tok = [f, f], [f, f], []
            yield
            for t in range(4):
                i = t % 2
                dl = Q.dma("sp", lambda e, t=t, i=i: e.dma_start(dc[:, i, :], A["decay"][t, :, 512 * c:512 * c + 512]),
                           f"dc{i}", dfree[i], st.f_h)
                for j in range(2):
                    b = bank[4 + j]
                    op = PE(lambda e, b=b, t=t, j=j: e.matmul(b.ap, hdn[0:64, 128 * t:128 * t + 128], ws[:, j, :],
                                                              start=True, stop=True), w, st.hd_tok, b.free)
                    a = V(lambda e, b=b, i=i, j=j: e.tensor_tensor(ht[:, j, :], b.ap, dc[:, i, :], MUL), op, dl,
                          hfree[j])
                    b.free = [a]
                    sp = split(ht[:, j, :], hh[:, j, t, :], hl[:, j, t, :], a, fr["h"])
                    hfree[j] = sp
                    tok.append(sp)
                    dfree[i] = [a]
                    yield
            st.hf_tok = tok

        def turn():
            for t in range(4):
                b = bank[6 + t % 2]
                for ct in range(4):
                    op = PE(lambda e, b=b, t=t, ct=ct: e.transpose(b.ap[:, 128 * ct:128 * ct + 128],
                                                                   z[:, ct, 128 * t:128 * t + 128], ident[:, :]),
                            z_tok[ct], b.free, id_l)
                zt_tok[t] = split(b.ap, zh[:, t, :], zl[:, t, :], op, fr["zt"])
                b.free = zt_tok[t]
                yield
            st.turned = [op]

        def convolve(od, c, last):
            ys = ExitStack()
            f = fence()
            yh = sbt(ys, f"yh_{od}{c}", [128, 2, 2, 512], FR)
            yl = sbt(ys, f"yl_{od}{c}", [128, 2, 2, 512], FR)
            ys.close()
            bu, bk, bi, bj = bank[4:8]
            ks = sqb
            tf_ = [fr["tmp"], f]
            ktf = [st.sq_free, f]
            yfree = [f, f]
            y_tok = [None] * 4

            def forward(j):
                nonlocal tf_, ktf
                i = j % 2
                tok = [zt_tok, st.hf_tok]
                first = [True, False, False, False]
                for k in range(4):
                    w = W.tile("dft", k, j)
                    bu.op = mm_w(bu.ap, w, zh[:, k, :], zl[:, k, :], k == 0, k == 3, zt_tok[k], bu.free)
                    bk.op = mm_w(bk.ap, w, hh[:, 0, k, :], hl[:, 0, k, :], k == 0, k == 3, st.hf_tok, bk.free)
                kr = AC(lambda e: e.activation(ks[:, 0, :], bk.ap, ACT.Copy), bk.op, ktf)
                bk.free = [kr]
                if j == 0:
                    for k in range(4):
                        w = W.tile("alt", k, 0)
                        bk.op = mm_w(bk.ap, w, hh[:, 0, k, :], hl[:, 0, k, :], k == 0, k == 3, st.hf_tok, bk.free)
                    kp = AC(lambda e: e.activation(tmp[:, 4, :], bk.ap, ACT.Copy), bk.op, tf_)
                    bk.free = [kp]
                    kx = tmp[:, 4, :]
                else:
                    kp, kx = kr, ks[:, 0, :]
                for k in range(4):
                    w = W.tile("dft", k, 4 + j)
                    bi.op = mm_w(bi.ap, w, zh[:, k, :], zl[:, k, :], k == 0, k == 3, zt_tok[k], bi.free)
                    bj.op = mm_w(bj.ap, w, hh[:, 1, k, :], hl[:, 1, k, :], k == 0, k == 3, st.hf_tok, bj.free)
                ki = AC(lambda e: e.activation(ks[:, 1, :], bj.ap, ACT.Copy), bj.op, ktf)
                bj.free = [ki]
                if j == 0:
                    ki = V(lambda e: e.memset(ks[0:1, 1, :], 0.0), ki)
                a = V(lambda e: e.tensor_tensor(tmp[:, 0, :], bu.ap, ks[:, 0, :], MUL), bu.op, kr, tf_)
                b = V(lambda e: e.tensor_tensor(tmp[:, 1, :], bi.ap, ks[:, 1, :], MUL), bi.op, ki, tf_)
                c_ = V(lambda e: e.tensor_tensor(tmp[:, 2, :], bu.ap, ks[:, 1, :], MUL), ki, tf_)
                d = V(lambda e: e.tensor_tensor(tmp[:, 3, :], bi.ap, kx, MUL), kp, tf_)
                bu.free, bi.free = [c_], [d]
                ktf = [d]
                yr = V(lambda e: e.tensor_tensor(tmp[:, 0, :], tmp[:, 0, :], tmp[:, 1, :], SUB), a, b)
                yi = V(lambda e: e.tensor_tensor(tmp[:, 2, :], tmp[:, 2, :], tmp[:, 3, :], ADD), c_, d)
                s1 = split(tmp[:, 0, :], yh[:, i, 0, :], yl[:, i, 0, :], yr, yfree[i])
                s2 = split(tmp[:, 2, :], yh[:, i, 1, :], yl[:, i, 1, :], yi, yfree[i])
                y_tok[j] = [s1, s2]
                tf_ = [s1, s2]

            def inverse(j):
                i = j % 2
                for q in range(2):
                    w = W.tiles([("idft", 4 * q + j, m) for m in range(4)])
                    for ct in range(4):
                        cs = slice(128 * ct, 128 * ct + 128)
                        b = bank[ct]
                        b.op = mm_x(b.ap, w, yh[:, i, q, cs], yl[:, i, q, cs], j == 0 and q == 0, j == 3 and q == 1,
                                    y_tok[j][q], b.free)
                yfree[i] = [bank[3].op]

            forward(0)
            for j in range(1, 4):
                forward(j)
                inverse(j - 1)
            fr["h"] = fr["zt"] = [Q.q["pe"][-13]]
            inverse(3)
            fr["h"] = fr["zt"] = [Q.q["pe"][-1]]
            st.sq_free = [ktf, ktf]
            o_tok = []
            for ct in range(4):
                b = bank[ct]
                m = 4 * c + ct
                a = V(lambda e, b=b, ct=ct, m=m: e.scalar_tensor_tensor(tmp[:, ct, :], z[:, ct, :],
                                                                        pc("hbias", 8 * od + m), b.ap, MUL, ADD),
                      b.op, z_tok[ct], tf_)
                b.free = [a]
                dst = z[:, ct, :] if not last else o[:, ct, :]
                r_ = V(lambda e, ct=ct, dst=dst: e.tensor_tensor(dst, tmp[:, ct, :], g[:, ct, :], MUL), a, g_tok[ct],
                       st.turned, st.o_free)
                if not last:
                    z_tok[ct] = r_
                else:
                    o_tok.append(r_)
                fr["g"][ct] = [r_]
                fr["z"][ct] = [a, r_]
            fr["tmp"] = [Q.q["dve"][-1], f]
            return o_tok

        st.o_free = f0
        n_done = []
        fin = [None] * KD

        def channels(c, part):
            for ct in range(4):
                m = 8 * part + 4 * c + ct
                b = bank[ct % 2]
                yield from project(b, "hy_in", m)
                if part == 0:
                    z_tok[ct] = conv(m, b, z[:, ct, :], fr["z"][ct], st.turned)
                else:
                    g_tok[ct] = conv(m, b, g[:, ct, :], fr["g"][ct])
                if part == 2:
                    b = bank[2 + ct % 2]
                    yield from project(b, "hy_in", 24 + 4 * c + ct)
                    th = AC(lambda e, b=b: e.activation(tmp[:, 4, :], b.ap, ACT.Tanh, scale=0.5), b.op, fr["tmp"])
                    s2 = V(lambda e, b=b: e.scalar_tensor_tensor(tmp[:, 4, :], tmp[:, 4, :], 1.0, b.ap, ADD, MUL), th)
                    b.free = [s2]
                    x = V(lambda e, ct=ct: e.scalar_tensor_tensor(g[:, ct, :], g[:, ct, :], 0.5, tmp[:, 4, :],
                                                                  MUL, MUL), s2, g_tok[ct])
                    fr["tmp"] = [fr["tmp"], x]
                    g_tok[ct] = x

        def chain(*gens):
            for x in gens:
                yield from x

        st.turned = f0
        for c in range(2):
            weave(channels(c, 0), filters(0, c), 32, 9)
            weave(channels(c, 1), turn(), 32, 8)
            convolve(0, c, False)
            weave(channels(c, 2), chain(filters(1, c), turn()), 64, 20)
            if c == 1:
                st.n_free = [Q.q["pe"][-1]]
                for ct in range(4):
                    fin[ct] = split(o[:, ct, :], nhi[:, ct, :], nlo[:, ct, :], o_tok[ct], st.n_free)
                st.o_free = [fin[0:4]]
            o_tok = convolve(1, c, True)
        for ct in range(4):
            fin[4 + ct] = split(o[:, ct, :], nhi[:, 4 + ct, :], nlo[:, 4 + ct, :], o_tok[ct], st.n_free)
        outputs("hy_out", only_squares, lambda m: adas[1][:, 16 + m, 0:1], tok=fin, hi=nhi, lo=nlo)
        drain()
        root(4, D, rc, [(rb, 1.0)])
        for m in range(KD):
            h = hT[:, m, :]
            st.h_tok[m] = [V(lambda e, h=h, m=m: e.scalar_tensor_tensor(h, h, pc("final_g", m), rb[:, :], MUL, MUL),
                             st.h_tok[m], st.h_read[m], st.r_tok)]
        ph.close()

    hgrn()
    if stage >= 2:
        ffn(0, after("attn_norm"))
        root(4, D, rc, [(rb, 1.0), (rb2, 0.125)], put_off=True)
    if stage >= 3:
        swa(after("ffn_norm1"))
        root(4, D, rc, [(rb, 1.0), (rb2, 0.5)], put_off=True)
    if stage >= 4:
        ffn(1, squares_of_both)
    if stage >= 6:
        mla(only_squares)
    if stage >= 7:
        hyena()

    outs = [Q.dma("sp", lambda e, m=m: e.dma_start(A["out"][m], hT[:, m, :]), "out", st.h_tok[m]) for m in range(KD)]
    W.align()
    Q.count()
    if chunks == 10 ** 6:
        ctx.close()
        return W.at // 8, W.spec, W.found
    with ctx:
        sems = {n: ctx.enter_context(nc.semaphore(f"s_{n}")) for n in ("pe", "act", "dve", "pool", *Q.dmas)}
        block = ctx.enter_context(nc.Block())

        @block.sync
        def _(eng):
            Q.emit("sp", eng, sems)
            eng.wait_ge(sems["out"], Q.dmas["out"])

        @block.scalar
        def _(eng):
            Q.emit("act", eng, sems)

        @block.vector
        def _(eng):
            Q.emit("dve", eng, sems)

        @block.gpsimd
        def _(eng):
            Q.emit("pool", eng, sems)

        @block.tensor
        def _(eng):
            Q.emit("pe", eng, sems)
    return W.at // 8, W.spec, W.found


def masks():
    s = np.arange(128)[:, None]
    t = np.arange(128)[None, :]
    out = [s == t]
    for lv in range(LV):
        b = 1 << lv
        out.append((s // (2 * b) == t // (2 * b)) & (s // b % 2 == 0) & (t // b % 2 == 1))
    return np.ascontiguousarray(np.stack(out, 1).astype(np.float32))


def distances():
    d = np.arange(128)[:, None] + 128 - np.arange(256)[None, :]
    ok = (d >= 0) & (d < 128)
    first = ok & (np.arange(256)[None, :] >= 128)
    return np.ascontiguousarray(np.stack([np.where(first, d, 1e30), np.where(ok, d, 1e30)], 1).astype(np.float32))


def rope():
    t = np.arange(T)
    inv = np.float32(10000.0) ** (-np.arange(16, dtype=np.float32) / np.float32(16))
    ang = np.concatenate([(t // 64).astype(np.float32)[:, None] * inv, (t % 64).astype(np.float32)[:, None] * inv], 1)
    c, s = np.cos(ang, dtype=np.float32).T, np.sin(ang, dtype=np.float32).T
    return np.ascontiguousarray(np.stack([np.concatenate([c, c, c, c]), np.concatenate([-s, s, -s, s])], 1))


def fourier():
    t = np.arange(T)
    w = 2 * np.pi * (np.outer(t, t) % 1024) / 1024
    c, s = np.cos(w), -np.sin(w)
    alt = np.where(t % 2, -1.0, 1.0)
    s[:, 0] = alt
    c2 = c[:, 0:128].copy()
    c2[:, 0] = alt
    ic, isn = 2 * np.cos(w) / 1024, -2 * np.sin(w) / 1024
    ic[0, :] = 1 / 1024
    isn[0, :] = alt / 1024
    f = np.float32
    return np.concatenate([c, s], 1).astype(f), c2.astype(f), np.concatenate([ic, isn], 0).astype(f)


def filter_tables():
    f = np.float32
    t = np.linspace(0.0, 1.0, T, dtype=f)[:, None]
    wpos = f(2.0 * np.pi / T) * np.arange(T, dtype=f)[:, None]
    bands = np.linspace(1e-4, 15, 16, dtype=f)[None, :]
    x = np.concatenate([t, np.cos(bands * wpos), -np.sin(bands * wpos)], 1).astype(f)
    pos = np.zeros((64, T), f)
    pos[0:33] = x.T
    deltas = np.abs(np.linspace(np.log(1e-2) / 0.3, np.log(1e-2) / 1.5, D, dtype=f))
    return pos, np.exp(-t * deltas).astype(f).reshape(4, 128, D)


def filter_weights(i):
    w = np.zeros((64, 3, 64), np.float32)
    w[0:33, 0] = i["hy_filt_w_in_2"][0]
    w[:, 1], w[:, 2] = i["hy_filt_w_hid_2"][0][0], i["hy_filt_w_hid_2"][0][1]
    return w


def cols(a):
    a = np.asarray(a).reshape(-1)
    return a.reshape(-1, 128).T


def params(i):
    p = {
        "hg_norm": cols(i["hg_norm"][0]), "lb0": cols(i["hg_lb_logits"][0]), "lb1": cols(i["hg_lb_logits"][1]),
        "out_norm": cols(i["hg_out_norm"][0]), "kv_norm": cols(i["kv_norm"]), "attn_norm": cols(i["attn_norm"][0]),
        "ffn_norm0": cols(i["ffn_norm"][0]), "ffn_norm1": cols(i["ffn_norm"][1]),
        "final_norm": cols(i["final_norm"]), "norm_g0": cols(i["norm_g_2"][0]), "norm_g1": cols(i["norm_g_2"][1]),
        "final_g": cols(i["final_g_2"]), "q_norm": cols(i["mla_q_norm_g_2"][0]),
        "kvl_norm": cols(i["mla_kv_norm_g_2"][0]),
        "sink": np.broadcast_to(np.asarray(i["attn_sinks"][0])[None, :], (128, 16)),
        "eps": np.full((128, 1), EPS, np.float32),
        "cw0": cols(i["ffn_conv_w"][0]), "cw1": cols(i["ffn_conv_w"][1]),
        "cb0": cols(i["ffn_conv_b"][0]), "cb1": cols(i["ffn_conv_b"][1]),
        "ada_b0": cols(i["ada_b_2"][0]), "ada_b1": cols(i["ada_b_2"][1]),
        "c": cols(i["c_2"][0]), "cc": cols(i["c_ctx_2"]),
        "hw": cols(i["hy_conv_w_2"][0]), "hb": cols(i["hy_conv_b_2"][0]), "hbias": cols(i["hy_bias_2"][0]),
        "fb": np.pad(np.asarray(i["hy_filt_b_2"][0]).T, ((0, 64), (0, 0))),
        "ff": np.pad(np.asarray(i["hy_filt_freq_2"][0]).T, ((0, 64), (0, 0))),
    }
    out = np.empty((128, NPAR), np.float32)
    for name, w in PAR:
        out[:, PC[name]:PC[name] + w] = p[name]
    return out


def matrices(i):
    kv = np.asarray(i["w_kv"])
    k0, k1, vv = kv[:, 0:64], kv[:, 64:128], kv[:, 128:256]
    mi = np.asarray(i["mla_w_in_2"][0])
    uq = np.asarray(i["mla_w_uq_2"][0]).reshape(384, 8, 192)
    ukv = np.asarray(i["mla_w_ukv_2"][0]).reshape(256, 8, 256)
    dft, alt, idft = fourier()
    return {
        "w_in": i["hg_w_in"][0], "w_out": i["hg_w_out"][0],
        "up0": i["ffn_w_up"][0], "up1": i["ffn_w_up"][1],
        "down0": i["ffn_w_down"][0], "down1": i["ffn_w_down"][1],
        "kv": np.concatenate([k0, k0, k1, k1, vv], 1),
        "mla_in": np.concatenate([mi[:, 0:704], mi[:, 672:704], mi[:, 640:672], mi[:, 704:]], 1),
        "uq": np.concatenate([uq[:, :, 0:128].reshape(384, 1024)] + [
            x for h in range(0, 8, 2) for x in (
                uq[:, h, 128:], uq[:, h + 1, 128:], uq[:, h, 160:], uq[:, h, 128:160], uq[:, h + 1, 160:],
                uq[:, h + 1, 128:160])], 1),
        "ukv": np.concatenate([ukv[:, :, 0:128].reshape(256, 1024), ukv[:, :, 128:].reshape(256, 1024)], 1),
        "mla_out": i["mla_w_out_2"][0], "ada0": i["ada_w_2"][0], "ada1": i["ada_w_2"][1],
        "hy_in": i["hy_w_in_2"][0], "hy_out": i["hy_w_out_2"][0], "dft": dft, "alt": alt, "idft": idft,
        "wq": i["attn_w_q"][0], "wo": i["attn_w_o"][0],
    }


def pack(spec, mats):
    out = np.zeros((len(spec) // 8, 128, 1024), np.float32)
    mats = {n: np.asarray(a) for n, a in mats.items()}
    for j, x in enumerate(spec):
        if x is not None:
            name, k, m = x
            out[j // 8, :, j % 8 * 128:j % 8 * 128 + 128] = mats[name][128 * k:128 * k + 128, 128 * m:128 * m + 128]
    return out


def feature_major(x):
    return np.ascontiguousarray(np.asarray(x).T.reshape(KD, 128, -1))


def prepare(inputs, fresh, stage=99):
    def declare(nc, shapes):
        return {n: nc.dram_tensor(f"in_{n}", s, F, kind="ExternalInput").ap()
                for n, s in shapes.items()}

    i = inputs
    pos, decay = filter_tables()
    arrays = {
        "par": params(i), "xT": feature_major(i["x"][0]), "ident": np.eye(128, dtype=np.float32), "masks": masks(),
        "pos": pos, "decay": decay, "filt": filter_weights(i), "filt_out": np.asarray(i["hy_filt_w_out_2"][0]),
        "dist": distances(), "rope": rope(),
        "ctx": np.ascontiguousarray(np.asarray(i["ctx_2"][0]).T.reshape(KD, 128, TC).transpose(1, 0, 2)),
    }
    res = (10 ** 6, None, set())
    for _ in range(2):
        nc = fresh()
        n = res[0]
        A = declare(nc, {**{k: a.shape for k, a in arrays.items()}, "stream": (n, 128, 1024)})
        A["out"] = nc.dram_tensor("out_0", (KD, 128, T), F, kind="ExternalOutput").ap()
        res = build(nc, A, n, res[2], stage)
    arrays["stream"] = pack(res[1], matrices(i))
    return nc, {f"in_{k}": a for k, a in arrays.items()}


def kernel(**inputs):
    import concourse.bacc as _bacc
    from concourse.bass_utils import run_bass_kernel_spmd as _run

    nc, arrays = prepare(inputs, lambda: _bacc.Bacc("TRN2", target_bir_lowering=False, num_devices=1))
    r = _run(nc, [arrays], core_ids=[0])
    out = r.results[0]["out_0"]
    return np.ascontiguousarray(out.reshape(D, T).T).reshape(1, T, D)
```

```python
from contextlib import ExitStack

import numpy as np

import concourse.bass as bass
from concourse import mybir

F = mybir.dt.float32
FR = mybir.dt.float32r
I32 = mybir.dt.int32
ALU = mybir.AluOpType
ACT = mybir.ActivationFunctionType
AX_X = mybir.AxisListType.X
MUL, ADD, SUB = ALU.mult, ALU.add, ALU.subtract

T = 512
D = 1024
KD = 8
FT = 22
HF = 11
TC = 256
RAW, HL = 4, 3
EPS = 1e-6
LV = 7


PAR = [("hg_norm", 8), ("lb0", 8), ("lb1", 8), ("out_norm", 1), ("kv_norm", 8), ("attn_norm", 8),
       ("ffn_norm0", 8), ("ffn_norm1", 8), ("final_norm", 8), ("norm_g0", 8), ("norm_g1", 8),
       ("final_g", 8), ("q_norm", 3), ("kvl_norm", 2), ("sink", 16), ("eps", 1),
       ("cw0", 66), ("cw1", 66), ("cb0", 22), ("cb1", 22), ("ada_b0", 24), ("ada_b1", 24),
       ("c", 8), ("cc", 8), ("hw", 72), ("hb", 24), ("hbias", 16), ("fb", 3), ("ff", 3), ("sel", 2)]
PC = {}
_n = 0
for _name, _w in PAR:
    PC[_name] = _n
    _n += _w
NPAR = _n


class Op:
    __slots__ = ("eng", "fn", "waits", "inc", "sem", "val")

    def __init__(self, eng, fn, waits, sem=None, val=0):
        self.eng, self.fn, self.waits, self.sem, self.val, self.inc = eng, fn, waits, sem, val, False


def flat(x, out):
    for y in x:
        if isinstance(y, Op):
            out.append(y)
        elif y:
            flat(y, out)
    return out


class Queues:

    def __init__(self):
        self.q = {e: [] for e in ("pe", "act", "dve", "pool", "sp")}
        self.dmas = {}

    def add(self, eng, fn, *waits):
        op = Op(eng, fn, flat(waits, []))
        self.q[eng].append(op)
        return op

    def dma(self, eng, fn, sem, *waits):
        self.dmas[sem] = self.dmas.get(sem, 0) + 16
        op = Op(eng, fn, flat(waits, []), sem, self.dmas[sem])
        self.q[eng].append(op)
        return op

    def count(self):
        for ops in self.q.values():
            for op in ops:
                for w in op.waits:
                    if w.sem is None:
                        w.inc = True
        for ops in self.q.values():
            n = 0
            for op in ops:
                if op.sem is None and op.inc:
                    n += 1
                    op.val = n

    def emit(self, name, eng, sems):
        seen = {}
        for op in self.q[name]:
            need = {}
            for w in op.waits:
                s = w.sem or w.eng
                need[s] = max(need.get(s, 0), w.val)
            for s, v in need.items():
                if seen.get(s, 0) < v:
                    eng.wait_ge(sems[s], v)
                    seen[s] = v
            ins = op.fn(eng)
            if op.sem is not None:
                ins.then_inc(sems[op.sem], 16)
            elif op.inc:
                ins.then_inc(sems[name], 1)


class Bank:

    def __init__(self, ap):
        self.ap, self.free = ap, []


class Tile:
    __slots__ = ("hi", "lo", "tok", "chunk")


class Weights:

    def __init__(self, Q, dram, raw, hi, lo, chunks):
        self.Q, self.dram, self.raw, self.hi, self.lo, self.chunks = Q, dram, raw, hi, lo, chunks
        self.spec, self.split, self.last, self.load = [], {}, {}, {}
        self.at = self.loaded = 0

    def fetch(self):
        while self.loaded < self.chunks:
            c, old = self.loaded, self.loaded - RAW
            if old >= 0 and old not in self.split:
                return
            waits = self.split.get(old)
            dst, src = self.raw[:, c % RAW, :], self.dram[c]
            self.load[c] = self.Q.dma("sp", lambda e, dst=dst, src=src: e.dma_start(dst, src), f"w{c % RAW}", [waits])
            self.loaded += 1
            if old < 0 and self.loaded % RAW:
                return

    def prepare(self, c):
        if c >= self.chunks or c in self.split:
            return
        old = self.last.get(c - HL)
        r, hi, lo = self.raw[:, c % RAW, :], self.hi[:, c % HL, :], self.lo[:, c % HL, :]
        a = self.Q.add("act", lambda e: e.activation(hi, r, ACT.Copy), self.load[c], old)
        v = self.Q.add("dve", lambda e: e.tensor_tensor(lo, r, hi.bitcast(F), SUB), a, old)
        self.split[c] = [a, v]
        self.fetch()

    def tiles(self, names):
        n, at = len(names), self.at
        c = at // 8
        assert (at + n - 1) // 8 == c
        if at % 8 == 0:
            self.prepare(c)
            self.prepare(c + 1)
        elif at % 8 == 6:
            self.prepare(c + 2)
        self.spec += names
        self.at += n
        t = Tile()
        o = at % 8 * 128
        t.hi, t.lo = self.hi[:, c % HL, o:o + n * 128], self.lo[:, c % HL, o:o + n * 128]
        t.tok, t.chunk = self.split[c], c
        return t

    def tile(self, name, k, m):
        return self.tiles([(name, k, m)])

    def used(self, t, op):
        self.last[t.chunk] = op

    def align(self):
        while self.at % 8:
            self.spec.append(None)
            self.at += 1


def weave(main, side, nm=1, ns=1, lead=0):
    side = iter(side) if side is not None else iter(())
    done = 0
    for n, _ in enumerate(main):
        while done * nm < (n + 1 - lead) * ns:
            next(side, None)
            done += 1
    for _ in side:
        pass


def build(nc, A, chunks, stage=99):
    Q = Queues()
    ctx = ExitStack()

    def sbt(stack, name, shape, dt=F):
        return stack.enter_context(nc.sbuf_tensor(name, shape, dt))

    def sb(name, shape, dt=F):
        return sbt(ctx, name, shape, dt)

    PE = lambda fn, *w: Q.add("pe", fn, *w)
    AC = lambda fn, *w: Q.add("act", fn, *w)
    V = lambda fn, *w: Q.add("dve", fn, *w)
    G = lambda fn, *w: Q.add("pool", fn, *w)

    def fence():
        return [Q.q[e][-1] for e in ("pe", "act", "dve", "pool") if Q.q[e]]

    hT = sb("hT", [128, KD, T])
    raw = sb("raw", [128, RAW, 1024])
    whi = sb("whi", [128, HL, 1024], FR)
    wlo = sb("wlo", [128, HL, 1024], FR)
    nhi = sb("nhi", [128, KD, T], FR)
    nlo = sb("nlo", [128, KD, T], FR)
    par = sb("par", [128, NPAR])
    ident = sb("ident", [128, 128])
    ones = sb("ones", [128, 128])
    rb = sb("rb", [128, T])
    rb2 = sb("rb2", [128, T])
    rc = sb("rc", [128, 8])
    sd = sb("sd", [128, 8])
    diag = sb("diag", [128, 4, 128])
    sqb = sb("sqb", [128, 2, T])
    lb = sb("lb", [128, 8, 8])
    PS = ctx.enter_context(nc.psum_tensor("PS", [128, 8 * 512], F))
    bank = [Bank(PS[:, 512 * i:512 * i + 512]) for i in range(8)]
    pc = lambda name, i=0: par[:, PC[name] + i:PC[name] + i + 1]

    W = Weights(Q, A["stream"], raw, whi, wlo, chunks)

    par_l = Q.dma("sp", lambda e: e.dma_start(par[:, :], A["par"]), "par")
    x_l = []
    for m in range(KD):
        if m == 2:
            W.fetch()
        x_l.append(Q.dma("sp", lambda e, m=m: e.dma_start(hT[:, m, :], A["xT"][m]), f"x{m}"))
    id_l = Q.dma("sp", lambda e: e.dma_start(ident[:, :], A["ident"]), "id")
    for _ in range(RAW - 1):
        W.fetch()
    one_o = V(lambda e: e.memset(ones[:, :], 1.0))

    def mm_w(out, w, xh, xl, first, last, *waits):
        PE(lambda e: e.matmul(out, w.hi, xh, start=first, stop=False), w.tok, waits)
        PE(lambda e: e.matmul(out, w.hi, xl, start=False, stop=False))
        op = PE(lambda e: e.matmul(out, w.lo, xh, start=False, stop=last))
        W.used(w, op)
        return op

    def mm_x(out, w, xh, xl, first, last, *waits, skip=False):
        PE(lambda e: e.matmul(out, xh, w.hi, start=first, stop=False, skip_group_check=skip), w.tok, waits)
        PE(lambda e: e.matmul(out, xh, w.lo, start=False, stop=False, skip_group_check=skip))
        op = PE(lambda e: e.matmul(out, xl, w.hi, start=False, stop=last, skip_group_check=skip))
        W.used(w, op)
        return op

    class State:
        pass

    st = State()
    st.n_tok = [[] for _ in range(KD)]
    st.n_free = []
    st.h_tok = [[x_l[m]] for m in range(KD)]
    st.h_read = [[] for _ in range(KD)]
    st.sq_free = [[], []]
    st.rb_free = []
    st.sc_free = []
    stat = bank[7]

    def project(b, name, m, ks=KD, k0=0, hi=None, lo=None, tok=None):
        hi, lo, tok = (nhi, nlo, st.n_tok) if hi is None else (hi, lo, tok)
        free = b.free
        for k in range(ks):
            w = W.tile(name, k0 + k, m)
            xh, xl = (hi[k], lo[k]) if isinstance(hi, list) else (hi[:, k, :], lo[:, k, :])
            op = mm_w(b.ap, w, xh, xl, k == 0, k == ks - 1, tok[k], free if k == 0 else None)
            b.op = op
            if k in (3, 7) and later:
                later.pop(0)()
            yield

    def run(gen):
        for _ in gen:
            pass

    later = []

    def drain():
        while later:
            later.pop(0)()

    def square_in(m, src, waits, first, last, nt=4, width=T, col=0, gain=1.0, put_off=False):
        s = m % 2
        dst = sqb[:, s, 0:width]
        q = AC(lambda e: e.activation(dst, src, ACT.Square, scale=gain), waits, st.sq_free[s])

        def sums():
            for t in range(nt):
                op = PE(lambda e, t=t: e.matmul(stat.ap[:, col + t:col + t + 1], sqb[:, s, 128 * t:128 * t + 128],
                                                ones[:, 0:1], start=first and t == 0, stop=last,
                                                skip_group_check=True),
                        q if t == 0 else None, one_o, stat.free if first and t == 0 else None)
            st.sq_free[s] = [op]
            st.stat_op = op

        if put_off:
            later.append(sums)
        else:
            sums()
        return q

    def spread(r, nt, dst_c, dsts, free=()):
        out, prev = [], st.sc_free
        for g in range(0, nt, 4):
            n = min(4, nt - g)
            c = slice(128 * g, 128 * (g + n))
            d = V(lambda e, g=g, n=n: e.tensor_tensor(
                diag[:, 0:n, :], ident[:, :].unsqueeze(1).to_broadcast((128, n, 128)),
                dst_c[:, g:g + n].unsqueeze(2).to_broadcast((128, n, 128)), MUL), r, id_l, prev)

            def rest(d=d, n=n, c=c):
                nonlocal out
                p = PE(lambda e: e.matmul(stat.ap[:, 0:128 * n], ones[:, :],
                                          diag[:, 0:n, :].rearrange("p a b -> p (a b)"), start=True, stop=True),
                       d, r, out, stat.free)
                o = [AC(lambda e, t=t, f=f: e.activation(t[:, c], stat.ap[:, 0:128 * n], ACT.Copy, scale=f), p, free)
                     for t, f in dsts]
                out = out + o
                st.sc_free = [p]
                stat.free = out

            if g + 4 < nt:
                rest()
                prev = st.sc_free
            else:
                last = rest
        return last, lambda: out

    def root(nt, width, dst_c, dsts, free=(), put_off=False, keep=None):
        def first():
            a = AC(lambda e: e.activation(sd[:, 0:nt], stat.ap[:, 0:nt], ACT.Sqrt, bias=pc("eps"),
                                          scale=1.0 / width), st.stat_op, par_l, st.sc_free)
            stat.free = [a]
            r = V(lambda e: e.reciprocal(dst_c[:, 0:nt], sd[:, 0:nt]), a, free)
            last, out = spread(r, nt, dst_c, dsts, free)

            def second():
                last()
                if keep is None:
                    st.r_tok = out() + [r]
                else:
                    keep.extend(out() + [r])

            if put_off:
                later.insert(0, second)
            else:
                second()

        if put_off:
            later.append(first)
        else:
            first()
            return st.r_tok

    def split_scaled(src, gain, dh, dl, *waits):
        a = AC(lambda e: e.activation(dh, src, ACT.Copy, scale=gain), waits)
        v = V(lambda e: e.scalar_tensor_tensor(dl, src, gain, dh.bitcast(F), MUL, SUB), a, waits)
        return [a, v]

    def split(src, dh, dl, *waits):
        a = AC(lambda e: e.activation(dh, src, ACT.Copy), waits)
        v = V(lambda e: e.tensor_tensor(dl, src, dh.bitcast(F), SUB), a, waits)
        return [a, v]

    def after(gain, put_off=True):
        def go(m):
            q = square_in(m, hT[:, m, :], st.h_tok[m], m == 0, m == KD - 1, put_off=put_off)
            st.n_tok[m] = split_scaled(hT[:, m, :], pc(gain, m), nhi[:, m, :], nlo[:, m, :], st.h_tok[m],
                                       par_l, st.n_free)
            st.h_read[m] = [q] + st.n_tok[m]
        return go

    def residual(m, b, scale=None):
        h = hT[:, m, :]
        if scale is None:
            v = V(lambda e: e.tensor_tensor(h, h, b.ap, ADD), b.op, st.h_tok[m], st.h_read[m])
        else:
            v = V(lambda e: e.scalar_tensor_tensor(h, b.ap, scale, h, MUL, ADD), b.op, st.h_tok[m], st.h_read[m],
                  st.ada_tok)
        b.free = [v]
        st.h_tok[m] = [v]

    def begin(name, banks, steps, **kw):
        for m, b in enumerate(banks):
            gen = project(b, name, m, **kw)
            begun.append((b, gen))
            for _ in range(steps):
                next(gen)
                yield

    begun = []

    def outputs(name, go, scale=None, bs=4, **kw):
        for m in range(KD):
            b, gen = begun.pop(0) if begun else (bank[m % bs], None)
            run(gen or project(b, name, m, **kw))
            residual(m, b, scale and scale(m))
            if go:
                go(m)

    l0, l1 = par[:, PC["lb0"]:PC["lb0"] + 8], par[:, PC["lb1"]:PC["lb1"] + 8]
    go = after("hg_norm", False)
    for m in range(KD):
        go(m)
    root(4, D, rc, [(rb, 1.0), (rb2, 0.5 * 128 ** -0.5)], put_off=True)
    o = V(lambda e: e.tensor_tensor(lb[:, 0, :], l0, l1, ALU.max), par_l)
    o1 = V(lambda e: e.tensor_tensor(lb[:, 1, :], l0, lb[:, 0, :], SUB), o)
    o2 = V(lambda e: e.tensor_tensor(lb[:, 2, :], l1, lb[:, 0, :], SUB), o)
    o1 = AC(lambda e: e.activation(lb[:, 3, :], lb[:, 1, :], ACT.Exp), o1)
    o2 = AC(lambda e: e.activation(lb[:, 4, :], lb[:, 2, :], ACT.Exp), o2)
    o = V(lambda e: e.tensor_tensor(lb[:, 5, :], lb[:, 3, :], lb[:, 4, :], ADD), o1, o2)
    o = V(lambda e: e.reciprocal(lb[:, 6, :], lb[:, 5, :]), o)
    o = V(lambda e: e.tensor_tensor(lb[:, 7, :], lb[:, 3, :], lb[:, 6, :], MUL), o)
    o = V(lambda e: e.tensor_scalar(lb[:, 0, :], lb[:, 7, :], -0.5, 0.5, MUL, ADD), o)
    lb_o = V(lambda e: e.tensor_tensor(lb[:, 1, :], lb[:, 7, :], lb[:, 0, :], ADD), o)

    def hgrn():
        ph = ExitStack()
        p = lambda name, shape, dt=F: sbt(ph, name, shape, dt)
        v = p("v", [128, 4, D])
        ohi = p("ohi", [128, KD, T], FR)
        olo = p("olo", [128, KD, T], FR)
        tq = p("tq", [128, 2, T])
        th = p("th", [128, 2, T])
        q = p("q", [128, 2, T])
        ff = p("ff", [128, 2, T])
        kk = p("kk", [128, 2, T])
        sg = p("sg", [128, 2, T])
        qa = p("qa", [128, T])
        fb = p("fb", [128, T])
        sc = p("sc", [128, 4, 128])
        kt = p("kt", [128, 3, 128])
        S = p("S", [128, 3, 128])
        og = p("og", [128, 2, T])
        mask = p("mask", [128, LV + 1, 128])
        mk = Q.dma("sp", lambda e: e.dma_start(mask[:, :, :], A["masks"]), "mask")
        z = V(lambda e: e.memset(sc[:, :, :], 0.0))

        v_tok = []
        for g in range(2):
            bs = [bank[4 * g + t] if 4 * g + t < 7 else bank[0] for t in range(4)]
            for k in range(KD):
                w = W.tiles([("w_in", k, 16 + 4 * g + j) for j in range(4)])
                for t in range(4):
                    s = slice(128 * t, 128 * t + 128)
                    op = mm_x(bs[t].ap, w, nhi[:, k, s], nlo[:, k, s], k == 0, k == KD - 1, st.n_tok[k],
                              bs[t].free if k == 0 else None)
                    bs[t].op = op
                if later:
                    later.pop(0)()
            drain()
            r = st.r_tok
            for t in range(4):
                b = bs[t]
                a = AC(lambda e, t=t, b=b, g=g: e.activation(v[:, t, 512 * g:512 * g + 512], b.ap, ACT.Copy,
                                                        scale=rc[:, t:t + 1]), b.op, r)
                b.free = [a]
                v_tok.append(a)

        st.q_free = [[], []]
        st.sg_free = [[], []]
        st.o_tok = [None] * KD

        def proj(h):
            s = h % 2
            bq, bf, bg = bank[0], bank[1], bank[2]
            old = st.q_free[s]
            yield from project(bq, "w_in", h)
            a = V(lambda e: e.tensor_tensor(tq[:, 0, :], bq.ap, rb2[:, :], MUL), bq.op, r, st.t_free)
            bq.free = [a]
            b = AC(lambda e: e.activation(th[:, 0, :], tq[:, 0, :], ACT.Tanh, scale=128 ** 0.5), a, st.t_free)
            qo = V(lambda e: e.scalar_tensor_tensor(q[:, s, :], th[:, 0, :], 1.0, tq[:, 0, :], ADD, MUL), b, old)
            yield from project(bf, "w_in", 8 + h)
            a = V(lambda e: e.tensor_tensor(tq[:, 1, :], bf.ap, rb[:, :], MUL), bf.op, st.t_free)
            bf.free = [a]
            b = AC(lambda e: e.activation(th[:, 1, :], tq[:, 1, :], ACT.Tanh, scale=0.5), a, st.t_free)
            f = V(lambda e: e.tensor_scalar(ff[:, s, :], th[:, 1, :], lb[:, 0, h:h + 1], lb[:, 1, h:h + 1], MUL, ADD),
                  b, lb_o, old)
            ko = V(lambda e: e.tensor_scalar(kk[:, s, :], ff[:, s, :], -1.0, 1.0, MUL, ADD), f)
            st.t_free = [qo]
            st.qkf = [qo, f, ko]
            yield from project(bg, "w_in", 24 + h)
            a = V(lambda e: e.tensor_tensor(tq[:, 0, :], bg.ap, rb[:, :], MUL), bg.op, qo)
            bg.free = [a]

            def gate():
                b = AC(lambda e: e.activation(th[:, 0, :], tq[:, 0, :], ACT.Tanh, scale=0.5), a, qo)
                g = V(lambda e: e.scalar_tensor_tensor(sg[:, s, :], th[:, 0, :], 1.0, tq[:, 0, :], ADD, MUL), b,
                      st.sg_free[s])
                st.t_free = [g, f]
                st.sg_tok = [g]

            st.gate = gate

        st.t_free = []
        st.kt_free, st.S_free, st.og_free = [], [], []
        st.sc_tok = [z]

        def scan(h):
            s = h % 2
            qq, kx, fx = q[:, s, :], kk[:, s, :], ff[:, s, :]
            qo, fo, ko = st.qkf
            hc = slice(128 * h, 128 * h + 128)

            def scores(level, b, qx, *waits):
                for c in range(4):
                    cs = slice(128 * c, 128 * c + 128)
                    op = PE(lambda e, cs=cs: e.matmul(b.ap[:, cs], kx[:, cs], qx[:, cs], start=True, stop=True),
                            waits if c == 0 else None, b.free if c == 0 else None)

                def pick():
                    cp = V(lambda e: e.copy_predicated(
                        sc[:, :, :], mask[:, level, :].bitcast(I32).unsqueeze(1).to_broadcast((128, 4, 128)),
                        b.ap.rearrange("p (c t) -> p c t", c=4)), op, mk, st.sc_tok)
                    st.sc_tok = [cp]
                    b.free = [cp]
                    cps.append(cp)

                cp_later.append(pick)
                return op

            a = V(lambda e: e.tensor_tensor(qa[:, :], qq, fx, MUL), qo, fo, st.qa_free)
            yield
            cps, cp_later = [], []
            op = scores(0, bank[3], qq, qo, ko)
            cp_later.pop()()
            yield
            st.gate()
            sgt = st.sg_tok
            qt, kt_, ft = [a], [ko], [fo]
            fsrc = fx
            for lv in range(LV):
                b = 1 << lv
                op = scores(lv + 1, bank[4 - lv % 2], qa, qt, kt_)
                n = T // (2 * b)
                fs = fsrc[:, 0:2 * n].rearrange("p (n a) -> p n a", a=2)
                qv = qa[:, :].rearrange("p (n a b) -> p n a b", a=2, b=b)
                kv = kx.rearrange("p (n a b) -> p n a b", a=2, b=b)
                sh = (128, n, b)
                qt = [V(lambda e, qv=qv, fs=fs, sh=sh: e.tensor_tensor(
                    qv[:, :, 1, :], qv[:, :, 1, :], fs[:, :, 0:1].to_broadcast(sh), MUL), op, qt, ft)]
                if cp_later:
                    cp_later.pop()()
                kt_ = [G(lambda e, kv=kv, fs=fs, sh=sh: e.tensor_tensor(
                    kv[:, :, 0, :], kv[:, :, 0, :], fs[:, :, 1:2].to_broadcast(sh), MUL), op, kt_, ft)]
                o0 = 0 if lv % 2 == 0 else 256
                fdst = fb[:, o0:o0 + n]
                ft = [G(lambda e, fs=fs, fdst=fdst, n=n: e.tensor_tensor(
                    fdst.unsqueeze(2), fs[:, :, 0:1], fs[:, :, 1:2], MUL), ft, st.fb_free, qt)]
                fsrc = fdst
                yield
            b3 = bank[3]
            for c in range(3):
                cs = slice(128 * c, 128 * c + 128)
                op = PE(lambda e, cs=cs: e.transpose(b3.ap[:, cs], kx[:, cs], ident[:, :]), kt_, b3.free, id_l)
            a = AC(lambda e: e.activation(kt[:, :, :].rearrange("p a b -> p (a b)"), b3.ap[:, 0:384], ACT.Copy),
                   op, st.kt_free)
            b3.free = [a]
            yield
            b4 = bank[4]
            for c in range(3):
                cs = slice(128 * c, 128 * c + 128)
                op = PE(lambda e, c=c, cs=cs: e.matmul(b4.ap[:, cs], kt[:, c, :], v[:, c, hc], start=True, stop=True),
                        a, b4.free, v_tok)
            st.kt_free = [op]
            so = [V(lambda e: e.tensor_copy(S[:, 0, :], b4.ap[:, 0:128]), op, st.S_free)]
            for c in (1, 2):
                so.append(V(lambda e, c=c: e.scalar_tensor_tensor(S[:, c, :], S[:, c - 1, :], fsrc[:, c:c + 1],
                                                                  b4.ap[:, 128 * c:128 * c + 128], MUL, ADD),
                            so[-1], ft, st.S_free))
            b4.free = [so[-1]]
            st.fb_free = [so[-1]]
            yield
            bo = bank[5 + h % 2]
            for c in range(4):
                cs = slice(128 * c, 128 * c + 128)
                op = PE(lambda e, c=c, cs=cs: e.matmul(bo.ap[:, cs], v[:, c, hc], sc[:, c, :], start=True,
                                                       stop=c == 0), bo.free, cps, v_tok)
                st.sc_tok = st.sc_tok + [op]
                if c:
                    op = PE(lambda e, c=c, cs=cs: e.matmul(bo.ap[:, cs], S[:, c - 1, :], qa[:, cs], start=False,
                                                           stop=True), so[c - 1], qt)
            st.S_free = st.qa_free = [op]
            st.q_free[s] = [op, kt_[0], ft[0], qt[0]]
            yield
            qs = square_in(h, bo.ap, op, True, True, put_off=True)
            yield
            drain()
            root(4, 128, rch, [(rbh, 1.0)], free=st.og_free, put_off=True)
            later.pop(0)()
            yield
            yield
            drain()
            rt = st.r_tok
            a = V(lambda e: e.scalar_tensor_tensor(og[:, 0, :], bo.ap, pc("out_norm"), rbh[:, :], MUL, MUL), rt, qs,
                  st.og_free)
            bo.free = [a]
            m = V(lambda e: e.scalar_tensor_tensor(og[:, 1, :], og[:, 0, :], 0.5, sg[:, s, :], MUL, MUL), a, sgt,
                  st.og_free)
            st.sg_free[s] = [m]
            st.o_tok[h] = split(og[:, 1, :], ohi[:, h, :], olo[:, h, :], m)
            st.og_free = [a] + st.o_tok[h]
            yield

        st.qa_free, st.fb_free = [], []
        rch = p("rch", [128, 4])
        rbh = p("rbh", [128, T])
        run(proj(0))
        for h in range(KD):
            nxt = proj(h + 1) if h + 1 < KD else begin("w_out", bank[0:3], KD - 1, hi=ohi, lo=olo, tok=st.o_tok)
            weave(scan(h), nxt, 16, 24)
        st.n_free = [Q.q["pe"][-1]]
        drain()
        outputs("w_out", after("ffn_norm0"), hi=ohi, lo=olo, tok=st.o_tok)
        root(4, D, rc, [(rb, 1.0), (rb2, 0.5)], put_off=True)
        ph.close()

    def ffn(layer, go, beside=None):
        ph = ExitStack()
        f0 = fence()
        p = lambda name, shape, dt=F: sbt(ph, f"{name}_f{layer}", shape, dt)
        hh = p("hh", [128, HF, T], FR)
        hl = p("hl", [128, HF, T], FR)
        gp = p("gp", [128, 2, T + 2])
        t = p("t", [128, 6, 2, T])
        up, dn = f"up{layer}", f"down{layer}"
        z = V(lambda e: e.memset(gp[:, :, 0:2], 0.0), f0)
        ad = adapt(layer, bank[6], 2 - layer, p("row", [4, 512]), f0)
        side = beside(p, f0) if beside else iter(())
        cw, cb = f"cw{layer}", f"cb{layer}"
        gfree, tfree = [[z], [z]], [f0, f0]
        hid, hfree = [None] * HF, f0

        def tail(f, bg, bv):
            s, i = f % 2, f % HF
            g = V(lambda e: e.tensor_tensor(gp[:, s, 2:T + 2], bg.ap, rb[:, :], MUL), bg.op, st.r_tok, gfree[s])
            bg.free = [g]
            c0 = AC(lambda e: e.activation(t[:, 0, s, :], gp[:, s, 2:T + 2], ACT.Identity, bias=pc(cb, f),
                                           scale=pc(cw, 44 + f)), g, tfree[s])
            c1 = V(lambda e: e.scalar_tensor_tensor(t[:, 1, s, :], gp[:, s, 1:T + 1], pc(cw, 22 + f), t[:, 0, s, :],
                                                    MUL, ADD), c0, tfree[s])
            c2 = V(lambda e: e.scalar_tensor_tensor(t[:, 2, s, :], gp[:, s, 0:T], pc(cw, f), t[:, 1, s, :],
                                                    MUL, ADD), c1)
            gfree[s] = [c0, c2]
            vv = V(lambda e: e.tensor_tensor(t[:, 4, s, :], bv.ap, rb2[:, :], MUL), bv.op)
            bv.free = [vv]
            th = AC(lambda e: e.activation(t[:, 3, s, :], t[:, 2, s, :], ACT.Tanh, scale=0.5), c2)
            s2 = V(lambda e: e.scalar_tensor_tensor(t[:, 0, s, :], t[:, 3, s, :], 1.0, t[:, 2, s, :], ADD, MUL), th)
            mo = V(lambda e: e.tensor_tensor(t[:, 5, s, :], t[:, 0, s, :], t[:, 4, s, :], MUL), s2, vv)
            hid[i] = split(t[:, 5, s, :], hh[:, i, :], hl[:, i, :], mo, hfree)
            tfree[s] = hid[i]

        for half in range(2):
            for f in range(half * HF, half * HF + HF):
                bg, bv = bank[2 * f % 6], bank[(2 * f + 1) % 6]
                run(project(bg, up, f))
                next(ad, None)
                run(project(bv, up, FT + f))
                if f:
                    next(ad, None)
                drain()
                tail(f, bg, bv)
                if f > 1:
                    next(side, None)
            if half:
                st.n_free = [Q.q["pe"][-1]]
            outputs(dn, go if half else None, bs=6, ks=HF, k0=half * HF, hi=hh, lo=hl, tok=hid)
            hfree = [Q.q["pe"][-1]]
        ph.close()

    def swa(go):
        ph = ExitStack()
        f0 = fence()
        p = lambda name, shape, dt=F: sbt(ph, name + "_s", shape, dt)
        khi = p("khi", [128, KD, T], FR)
        klo = p("klo", [128, KD, T], FR)
        kz = p("kz", [128, 2, 2, T + 128])
        vz = p("vz", [128, 4, 2, 2, 128])
        qb = p("qb", [128, 2, T])
        s2 = p("s", [128, 2, 8, 256])
        pt = p("pt", [128, 4, 512])
        dist = p("dist", [128, 2, 256])
        sm2 = p("sm", [128, 2, 8, 8])
        ds = Q.dma("sp", lambda e: e.dma_start(dist[:, :, :], A["dist"]), "dist", f0)
        zk = G(lambda e: e.memset(kz[:, :, :, :], 0.0), f0)
        zv = G(lambda e: e.memset(vz[:, :, :, :, :], 0.0), f0)
        sink = par[:, PC["sink"]:PC["sink"] + 16]

        q_tok, q_free = [None, None], [f0, f0]

        def proj(i):
            b = bank[7]
            yield from project(b, "wq", i)
            q_tok[i % 2] = V(lambda e: e.tensor_tensor(qb[:, i % 2, :], b.ap, rb2[:, :], MUL), b.op, st.r_tok,
                             q_free[i % 2])
            b.free = [q_tok[i % 2]]

        run(project(bank[6], "wq", 0))
        ktok = [split_scaled(hT[:, k, :], pc("kv_norm", k), khi[:, k, :], klo[:, k, :], st.h_tok[k], par_l, f0)
                for k in range(KD)]
        for k in range(KD):
            st.h_read[k] = st.h_read[k] + ktok[k]
        run(project(bank[5], "wq", 1))
        kt = []
        for n in range(2):
            b = bank[n]
            run(project(b, "kv", n, hi=khi, lo=klo, tok=ktok))
            if n == 0:
                drain()
                for i in range(2):
                    b_ = bank[6 - i]
                    q_tok[i] = V(lambda e, i=i, b_=b_: e.tensor_tensor(qb[:, i, :], b_.ap, rb2[:, :], MUL), b_.op,
                                 st.r_tok, f0)
                    b_.free = [q_tok[i]]
            for e_ in range(2):
                ps = slice(64 * e_, 64 * e_ + 64)
                o = V(lambda e, n=n, e_=e_, ps=ps, b=b: e.tensor_tensor(kz[ps, n, e_, 128:T + 128], b.ap[ps, :],
                                                                        rb[ps, :], MUL), b.op, st.r_tok, zk)
                kt.append(o)
            b.free = [o]
        vt, kv_read = [], []

        def value_rows():
            b = bank[4]
            for k in range(KD):
                w = W.tile("kv", k, 2)
                for t in range(4):
                    c = slice(128 * t, 128 * t + 128)
                    b.op = mm_x(b.ap[:, c], w, khi[:, k, c], klo[:, k, c], k == 0 and t == 0, k == KD - 1, ktok[k],
                                b.free, skip=True)
                yield
            kv_read.append(b.op)
            for t in range(4):
                for e_ in range(2):
                    vt.append(AC(lambda e, t=t, e_=e_: e.activation(
                        vz[:, t, :, e_, 64 * e_:64 * e_ + 64],
                        b.ap[:, 128 * t:128 * t + 128].rearrange("p (a d) -> p a d", a=2), ACT.Copy,
                        scale=rc[:, t:t + 1]), b.op, st.r_tok, zv))
            b.free = vt[-1:]

        on_tok = [None] * KD
        fr = {"s": [f0, f0], "pt": [f0] * 4, "sm": [f0, f0]}
        normed = [None, None]

        def softmax(i):
            kv, z = i // 4, i % 2
            s, sm = s2[:, z], sm2[:, z]
            sc_o = []
            for blk in range(4):
                b = bank[blk]
                for e_ in range(2):
                    op = PE(lambda e, b=b, e_=e_, blk=blk: e.matmul(
                        b.ap[:, 256 * e_:256 * e_ + 256], qb[:, z, 128 * blk:128 * blk + 128],
                        kz[:, kv, e_, 128 * blk:128 * blk + 256], start=True, stop=True), q_tok[z], kt, b.free)
                for e_ in range(2):
                    slope = float(np.float32(2.0 ** (-8.0 * (2 * i + e_ + 1) / 16)))
                    o = V(lambda e, b=b, e_=e_, blk=blk, slope=slope: e.scalar_tensor_tensor(
                        s[:, 2 * blk + e_, :], dist[:, min(blk, 1), :], -slope, b.ap[:, 256 * e_:256 * e_ + 256],
                        MUL, ADD), op, ds, fr["s"][z])
                    sc_o.append(o)
                b.free = [o]
                yield
            q_free[z] = [op]
            free = fr["sm"][z]
            mx = V(lambda e: e.tensor_reduce(sm[:, 0, :], s[:, :, :], AX_X, ALU.max), sc_o, free)
            sk = sink[:, 2 * i:2 * i + 2].unsqueeze(1).to_broadcast((128, 4, 2))
            v4 = lambda j: sm[:, j, :].rearrange("p (b h) -> p b h", h=2)
            o = V(lambda e: e.tensor_tensor(v4(1), v4(0), sk, ALU.max), mx, free)
            nm = V(lambda e: e.tensor_scalar(sm[:, 2, :], sm[:, 1, :], -1.0, None, MUL), o, free)
            d = V(lambda e: e.tensor_tensor(v4(3), v4(2), sk, ADD), nm, free)
            yield
            ex = []
            for j in range(8):
                ex.append(AC(lambda e, j=j: e.activation(s[:, j, :], s[:, j, :], ACT.Exp, bias=sm[:, 2, j:j + 1],
                                                         accum_out=sm[:, 4, j:j + 1]), nm, mx, free))
                if j % 2:
                    yield
            es = AC(lambda e: e.activation(sm[:, 5, :], sm[:, 3, :], ACT.Exp), d, free)
            o = V(lambda e: e.tensor_tensor(sm[:, 6, :], sm[:, 4, :], sm[:, 5, :], ADD), es, ex)
            rd = V(lambda e: e.reciprocal(sm[:, 7, :], sm[:, 6, :]), o)
            pn = normed[z] = []
            for j in range(8):
                pn.append(V(lambda e, j=j: e.tensor_scalar(s[:, j, :], s[:, j, :], sm[:, 7, j:j + 1], None, MUL), rd,
                            ex[j]))
                if j % 2:
                    yield
            fr["sm"][z] = [pn[-1], es]

        def values(i):
            kv, z = i // 4, i % 2
            s, pn = s2[:, z], normed[z]
            b6 = bank[6]

            def turn(blk):
                b = bank[4 + blk % 2]
                for j in range(4):
                    op = PE(lambda e, b=b, j=j, blk=blk: e.transpose(
                        b.ap[:, 128 * j:128 * j + 128], s[:, 2 * blk + j // 2, 128 * (j % 2):128 * (j % 2) + 128],
                        ident[:, :]), pn[2 * blk + j // 2], b.free, id_l)
                fr["s"][z] = [op]
                c = AC(lambda e, b=b, blk=blk: e.activation(pt[:, blk, :], b.ap, ACT.Copy), op, fr["pt"][blk])
                b.free = [c]
                return c

            c = turn(0)
            yield
            for blk in range(4):
                c_ = c
                if blk < 3:
                    c = turn(blk + 1)
                    yield
                todo = [(e_, kb) for e_ in range(2) for kb in range(2) if blk or kb]
                for n, (e_, kb) in enumerate(todo):
                    op = PE(lambda e, n=n, e_=e_, kb=kb, blk=blk, last=len(todo) - 1: e.matmul(
                        b6.ap[:, 128 * blk:128 * blk + 128], vz[:, blk - 1 + kb, kv, e_, :],
                        pt[:, blk, 128 * (2 * e_ + kb):128 * (2 * e_ + kb) + 128], start=n == 0, stop=n == last),
                        c_, vt, b6.free if blk == 0 else None)
                fr["pt"][blk] = [op]
                yield
            on_tok[i] = split(b6.ap, khi[:, i, :], klo[:, i, :], op, kv_read)
            b6.free = on_tok[i]

        none = iter(())
        for i in range(-1, KD):
            a = softmax(i + 1) if i + 1 < KD else none
            if i < 0:
                pr = value_rows()
            elif i + 2 < KD:
                pr = proj(i + 2)
            else:
                pr = begin("wo", bank[7:8], i, hi=khi, lo=klo, tok=on_tok) if i == KD - 2 else none
            v = values(i) if i >= 0 else none
            for _ in range(5):
                next(a, None)
                if i < 0:
                    next(pr, None)
            for n in range(9):
                next(pr, None)
                if n < 4:
                    next(pr, None)
                next(v, None)
                next(a, None)
            for x in (v, a, pr):
                run(x)
        st.n_free = [Q.q["pe"][-1]]
        outputs("wo", go, hi=khi, lo=klo, tok=on_tok)
        ph.close()

    scv = sb("scv", [128, 3, KD, 2])
    adas = [sb(f"ada{j}", [128, 24, 2]) for j in range(2)]
    gss = [sb(f"gs{j}", [128, KD, 2]) for j in range(2)]
    cv = par[:, PC["c"]:PC["c"] + 16].rearrange("p (v k) -> p k v", v=2)
    a_ = AC(lambda e: e.activation(scv[:, 0], cv, ACT.Tanh, scale=0.5), par_l)
    a_ = V(lambda e: e.scalar_tensor_tensor(scv[:, 1], scv[:, 0], 1.0, cv, ADD, MUL), a_)
    sc_o = V(lambda e: e.tensor_scalar(scv[:, 2], scv[:, 1], 0.5, None, MUL), a_)
    scs = sb("scs", [128, KD, 4], FR)
    scs4 = scs[:, :, :].rearrange("p k (v s) -> p k v s", s=2)
    a_ = AC(lambda e: e.activation(scs4[:, :, :, 0], scv[:, 2], ACT.Copy), sc_o)
    sc_o = V(lambda e: e.tensor_tensor(scs4[:, :, :, 1], scv[:, 2], scs4[:, :, :, 0].bitcast(F), SUB), a_)
    st.ada_tok = []

    def adapt(layer, b, nv, row, rfree):
        ada, gs = adas[layer], gss[layer]
        bias = par[:, PC[f"ada_b{layer}"]:PC[f"ada_b{layer}"] + 24].unsqueeze(2).to_broadcast((128, 24, nv))
        sel = par[0:2 * nv, PC["sel"]:PC["sel"] + nv]
        for g in range(6):
            for k in range(KD):
                w = W.tiles([(f"ada{layer}", k, 4 * g + j) for j in range(4)])
                PE(lambda e, w=w, k=k: e.matmul(b.ap[0:2 * nv, :], scs[:, k, 0:2 * nv], w.hi, start=k == 0,
                                                stop=False), w.tok, sc_o, b.free)
                op = PE(lambda e, w=w, k=k: e.matmul(b.ap[0:2 * nv, :], scs[:, k, 0:2 * nv], w.lo, start=False,
                                                     stop=k == KD - 1))
                W.used(w, op)
                if k % 2:
                    yield
            a = AC(lambda e: e.activation(row[0:2 * nv, :], b.ap[0:2 * nv, :], ACT.Copy), op, rfree)
            yield
            for j in range(4):
                op = PE(lambda e, j=j: e.matmul(b.ap[:, nv * j:nv * j + nv], row[0:2 * nv, 128 * j:128 * j + 128], sel,
                                                start=True, stop=True), a, par_l)
            o = V(lambda e, g=g: e.tensor_tensor(
                ada[:, 4 * g:4 * g + 4, 0:nv], b.ap[:, 0:4 * nv].rearrange("p (m v) -> p m v", v=nv),
                bias[:, 4 * g:4 * g + 4, :], ADD), op, par_l)
            b.free = [o]
            rfree = [op]
            yield
        g = par[:, PC[f"norm_g{layer}"]:PC[f"norm_g{layer}"] + 8].unsqueeze(2).to_broadcast((128, KD, nv))
        o1 = V(lambda e: e.tensor_scalar(gs[:, :, 0:nv], ada[:, 8:16, 0:nv], 1.0, None, ADD), o)
        o2 = V(lambda e: e.tensor_tensor(gs[:, :, 0:nv], gs[:, :, 0:nv], g, MUL), o1)
        if layer == 0:
            fn = par[:, PC["final_norm"]:PC["final_norm"] + 8]
            o2 = V(lambda e: e.tensor_tensor(gs[:, :, 0], gs[:, :, 0], fn, MUL), o2)
        st.ada_tok = st.ada_tok + [o, o2]

    def modulated(layer, src, r, dh, dl, k, v, tmp, n, waits, tfree, dfree):
        mul = G if k % 3 == 1 else V
        a = mul(lambda e: e.tensor_tensor(tmp[:, 0, 0:n], src, r, MUL), waits, tfree)
        u = AC(lambda e: e.activation(tmp[:, 1, 0:n], tmp[:, 0, 0:n], ACT.Identity, bias=adas[layer][:, k, v:v + 1],
                                      scale=gss[layer][:, k, v:v + 1]), a, st.ada_tok, tfree)
        return a, split(tmp[:, 1, 0:n], dh, dl, u, dfree)

    def only_squares(m):
        q = square_in(m, hT[:, m, :], st.h_tok[m], m == 0, m == KD - 1, put_off=True)
        st.h_read[m] = [q]

    def squares_of_both(m):
        q = square_in(0, hT[:, m, :], st.h_tok[m], m == 0, m == KD - 1, put_off=True)
        q2 = square_in(1, hT[:, m, :], st.h_tok[m], False, m == KD - 1, col=4, gain=pc("final_norm", m),
                       put_off=True)
        st.h_read[m] = [q, q2]

    cst = State()
    cst.chi, cst.clo, cst.tok = None, None, [None] * KD

    def context(p, f0):
        ctx_t, tmc, rbc, rcc = p("ctx", [128, KD, TC]), p("tmc", [128, 2, TC]), p("rbc", [128, TC]), p("rcc", [128, 4])
        cl = Q.dma("sp", lambda e: e.dma_start(ctx_t[:, :, :], A["ctx"]), "ctx", f0)
        for k in range(KD):
            square_in(k, ctx_t[:, k, :], [cl], k == 0, k == KD - 1, nt=2, width=TC, put_off=True)
            yield
        r = []
        root(2, D, rcc, [(rbc, 1.0)], free=f0, put_off=True, keep=r)
        yield
        yield
        free = f0
        for k in range(KD):
            _, cst.tok[k] = modulated(0, ctx_t[:, k, :], rbc[:, :], cst.chi[:, k, :], cst.clo[:, k, :], k, 1, tmc, TC,
                                      [r, cl], free, cst.f0)
            free = cst.tok[k]
            yield

    def mla(go):
        ph = ExitStack()
        f0 = fence()
        p = lambda name, shape, dt=F: sbt(ph, name + "_m", shape, dt)
        ckh, ckl = [cst.all[:, 1536 * j:1536 * j + 1536].rearrange("p (a b) -> p a b", a=2) for j in range(2)]
        cq12 = p("cq12", [128, 2, 2, T], FR)
        cqh, cql = [[cst.all[:, 3072 + 512 * j:3584 + 512 * j], cq12[:, j, 0, :], cq12[:, j, 1, :]] for j in range(2)]
        v = p("v", [128, 6, D])
        krz = p("krz", [128, 2, T + TC])
        cs = p("cs", [128, 2, T])
        rbq = rb2
        rbk = p("rbk", [128, T + TC])
        rcq, rck = p("rcq", [128, 4]), p("rck", [128, 6])
        ph2 = ExitStack()
        p2 = lambda name, shape, dt=F: sbt(ph2, name + "_m", shape, dt)
        tmp = p2("tmp", [128, 2, 2, T])
        krt = p2("krt", [64, 2, T])
        chi, clo, c_tok = cst.chi, cst.clo, cst.tok
        rl = Q.dma("sp", lambda e: e.dma_start(cs[:, :, :], A["rope"]), "rope", f0)
        z = G(lambda e: e.memset(krz[:, :, :], 0.0), f0)

        def context_project(b, m):
            for k in range(KD):
                w = W.tile("mla_in", k, m)
                b.op = mm_w(b.ap[:, 0:TC], w, chi[:, k, :], clo[:, k, :], k == 0, k == KD - 1, c_tok[k], b.free)

        drain()
        a = AC(lambda e: e.activation(sd[:, 0:4], stat.ap[:, 0:4], ACT.Sqrt, bias=pc("eps"), scale=1.0 / D),
               st.stat_op, st.sc_free)
        r1 = V(lambda e: e.reciprocal(rc[:, 0:4], sd[:, 0:4]), a)
        a = V(lambda e: e.tensor_tensor(rc[:, 4:8], rc[:, 0:4], rc[:, 0:4], MUL), r1)
        a = V(lambda e: e.tensor_tensor(sd[:, 4:8], rc[:, 4:8], stat.ap[:, 4:8], MUL), a)
        stat.free = [a]
        a = AC(lambda e: e.activation(sd[:, 0:4], sd[:, 4:8], ACT.Sqrt, bias=pc("eps"), scale=1.0 / D), a)
        a = V(lambda e: e.reciprocal(rc[:, 4:8], sd[:, 0:4]), a)
        r2 = V(lambda e: e.tensor_tensor(rc[:, 4:8], rc[:, 4:8], rc[:, 0:4], MUL), a)
        cb = bank[4:7]
        for j in range(2):
            context_project(cb[j], 3 + j)
        last, out = spread(r2, 4, rc[:, 4:8], [(rb2, 1.0)])
        last()
        r_x = out()
        context_project(cb[2], 5)
        last, out = spread(r1, 4, rc[:, 0:4], [(rb, 1.0)])
        last()
        r_h = out()
        tf = [[], []]
        for k in range(KD):
            a, st.n_tok[k] = modulated(0, hT[:, k, :], rb2[:, :], nhi[:, k, :], nlo[:, k, :], k, 0, tmp[:, k % 2], T,
                                       [st.h_tok[k], r_x, f0], tf[k % 2], st.n_free)
            st.h_read[k] = st.h_read[k] + [a]
            tf[k % 2] = st.n_tok[k]
        def cq():
            for j in range(3):
                b = bank[1 + j]
                yield from project(b, "mla_in", j)
                q = square_in(j, b.ap, b.op, j == 0, j == 2)
                b.free = [q] + split_scaled(b.ap, pc("q_norm", j), cqh[j], cql[j], b.op, cb[2].op)
                cq_tok.append(b.free[1:])

        cq_tok, ck_tok = [], []
        run(cq())
        r_q = root(4, 384, rcq, [(rbq, 192 ** -0.5)], free=st.n_tok)
        for j in range(2):
            bx, bc = bank[1 + j], cb[j]
            run(project(bx, "mla_in", 3 + j))
            q = square_in(0, bx.ap, bx.op, j == 0, j == 1)
            q2 = square_in(1, bc.ap[:, 0:TC], bc.op, False, j == 1, nt=2, width=TC, col=4)
            bx.free = [q] + split_scaled(bx.ap, pc("kvl_norm", j), ckh[:, j, 0:T], ckl[:, j, 0:T], bx.op, cb[2].op)
            bc.free = [q2] + split_scaled(bc.ap[:, 0:TC], pc("kvl_norm", j), ckh[:, j, T:], ckl[:, j, T:], bc.op, cb[2].op)
            ck_tok.append(bx.free[1:] + bc.free[1:])
        bx, bc = bank[3], cb[2]
        run(project(bx, "mla_in", 5))
        r_k = root(6, 256, rck, [(rbk, 1.0)], free=r_q)
        t1 = V(lambda e: e.tensor_tensor(krt[:, 0, :], bx.ap[0:64, :], cs[0:64, 0, :], MUL), bx.op, rl, f0)
        t2 = V(lambda e: e.tensor_tensor(krt[:, 1, :], bx.ap[64:128, :], cs[64:128, 1, :], MUL), bx.op, rl, f0)
        bx.free = [t2]
        kr = []
        for e_ in range(2):
            ps = slice(64 * e_, 64 * e_ + 64)
            kr.append(V(lambda e, ps=ps, e_=e_: e.tensor_tensor(krz[ps, e_, 0:T], krt[:, 0, :], krt[:, 1, :], ADD),
                        t1, t2, z))
            kr.append(AC(lambda e, ps=ps, e_=e_: e.activation(krz[ps, e_, T:], bc.ap[0:64, 0:TC], ACT.Copy),
                         bc.op, z))
        bc.free = [kr[3]]
        cso = [V(lambda e, j=j: e.tensor_tensor(cs[:, j, :], cs[:, j, :], rbq[:, :], MUL), r_q, rl, t1, t2)
               for j in range(2)]
        v_tok = []
        for g in range(2):
            for k in range(2):
                w = W.tiles([("ukv", k, 8 + 4 * g + j) for j in range(4)])
                for t in range(6):
                    c = slice(128 * t, 128 * t + 128)
                    bank[t].op = mm_x(bank[t].ap, w, ckh[:, k, c], ckl[:, k, c], k == 0, k == 1, ck_tok[k],
                                      bank[t].free if k == 0 else None)
            for t in range(6):
                a = AC(lambda e, t=t, g=g: e.activation(v[:, t, 512 * g:512 * g + 512], bank[t].ap, ACT.Copy,
                                                        scale=rck[:, t:t + 1]), bank[t].op, r_k, f0)
                bank[t].free = [a]
                v_tok.append(a)
        for m in range(KD):
            h = hT[:, m, :]
            o = V(lambda e, h=h, m=m: e.scalar_tensor_tensor(h, h, pc("final_norm", m), rb[:, :], MUL, MUL),
                  st.h_tok[m], st.h_read[m], r_h)
            st.h_tok[m] = [o]
        f1 = fence()
        ph2.close()
        qn = p("qn", [128, 2, T])
        kn = p("kn", [128, 2, T + TC])
        qr = p("qr", [128, 2, T])
        tr = sqb
        s = p("s", [128, 2, T + TC])
        pt = p("pt", [128, 2, T + TC])
        sg = p("sg", [128, 2, T])
        ov = p("o", [128, KD - 1, T])
        o = [ov[:, j, :] for j in range(KD - 1)] + [qn[:, 0, :]]
        sm = p("sm", [128, 4, 4])
        fr = {"qn": [f1, f1], "kn": [f1, f1], "qr": [f1, f1], "tr": [f1, st.sq_free], "s": [f1, f1], "pt": [f1, f1],
              "sg": [f1, f1], "sm": [f1, f1]}
        tk = {}
        rk = [r_q, r_k]

        def proj(h):
            z = h % 2
            y = h // 2 % 2
            b = bank[7]
            if z == 0:
                for j in range(2):
                    yield from project(b, "uq", 8 + 2 * (h // 2) + j, ks=3, hi=cqh, lo=cql, tok=cq_tok)
                    a = V(lambda e, j=j: e.tensor_tensor(tr[:, j, :], b.ap, cs[:, j, :], MUL), b.op, cso, fr["tr"])
                    b.free = [a]
                a = V(lambda e: e.tensor_tensor(qr[:, y, :], tr[:, 0, :], tr[:, 1, :], ADD), a, fr["qr"][y])
                fr["tr"] = [a]
                tk["qr", y] = a
            yield from project(b, "uq", h, ks=3, hi=cqh, lo=cql, tok=cq_tok)
            a = V(lambda e: e.tensor_tensor(qn[:, z, :], b.ap, rbq[:, :], MUL), b.op, rk, fr["qn"][z])
            b.free = [a]
            tk["qn", z] = a
            b5 = bank[5]
            for k in range(2):
                w = W.tile("ukv", k, h)
                b.op = mm_w(b.ap, w, ckh[:, k, 0:T], ckl[:, k, 0:T], k == 0, k == 1, ck_tok[k], b.free)
                b5.op = mm_w(b5.ap[:, 256:512], w, ckh[:, k, T:], ckl[:, k, T:], k == 0, k == 1, ck_tok[k], b5.free)
            a = V(lambda e: e.tensor_tensor(kn[:, z, 0:T], b.ap, rbk[:, 0:T], MUL), b.op, rk, fr["kn"][z])
            a2 = V(lambda e: e.tensor_tensor(kn[:, z, T:], b5.ap[:, 256:512], rbk[:, T:], MUL), b5.op, rk,
                   fr["kn"][z])
            b.free = [a]
            b5.free = b5.free + [a2]
            tk["kn", z] = [a, a2]
            yield
            yield from project(b, "mla_in", 6 + h)
            a = AC(lambda e: e.activation(sg[:, z, :], b.ap, ACT.Tanh, scale=0.5), b.op, fr["sg"][z])
            a = V(lambda e: e.scalar_tensor_tensor(sg[:, z, :], sg[:, z, :], 1.0, b.ap, ADD, MUL), a)
            b.free = [a]
            tk["sg", z] = a

        def attend(h):
            z, y, e_ = h % 2, h // 2 % 2, h % 2
            exps = {}

            def scores(blk):
                i = blk % 2
                ba, bb = bank[2 * i], bank[2 * i + 1]
                c = slice(128 * blk, 128 * blk + 128)
                for b, ks, n in ((ba, slice(0, T), T), (bb, slice(T, T + TC), TC)):
                    PE(lambda e, b=b, ks=ks, n=n: e.matmul(b.ap[:, 0:n], qn[:, z, c], kn[:, z, ks], start=True,
                                                           stop=False), tk["qn", z], tk["kn", z], b.free)
                    op = PE(lambda e, b=b, ks=ks, n=n: e.matmul(b.ap[:, 0:n], qr[:, y, c], krz[:, e_, ks],
                                                                start=False, stop=True), tk["qr", y], kr)
                sv = PS[:, 1024 * i:1024 * i + T + TC]
                mx = V(lambda e: e.tensor_reduce(sm[:, i, 0:1], sv, AX_X, ALU.max), op, fr["sm"][i])
                nm = V(lambda e: e.tensor_scalar(sm[:, i, 1:2], sm[:, i, 0:1], -1.0, None, MUL), mx, fr["sm"][i])
                ex = AC(lambda e: e.activation(s[:, i, :], sv, ACT.Exp, bias=sm[:, i, 1:2], accum_out=sm[:, i, 2:3]),
                        nm, fr["s"][i], fr["sm"][i])
                ba.free = bb.free = [ex, mx]
                rd = V(lambda e: e.reciprocal(sm[:, i, 3:4], sm[:, i, 2:3]), ex)
                exps[blk] = V(lambda e: e.tensor_scalar(s[:, i, :], s[:, i, :], sm[:, i, 3:4], None, MUL), rd)
                fr["sm"][i] = [exps[blk], ex]
                return op

            op = scores(0)
            b4, b5, b6 = bank[4], bank[5], bank[6]
            for blk in range(4):
                i = blk % 2
                yield
                if blk < 3:
                    op = scores(blk + 1)
                    if blk == 2:
                        fr["qn"][z] = fr["kn"][z] = [op]
                        if e_:
                            fr["qr"][y] = [op]
                yield
                for t in range(6):
                    tr_ = PE(lambda e, t=t, i=i: e.transpose(PS[:, 2048 + 128 * t:2176 + 128 * t],
                                                             s[:, i, 128 * t:128 * t + 128], ident[:, :]),
                             exps[blk], b4.free, b5.free)
                fr["s"][i] = [tr_]
                cp = AC(lambda e, i=i: e.activation(pt[:, i, :], PS[:, 2048:2048 + T + TC], ACT.Copy), tr_,
                        fr["pt"][i])
                b4.free = b5.free = [cp]
                yield
                for t in range(6):
                    op2 = PE(lambda e, t=t, i=i, blk=blk: e.matmul(
                        b6.ap[:, 128 * blk:128 * blk + 128], v[:, t, 128 * h:128 * h + 128],
                        pt[:, i, 128 * t:128 * t + 128], start=t == 0, stop=t == 5), cp, v_tok,
                        b6.free if blk == 0 else None)
                fr["pt"][i] = [op2]
                yield
            m = V(lambda e: e.scalar_tensor_tensor(o[h], b6.ap, 0.5, sg[:, z, :], MUL, MUL), op2, tk["sg", z],
                  f1, fr["qn"][0] if h == KD - 1 else None)
            b6.free = [m]
            fr["sg"][z] = [m]
            o_op.append(m)

        o_op, o_tok = [], []
        run(proj(0))
        for h in range(KD):
            if h == KD - 1:
                st.n_free = [Q.q["pe"][-1]]
                o_tok = [split(o[j], nhi[:, j, :], nlo[:, j, :], o_op[j], st.n_free) for j in range(KD - 1)]
                o_tok.append(None)
            nxt = proj(h + 1) if h + 1 < KD else begin("mla_out", bank[7:8], KD - 1, tok=o_tok, hi=nhi, lo=nlo)
            weave(attend(h), nxt, 16, 12 if h % 2 == 0 else 18)
        o_tok[7] = split(o[7], nhi[:, 7, :], nlo[:, 7, :], o_op[7], st.n_free)
        outputs("mla_out", go, lambda m: adas[0][:, 16 + m, 0:1], tok=o_tok, hi=nhi, lo=nlo)
        st.n_free = [Q.q["pe"][-1]]
        ph.close()

    def hyena():
        ph = ExitStack()
        f0 = fence()
        p = lambda name, shape, dt=F: sbt(ph, name + "_h", shape, dt)
        zh, zl = p("zh", [128, 4, 512], FR), p("zl", [128, 4, 512], FR)
        hh, hl = p("hh", [128, 2, 4, 512], FR), p("hl", [128, 2, 4, 512], FR)
        z = p("z", [128, 4, T])
        g = p("g", [128, 4, T])
        o = p("o", [128, 4, T])
        tmp = p("tmp", [128, 5, T])
        up = p("up", [128, 2, T + 2])
        hdn = rb2
        zu = V(lambda e: e.memset(up[:, :, 0:1], 0.0), f0)
        zu = V(lambda e: e.memset(up[:, :, T + 1:T + 2], 0.0), zu)

        drain()
        r = root(4, D, rc, [(rb, 1.0)], free=f0)

        fs = ExitStack()
        pos = sbt(fs, "pos", [64, T])
        fw = sbt(fs, "fw", [64, 3, 64])
        fa = sbt(fs, "fa", [64, 4, T])
        pl = Q.dma("sp", lambda e: e.dma_start(pos[:, :], A["pos"]), "pos", f0)
        fl = Q.dma("sp", lambda e: e.dma_start(fw[:, :, :], A["filt"]), "filt", f0)

        def hidden():
            src, tok = pos, [pl, fl]
            for l in range(3):
                b = bank[1]
                op = PE(lambda e, src=src, l=l: e.matmul(b.ap[0:64, :], fw[:, l, :], src[0:64, :], start=True,
                                                         stop=True), tok, fl, b.free)
                a = V(lambda e, l=l: e.tensor_scalar(fa[:, 0, :], b.ap[0:64, :], par[0:64, PC["fb"] + l:PC["fb"] + l + 1],
                                                     par[0:64, PC["ff"] + l:PC["ff"] + l + 1], ADD, MUL), op, par_l, f0)
                b.free = [a]
                n = V(lambda e: e.tensor_scalar(fa[:, 1, :], fa[:, 0, :], float(np.float32(1 / (2 * np.pi))), None, MUL),
                      a)
                n = V(lambda e: e.tensor_scalar(fa[:, 2, :], fa[:, 1, :], 12582912.0, None, ADD), n)
                n = V(lambda e: e.tensor_scalar(fa[:, 1, :], fa[:, 2, :], -12582912.0, None, ADD), n)
                n = V(lambda e: e.scalar_tensor_tensor(fa[:, 2, :], fa[:, 1, :], -6.28125, fa[:, 0, :], MUL, ADD), n)
                n = V(lambda e: e.scalar_tensor_tensor(fa[:, 3, :], fa[:, 1, :], -(2 * np.pi - 6.28125), fa[:, 2, :],
                                                       MUL, ADD), n)
                n = V(lambda e: e.tensor_scalar(fa[:, 0, :], fa[:, 3, :], 3.1415925, -3.1415925, ALU.min, ALU.max), n)
                a = AC(lambda e: e.activation(hdn[0:64, :], fa[:, 0, :], ACT.Sin), n, f0, op)
                src, tok = hdn, [a]
                yield
            st.hd_tok = tok

        def operands():
            for k in range(KD):
                a, st.n_tok[k] = modulated(1, hT[:, k, :], rb[:, :], nhi[:, k, :], nlo[:, k, :], k, 0,
                                           tmp[:, 2 * (k % 2):2 * (k % 2) + 2], T, [st.h_tok[k], r, f0], tf[k % 2],
                                           st.n_free)
                st.h_read[k] = st.h_read[k] + [a]
                tf[k % 2] = st.n_tok[k]
                yield

        tf = [[], []]
        weave(operands(), hidden())
        tmp_free, up_free = [tf, zu], [[zu], [zu]]
        st.f_h = fence()
        fs.close()
        z_tok, g_tok, zt_tok = [None] * 4, [None] * 4, [None] * 4
        fr = {"z": [f0] * 4, "g": [f0] * 4, "zt": f0, "h": f0, "tmp": tmp_free, "up": up_free, "y": [[], []]}

        def conv(m, b, dst, *waits):
            i = m % 2
            a = AC(lambda e: e.activation(up[:, i, 1:T + 1], b.ap, ACT.Copy), b.op, fr["up"][i])
            c0 = AC(lambda e: e.activation(tmp[:, 2 * i, :], b.ap, ACT.Identity, bias=pc("hb", m), scale=pc("hw", 24 + m)),
                    b.op, fr["tmp"])
            b.free = [a, c0]
            c1 = V(lambda e: e.scalar_tensor_tensor(tmp[:, 2 * i + 1, :], up[:, i, 0:T], pc("hw", m), tmp[:, 2 * i, :],
                                                    MUL, ADD), a, c0, fr["tmp"])
            c2 = V(lambda e: e.scalar_tensor_tensor(dst, up[:, i, 2:T + 2], pc("hw", 48 + m), tmp[:, 2 * i + 1, :],
                                                    MUL, ADD), c1, waits)
            fr["up"][i] = [c1, c2]
            fr["tmp"] = [fr["tmp"], c1, c2][-3:]
            return c2

        def filters(od, c):
            hs = ExitStack()
            f = fence()
            n_ = f"_{od}{c}"
            wl = sbt(hs, "wl" + n_, [64, 2, 512])
            ws = sbt(hs, "ws" + n_, [64, 2, 512])
            dc = sbt(hs, "dc" + n_, [128, 2, 512])
            ht = sbt(hs, "ht" + n_, [128, 2, 512])
            hs.close()
            base = od * 2048 + 512 * c
            l0_ = Q.dma("sp", lambda e: e.dma_start(wl[:, 0, :], A["filt_out"][:, base:base + 512]), "fo0", f, st.f_h)
            l1_ = Q.dma("sp", lambda e: e.dma_start(wl[:, 1, :], A["filt_out"][:, base + 1024:base + 1536]), "fo1", f,
                        st.f_h)
            w = [V(lambda e, j=j: e.tensor_tensor(ws[:, j, :], wl[:, 0, :], wl[:, 1, :], (ADD, SUB)[j]), l0_, l1_, f)
                 for j in range(2)]
            dfree, hfree, tok = [f, f], [f, f], []

            def decay(t):
                i = t % 2
                return Q.dma("sp", lambda e: e.dma_start(dc[:, i, :], A["decay"][t, :, 512 * c:512 * c + 512]),
                             f"dc{i}", dfree[i], st.f_h)

            loads = [decay(0), decay(1)]
            for _ in range(3):
                yield
            for t in range(4):
                i = t % 2
                dl = loads[t]
                for j in range(2):
                    b = bank[4 + j]
                    op = PE(lambda e, b=b, t=t, j=j: e.matmul(b.ap, hdn[0:64, 128 * t:128 * t + 128], ws[:, j, :],
                                                              start=True, stop=True), w, st.hd_tok, b.free)
                    a = V(lambda e, b=b, i=i, j=j: e.tensor_tensor(ht[:, j, :], b.ap, dc[:, i, :], MUL), op, dl,
                          hfree[j])
                    b.free = [a]
                    sp = split(ht[:, j, :], hh[:, j, t, :], hl[:, j, t, :], a, fr["h"])
                    hfree[j] = sp
                    tok.append(sp)
                    dfree[i] = [a]
                    if j == 1 and t < 2:
                        loads.append(decay(t + 2))
                    yield
            st.hf_tok = tok

        def turn():
            zs = ExitStack()
            f = fence()
            st.turns += 1
            zf = sbt(zs, f"zf_{st.turns}", [128, 4, 512])
            zs.close()
            tok = []
            for ct in range(4):
                for j in range(2):
                    o_ = V(lambda e, ct=ct, j=j: e.tensor_tensor(
                        zf[:, ct, 256 * j:256 * j + 256], z[:, ct, 0:256], z[:, ct, 511:255:-1], (ADD, SUB)[j]),
                        z_tok[ct], f, st.f_h)
                tok.append(o_)
                yield
            for t in range(4):
                b = bank[6 + t % 2]
                for ct in range(4):
                    op = PE(lambda e, b=b, t=t, ct=ct: e.transpose(b.ap[:, 128 * ct:128 * ct + 128],
                                                                   zf[:, ct, 128 * t:128 * t + 128], ident[:, :]),
                            tok[ct], b.free, id_l)
                zt_tok[t] = split(b.ap, zh[:, t, :], zl[:, t, :], op, fr["zt"])
                b.free = zt_tok[t]
                yield
            st.turned = tok[3:]

        def convolve(od, c, last):
            ys = ExitStack()
            f = fence()
            yh = sbt(ys, f"yh_{od}{c}", [128, 2, 2, 512], FR)
            yl = sbt(ys, f"yl_{od}{c}", [128, 2, 2, 512], FR)
            ys.close()
            bu, bk, bi, bj = bank[4:8]
            ks = sqb
            tf_ = [fr["tmp"], f]
            ktf = [st.sq_free, f]
            yfree = [f, f]
            y_tok = [None] * 4

            def forward(j):
                nonlocal tf_, ktf
                i = j % 2
                tok = [zt_tok, st.hf_tok]
                first = [True, False, False, False]
                for k in range(4):
                    w = W.tile("dft", k, j)
                    bk.op = mm_w(bk.ap, w, hh[:, 0, k, :], hl[:, 0, k, :], k == 0, k == 3, st.hf_tok, bk.free)
                kr = AC(lambda e: e.activation(ks[:, 0, :], bk.ap, ACT.Copy), bk.op, ktf)
                bk.free = [kr]
                if j == 0:
                    for k in range(4):
                        w = W.tile("alt", k, 0)
                        bk.op = mm_w(bk.ap, w, hh[:, 0, k, :], hl[:, 0, k, :], k == 0, k == 3, st.hf_tok, bk.free)
                    kp = AC(lambda e: e.activation(tmp[:, 4, :], bk.ap, ACT.Copy), bk.op, tf_)
                    bk.free = [kp]
                    kx = tmp[:, 4, :]
                else:
                    kp, kx = kr, ks[:, 0, :]
                for k in range(4):
                    w = W.tile("dft", k, 4 + j)
                    bj.op = mm_w(bj.ap, w, hh[:, 1, k, :], hl[:, 1, k, :], k == 0, k == 3, st.hf_tok, bj.free)
                for k in range(2):
                    w = W.tile("mdft", k, j)
                    bu.op = mm_w(bu.ap, w, zh[:, k, :], zl[:, k, :], k == 0, k == 1, zt_tok[k], bu.free)
                for k in range(2):
                    w = W.tile("mdft", k, 4 + j)
                    bi.op = mm_w(bi.ap, w, zh[:, 2 + k, :], zl[:, 2 + k, :], k == 0, k == 1, zt_tok[2 + k], bi.free)
                ki = AC(lambda e: e.activation(ks[:, 1, :], bj.ap, ACT.Copy), bj.op, ktf)
                bj.free = [ki]
                if j == 0:
                    ki = V(lambda e: e.memset(ks[0:1, 1, :], 0.0), ki)
                a = V(lambda e: e.tensor_tensor(tmp[:, 0, :], bu.ap, ks[:, 0, :], MUL), bu.op, kr, tf_)
                b = V(lambda e: e.tensor_tensor(tmp[:, 1, :], bi.ap, ks[:, 1, :], MUL), bi.op, ki, tf_)
                c_ = V(lambda e: e.tensor_tensor(tmp[:, 2, :], bu.ap, ks[:, 1, :], MUL), ki, tf_)
                d = V(lambda e: e.tensor_tensor(tmp[:, 3, :], bi.ap, kx, MUL), kp, tf_)
                bu.free, bi.free = [c_], [d]
                ktf = [d]
                yr = V(lambda e: e.tensor_tensor(tmp[:, 0, :], tmp[:, 0, :], tmp[:, 1, :], SUB), a, b)
                yi = V(lambda e: e.tensor_tensor(tmp[:, 2, :], tmp[:, 2, :], tmp[:, 3, :], ADD), c_, d)
                s1 = split(tmp[:, 0, :], yh[:, i, 0, :], yl[:, i, 0, :], yr, yfree[i])
                s2 = split(tmp[:, 2, :], yh[:, i, 1, :], yl[:, i, 1, :], yi, yfree[i])
                y_tok[j] = [s1, s2]
                tf_ = [s1, s2]

            def inverse(j):
                i = j % 2
                for q in range(2):
                    w = W.tiles([("idft", j, 2 * q + m) for m in range(2)])
                    half = slice(256 * q, 256 * q + 256)
                    for ct in range(4):
                        cs = slice(128 * ct, 128 * ct + 128)
                        b = bank[ct]
                        b.op = mm_x(b.ap[:, half], w, yh[:, i, q, cs], yl[:, i, q, cs], j == 0 and q == 0, j == 3,
                                    y_tok[j][q], b.free, skip=True)
                yfree[i] = [bank[3].op]

            forward(0)
            for j in range(1, 4):
                forward(j)
                inverse(j - 1)
            inverse(3)
            if last and c == 1:
                run(begin("hy_out", bank[4:7], 4, tok=fin, hi=nhi, lo=nlo))
            fr["h"] = fr["zt"] = [Q.q["pe"][-1]]
            o_tok = []
            for ct in range(4):
                b = bank[ct]
                m = 4 * c + ct
                odd = ks[:, ct % 2, 256 * (ct // 2):256 * (ct // 2) + 256]
                cp = AC(lambda e, b=b, odd=odd: e.activation(odd, b.ap[:, 256:512], ACT.Copy), b.op, ktf)
                a1 = V(lambda e, b=b, ct=ct, odd=odd: e.tensor_tensor(tmp[:, ct, 0:256], b.ap[:, 0:256], odd, ADD),
                       cp, tf_)
                a2 = V(lambda e, b=b, ct=ct, odd=odd: e.tensor_tensor(tmp[:, ct, 256:512], b.ap[:, 255::-1],
                                                                      odd[:, ::-1], SUB), cp, tf_)
                b.free = [a1, a2]
                a = V(lambda e, ct=ct, m=m: e.scalar_tensor_tensor(tmp[:, ct, :], z[:, ct, :],
                                                                   pc("hbias", 8 * od + m), tmp[:, ct, :], MUL, ADD),
                      a1, a2, z_tok[ct])
                dst = z[:, ct, :] if not last else o[:, ct, :]
                r_ = V(lambda e, ct=ct, dst=dst: e.tensor_tensor(dst, tmp[:, ct, :], g[:, ct, :], MUL), a, g_tok[ct],
                       st.turned, st.o_free)
                if not last:
                    z_tok[ct] = r_
                else:
                    o_tok.append(r_)
                fr["g"][ct] = [r_]
                fr["z"][ct] = [a, r_]
            fr["tmp"] = [Q.q["dve"][-1], f]
            st.sq_free = [[a2], [a2]]
            return o_tok

        st.o_free = f0
        fin = [None] * KD

        def channels(c, part):
            for ct in range(4):
                m = 8 * part + 4 * c + ct
                b = bank[ct % 2]
                yield from project(b, "hy_in", m)
                if part == 0:
                    z_tok[ct] = conv(m, b, z[:, ct, :], fr["z"][ct], st.turned)
                else:
                    g_tok[ct] = conv(m, b, g[:, ct, :], fr["g"][ct])
                if part == 2:
                    b = bank[2 + ct % 2]
                    yield from project(b, "hy_in", 24 + 4 * c + ct)
                    th = AC(lambda e, b=b: e.activation(tmp[:, 4, :], b.ap, ACT.Tanh, scale=0.5), b.op, fr["tmp"])
                    s2 = V(lambda e, b=b: e.scalar_tensor_tensor(tmp[:, 4, :], tmp[:, 4, :], 1.0, b.ap, ADD, MUL), th)
                    b.free = [s2]
                    x = V(lambda e, ct=ct: e.scalar_tensor_tensor(g[:, ct, :], g[:, ct, :], 0.5, tmp[:, 4, :],
                                                                  MUL, MUL), s2, g_tok[ct])
                    fr["tmp"] = [fr["tmp"], x]
                    g_tok[ct] = x

        def chain(*gens):
            for x in gens:
                yield from x

        st.turned, st.turns = f0, 0
        for c in range(2):
            weave(channels(c, 0), filters(0, c), *((25, 11, 7) if c == 0 else (20, 11, 12)))
            weave(channels(c, 1), turn(), 22, 8, 9)
            convolve(0, c, False)
            weave(channels(c, 2), chain(filters(1, c), turn()), 54, 19, 8)
            if c == 1:
                st.n_free = [Q.q["pe"][-1]]
                for ct in range(4):
                    fin[ct] = split(o[:, ct, :], nhi[:, ct, :], nlo[:, ct, :], o_tok[ct], st.n_free)
                st.o_free = [fin[0:4]]
            o_tok = convolve(1, c, True)
        for ct in range(4):
            fin[4 + ct] = split(o[:, ct, :], nhi[:, 4 + ct, :], nlo[:, 4 + ct, :], o_tok[ct], st.n_free)
        outputs("hy_out", only_squares, lambda m: adas[1][:, 16 + m, 0:1], tok=fin, hi=nhi, lo=nlo)
        drain()
        root(4, D, rc, [(rb, 1.0)])
        for m in range(KD):
            h = hT[:, m, :]
            st.h_tok[m] = [V(lambda e, h=h, m=m: e.scalar_tensor_tensor(h, h, pc("final_g", m), rb[:, :], MUL, MUL),
                             st.h_tok[m], st.h_read[m], st.r_tok)]
        ph.close()

    hgrn()
    if stage >= 2:
        ffn(0, after("attn_norm"))
        root(4, D, rc, [(rb, 1.0), (rb2, 0.125)], put_off=True)
    if stage >= 3:
        swa(after("ffn_norm1"))
        root(4, D, rc, [(rb, 1.0), (rb2, 0.5)], put_off=True)
    cs_ = ExitStack()
    if stage >= 4:
        cst.f0 = fence()
        cst.all = sbt(cs_, "call", [128, 2 * KD * TC], FR)
        cst.chi, cst.clo = [cst.all[:, j * KD * TC:(j + 1) * KD * TC].rearrange("p (k t) -> p k t", k=KD)
                            for j in range(2)]
        ffn(1, squares_of_both, context)
    if stage >= 6:
        mla(only_squares)
    cs_.close()
    if stage >= 7:
        hyena()

    outs = [Q.dma("sp", lambda e, m=m: e.dma_start(A["out"][m], hT[:, m, :]), "out", st.h_tok[m]) for m in range(KD)]
    W.align()
    Q.count()
    if chunks == 10 ** 6:
        ctx.close()
        return W.at // 8, W.spec
    with ctx:
        sems = {n: ctx.enter_context(nc.semaphore(f"s_{n}")) for n in ("pe", "act", "dve", "pool", *Q.dmas)}
        block = ctx.enter_context(nc.Block())

        @block.sync
        def _(eng):
            Q.emit("sp", eng, sems)
            eng.wait_ge(sems["out"], Q.dmas["out"])

        @block.scalar
        def _(eng):
            Q.emit("act", eng, sems)

        @block.vector
        def _(eng):
            Q.emit("dve", eng, sems)

        @block.gpsimd
        def _(eng):
            Q.emit("pool", eng, sems)

        @block.tensor
        def _(eng):
            Q.emit("pe", eng, sems)
    return W.at // 8, W.spec


def masks():
    s = np.arange(128)[:, None]
    t = np.arange(128)[None, :]
    out = [s == t]
    for lv in range(LV):
        b = 1 << lv
        out.append((s // (2 * b) == t // (2 * b)) & (s // b % 2 == 0) & (t // b % 2 == 1))
    return np.ascontiguousarray(np.stack(out, 1).astype(np.float32))


def distances():
    d = np.arange(128)[:, None] + 128 - np.arange(256)[None, :]
    ok = (d >= 0) & (d < 128)
    first = ok & (np.arange(256)[None, :] >= 128)
    return np.ascontiguousarray(np.stack([np.where(first, d, 1e30), np.where(ok, d, 1e30)], 1).astype(np.float32))


def rope():
    t = np.arange(T)
    inv = np.float32(10000.0) ** (-np.arange(16, dtype=np.float32) / np.float32(16))
    ang = np.concatenate([(t // 64).astype(np.float32)[:, None] * inv, (t % 64).astype(np.float32)[:, None] * inv], 1)
    c, s = np.cos(ang, dtype=np.float32).T, np.sin(ang, dtype=np.float32).T
    return np.ascontiguousarray(np.stack([np.concatenate([c, c, c, c]), np.concatenate([-s, s, -s, s])], 1))


def fourier():
    t = np.arange(T)
    w = 2 * np.pi * (np.outer(t, t) % 1024) / 1024
    c, s = np.cos(w), -np.sin(w)
    alt = np.where(t % 2, -1.0, 1.0)
    s[:, 0] = alt
    c2 = c[:, 0:128].copy()
    c2[:, 0] = alt
    w = 2 * np.pi * (np.outer(2 * t[0:256] - T + 1, t) % 2048) / 2048
    mc, ms = np.cos(w), -np.sin(w)
    ms[:, 0] = -alt[0:256]
    ic, isn = 2 * mc.T / 1024, 2 * ms.T / 1024
    ic[0, :] = 1 / 1024
    isn[0, :] = -alt[0:256] / 1024
    cat = lambda a, b: np.concatenate([a, b], 1).astype(np.float32)
    return cat(c, s), c2.astype(np.float32), cat(mc, ms), cat(ic, isn)


def filter_tables():
    f = np.float32
    t = np.linspace(0.0, 1.0, T, dtype=f)[:, None]
    wpos = f(2.0 * np.pi / T) * np.arange(T, dtype=f)[:, None]
    bands = np.linspace(1e-4, 15, 16, dtype=f)[None, :]
    x = np.concatenate([t, np.cos(bands * wpos), -np.sin(bands * wpos)], 1).astype(f)
    pos = np.zeros((64, T), f)
    pos[0:33] = x.T
    deltas = np.abs(np.linspace(np.log(1e-2) / 0.3, np.log(1e-2) / 1.5, D, dtype=f))
    return pos, np.exp(-t * deltas).astype(f).reshape(4, 128, D)


def filter_weights(i):
    w = np.zeros((64, 3, 64), np.float32)
    w[0:33, 0] = i["hy_filt_w_in_2"][0]
    w[:, 1], w[:, 2] = i["hy_filt_w_hid_2"][0][0], i["hy_filt_w_hid_2"][0][1]
    return w


def cols(a):
    a = np.asarray(a).reshape(-1)
    return a.reshape(-1, 128).T


def params(i):
    p = {
        "hg_norm": cols(i["hg_norm"][0]), "lb0": cols(i["hg_lb_logits"][0]), "lb1": cols(i["hg_lb_logits"][1]),
        "out_norm": cols(i["hg_out_norm"][0]), "kv_norm": cols(i["kv_norm"]), "attn_norm": cols(i["attn_norm"][0]),
        "ffn_norm0": cols(i["ffn_norm"][0]), "ffn_norm1": cols(i["ffn_norm"][1]),
        "final_norm": cols(i["final_norm"]), "norm_g0": cols(i["norm_g_2"][0]), "norm_g1": cols(i["norm_g_2"][1]),
        "final_g": cols(i["final_g_2"]), "q_norm": cols(i["mla_q_norm_g_2"][0]),
        "kvl_norm": cols(i["mla_kv_norm_g_2"][0]),
        "sink": np.broadcast_to(np.asarray(i["attn_sinks"][0])[None, :], (128, 16)),
        "eps": np.full((128, 1), EPS, np.float32),
        "cw0": cols(i["ffn_conv_w"][0]), "cw1": cols(i["ffn_conv_w"][1]),
        "cb0": cols(i["ffn_conv_b"][0]), "cb1": cols(i["ffn_conv_b"][1]),
        "ada_b0": cols(i["ada_b_2"][0]), "ada_b1": cols(i["ada_b_2"][1]),
        "c": cols(i["c_2"][0]), "cc": cols(i["c_ctx_2"]),
        "hw": cols(i["hy_conv_w_2"][0]), "hb": cols(i["hy_conv_b_2"][0]), "hbias": cols(i["hy_bias_2"][0]),
        "fb": np.pad(np.asarray(i["hy_filt_b_2"][0]).T, ((0, 64), (0, 0))),
        "ff": np.pad(np.asarray(i["hy_filt_freq_2"][0]).T, ((0, 64), (0, 0))),
        "sel": np.pad(np.repeat(np.eye(2, dtype=np.float32), 2, 0), ((0, 124), (0, 0))),
    }
    out = np.empty((128, NPAR), np.float32)
    for name, w in PAR:
        out[:, PC[name]:PC[name] + w] = p[name]
    return out


def matrices(i):
    kv = np.asarray(i["w_kv"])
    k0, k1, vv = kv[:, 0:64], kv[:, 64:128], kv[:, 128:256]
    mi = np.asarray(i["mla_w_in_2"][0])
    uq = np.asarray(i["mla_w_uq_2"][0]).reshape(384, 8, 192)
    ukv = np.asarray(i["mla_w_ukv_2"][0]).reshape(256, 8, 256)
    dft, alt, mdft, idft = fourier()
    return {
        "w_in": i["hg_w_in"][0], "w_out": i["hg_w_out"][0],
        "up0": i["ffn_w_up"][0], "up1": i["ffn_w_up"][1],
        "down0": i["ffn_w_down"][0], "down1": i["ffn_w_down"][1],
        "kv": np.concatenate([k0, k0, k1, k1, vv], 1),
        "mla_in": np.concatenate([mi[:, 0:704], mi[:, 672:704], mi[:, 640:672], mi[:, 704:]], 1),
        "uq": np.concatenate([uq[:, :, 0:128].reshape(384, 1024)] + [
            x for h in range(0, 8, 2) for x in (
                uq[:, h, 128:], uq[:, h + 1, 128:], uq[:, h, 160:], uq[:, h, 128:160], uq[:, h + 1, 160:],
                uq[:, h + 1, 128:160])], 1),
        "ukv": np.concatenate([ukv[:, :, 0:128].reshape(256, 1024), ukv[:, :, 128:].reshape(256, 1024)], 1),
        "mla_out": i["mla_w_out_2"][0], "ada0": i["ada_w_2"][0], "ada1": i["ada_w_2"][1],
        "hy_in": i["hy_w_in_2"][0], "hy_out": i["hy_w_out_2"][0], "dft": dft, "alt": alt, "mdft": mdft, "idft": idft,
        "wq": i["attn_w_q"][0], "wo": i["attn_w_o"][0],
    }


def pack(spec, mats):
    out = np.zeros((len(spec) // 8, 128, 1024), np.float32)
    mats = {n: np.asarray(a) for n, a in mats.items()}
    for j, x in enumerate(spec):
        if x is not None:
            name, k, m = x
            out[j // 8, :, j % 8 * 128:j % 8 * 128 + 128] = mats[name][128 * k:128 * k + 128, 128 * m:128 * m + 128]
    return out


def feature_major(x):
    return np.ascontiguousarray(np.asarray(x).T.reshape(KD, 128, -1))


def prepare(inputs, fresh, stage=99):
    def declare(nc, shapes):
        return {n: nc.dram_tensor(f"in_{n}", s, F, kind="ExternalInput").ap()
                for n, s in shapes.items()}

    i = inputs
    pos, decay = filter_tables()
    arrays = {
        "par": params(i), "xT": feature_major(i["x"][0]), "ident": np.eye(128, dtype=np.float32), "masks": masks(),
        "pos": pos, "decay": decay, "filt": filter_weights(i), "filt_out": np.asarray(i["hy_filt_w_out_2"][0]),
        "dist": distances(), "rope": rope(),
        "ctx": np.ascontiguousarray(np.asarray(i["ctx_2"][0]).T.reshape(KD, 128, TC).transpose(1, 0, 2)),
    }
    res = (10 ** 6, None)
    for _ in range(2):
        nc = fresh()
        n = res[0]
        A = declare(nc, {**{k: a.shape for k, a in arrays.items()}, "stream": (n, 128, 1024)})
        A["out"] = nc.dram_tensor("out_0", (KD, 128, T), F, kind="ExternalOutput").ap()
        res = build(nc, A, n, stage)
    arrays["stream"] = pack(res[1], matrices(i))
    return nc, {f"in_{k}": a for k, a in arrays.items()}


def kernel(**inputs):
    import concourse.bacc as _bacc
    from concourse.bass_utils import run_bass_kernel_spmd as _run

    nc, arrays = prepare(inputs, lambda: _bacc.Bacc("TRN2", target_bir_lowering=False, num_devices=1))
    r = _run(nc, [arrays], core_ids=[0])
    out = r.results[0]["out_0"]
    return np.ascontiguousarray(out.reshape(D, T).T).reshape(1, T, D)
```
